# Optimizing a Trainium2 kernel written in Bass

```python
import jax, jax.numpy as jnp
from jax import lax
import numpy as np

D_MODEL = 1024
BATCH = 1
SEQ = 256
DEPTH = 2
DEC_BATCH = 8
DEC_SEQ = 1
PAST_LEN = 256
PAGE_SIZE = 128

N_META = 16
N_A_LAYERS = DEPTH // 2
N_B_LAYERS = DEPTH - N_A_LAYERS
A_HEADS = 4
A_DK_TOT = D_MODEL // 2
A_DV_TOT = D_MODEL
A_DK = A_DK_TOT // A_HEADS
A_DV = A_DV_TOT // A_HEADS
A_GATE_RANK = 16
A_GATE_TAU = 16.0
A_CHUNK = 64
A_IN = 2 * A_DK_TOT + 2 * A_DV_TOT + A_GATE_RANK
B_HEADS = 16
B_HD = D_MODEL // B_HEADS
B_QBLOCK = 128
KV_IN = 2 * D_MODEL + B_HEADS
D_FF = ((8 * D_MODEL // 3 + 255) // 256) * 256
EPS = 1e-6

kernel_name = 'gla_fox_yoco_macaron_meta_step'

def rmsnorm(x, g):
    xf = x.astype(jnp.float32)
    y = xf * lax.rsqrt(jnp.mean(xf * xf, axis=-1, keepdims=True) + EPS)
    return (y * g.astype(jnp.float32)).astype(x.dtype)

def swiglu(x, w_gate, w_up, w_down):
    return (jax.nn.silu(x @ w_gate) * (x @ w_up)) @ w_down

def gla_project(h, w_in, w_alpha2, b_alpha):
    bsz, t = h.shape[0], h.shape[1]
    p = h @ w_in
    q, k, v, r, a = jnp.split(p, [A_DK_TOT, 2 * A_DK_TOT, 2 * A_DK_TOT + A_DV_TOT, 2 * A_DK_TOT + 2 * A_DV_TOT], axis=-1)
    la = jax.nn.log_sigmoid((a @ w_alpha2 + b_alpha).astype(jnp.float32)) / A_GATE_TAU
    q = q.reshape(bsz, t, A_HEADS, A_DK) * (A_DK ** -0.5)
    k = k.reshape(bsz, t, A_HEADS, A_DK)
    v = v.reshape(bsz, t, A_HEADS, A_DV)
    la = la.reshape(bsz, t, A_HEADS, A_DK)
    return q, k, v, la, r

def gla_chunk(s0, q, k, v, la):
    qf, kf, vf = q.astype(jnp.float32), k.astype(jnp.float32), v.astype(jnp.float32)
    c = q.shape[1]
    b = jnp.cumsum(la, axis=1)
    causal = jnp.tril(jnp.ones((c, c), dtype=bool))[None, :, :, None, None]
    decay = jnp.exp(jnp.where(causal, b[:, :, None] - b[:, None, :], -jnp.inf))
    scores = jnp.einsum('bthd,bshd,btshd->bhts', qf, kf, decay)
    o = jnp.einsum('bhts,bshv->bthv', scores, vf) + jnp.einsum('bthd,bhdv->bthv', qf * jnp.exp(b), s0)
    b_end = b[:, -1]
    s1 = jnp.exp(b_end)[..., None] * s0 + jnp.einsum('bshd,bshv->bhdv', kf * jnp.exp(b_end[:, None] - b), vf)
    return s1, o

def gla_sequence(s0, q, k, v, la):
    bsz, t = q.shape[0], q.shape[1]
    n = t // A_CHUNK

    def chunks(a):
        return jnp.moveaxis(a.reshape((bsz, n, A_CHUNK) + a.shape[2:]), 1, 0)

    s, o = lax.scan(lambda st, xs: gla_chunk(st, *xs), s0, (chunks(q), chunks(k), chunks(v), chunks(la)))
    return s, jnp.moveaxis(o, 0, 1).reshape(bsz, t, A_HEADS, A_DV)

def gla_output(o, r, g_head, w_out):
    bsz, t = o.shape[0], o.shape[1]
    o = rmsnorm(o, g_head).reshape(bsz, t, A_DV_TOT).astype(r.dtype)
    return (o * jax.nn.silu(r)) @ w_out

def shared_kv(x, g, w_in, b_f):
    bsz, t = x.shape[0], x.shape[1]
    p = rmsnorm(x, g) @ w_in
    k = p[..., :D_MODEL].reshape(bsz, t, B_HEADS, B_HD)
    v = p[..., D_MODEL:2 * D_MODEL].reshape(bsz, t, B_HEADS, B_HD)
    logf = jax.nn.log_sigmoid((p[..., 2 * D_MODEL:] + b_f).astype(jnp.float32))
    return k, v, logf

def fox_attend(q, k, v, c_q, c_k, pos_q, pos_k):
    s = jnp.einsum('bthd,bshd->bhts', q, k).astype(jnp.float32) * (B_HD ** -0.5)
    s = s + jnp.swapaxes(c_q, 1, 2)[:, :, :, None] - jnp.swapaxes(c_k, 1, 2)[:, :, None, :]
    s = jnp.where((pos_k[None, :] <= pos_q[:, None])[None, None], s, -jnp.inf)
    p = jax.nn.softmax(s, axis=-1).astype(v.dtype)
    return jnp.einsum('bhts,bshd->bthd', p, v)

def setup_inputs(seed: int = 0) -> dict:
    key = jax.random.key(seed)
    ks = iter(jax.random.split(key, 40))
    n_pages = PAST_LEN // PAGE_SIZE
    n_used = DEC_BATCH * n_pages
    n_phys = n_used + max(1, n_used // 4)

    def nrm(shape, scale=1.0):
        return jax.random.normal(next(ks), shape, jnp.float32) * scale

    def gain(shape):
        return 1.0 + 0.02 * jax.random.normal(next(ks), shape, jnp.float32)

    page_table = jax.random.permutation(next(ks), n_phys)[:n_used].reshape(DEC_BATCH, n_pages).astype(jnp.int32)
    return {
        'x_prompt': nrm((BATCH, SEQ, D_MODEL)),
        'x_sample': nrm((DEC_BATCH, DEC_SEQ, D_MODEL)),
        'state_gla': nrm((N_A_LAYERS, DEC_BATCH, A_HEADS, A_DK, A_DV), 0.5),
        'cache_k': nrm((n_phys, PAGE_SIZE, B_HEADS, B_HD)),
        'cache_v': nrm((n_phys, PAGE_SIZE, B_HEADS, B_HD)),
        'cache_logf': jax.nn.log_sigmoid(nrm((n_phys, PAGE_SIZE, B_HEADS)) + 2.0),
        'page_table': page_table,
        'meta_tokens': nrm((N_META, D_MODEL)),
        'norm_ffn1': gain((DEPTH, D_MODEL)),
        'ffn1_w_gate': nrm((DEPTH, D_MODEL, D_FF), D_MODEL ** -0.5),
        'ffn1_w_up': nrm((DEPTH, D_MODEL, D_FF), D_MODEL ** -0.5),
        'ffn1_w_down': nrm((DEPTH, D_FF, D_MODEL), D_FF ** -0.5),
        'norm_mix': gain((DEPTH, D_MODEL)),
        'norm_ffn2': gain((DEPTH, D_MODEL)),
        'ffn2_w_gate': nrm((DEPTH, D_MODEL, D_FF), D_MODEL ** -0.5),
        'ffn2_w_up': nrm((DEPTH, D_MODEL, D_FF), D_MODEL ** -0.5),
        'ffn2_w_down': nrm((DEPTH, D_FF, D_MODEL), D_FF ** -0.5),
        'gla_w_in': nrm((N_A_LAYERS, D_MODEL, A_IN), D_MODEL ** -0.5),
        'gla_w_alpha2': nrm((N_A_LAYERS, A_GATE_RANK, A_DK_TOT), A_GATE_RANK ** -0.5),
        'gla_b_alpha': nrm((N_A_LAYERS, A_DK_TOT), 0.02),
        'gla_g_head': gain((N_A_LAYERS, A_DV)),
        'gla_w_out': nrm((N_A_LAYERS, A_DV_TOT, D_MODEL), A_DV_TOT ** -0.5),
        'kv_norm': gain((D_MODEL,)),
        'kv_w_in': nrm((D_MODEL, KV_IN), D_MODEL ** -0.5),
        'kv_b_f': nrm((B_HEADS,), 0.02),
        'fox_w_q': nrm((N_B_LAYERS, D_MODEL, D_MODEL), D_MODEL ** -0.5),
        'fox_w_out': nrm((N_B_LAYERS, D_MODEL, D_MODEL), D_MODEL ** -0.5),
        'final_norm': gain((D_MODEL,)),
    }

def reference(x_prompt, x_sample, state_gla, cache_k, cache_v, cache_logf, page_table, meta_tokens,
              norm_ffn1, ffn1_w_gate, ffn1_w_up, ffn1_w_down, norm_mix, norm_ffn2,
              ffn2_w_gate, ffn2_w_up, ffn2_w_down, gla_w_in, gla_w_alpha2, gla_b_alpha, gla_g_head,
              gla_w_out, kv_norm, kv_w_in, kv_b_f, fox_w_q, fox_w_out, final_norm):

    def trunk(x, gla_mix, kv_ctx, fox_mix):
        states = []
        rows = ctx = None
        for l in range(DEPTH):
            x = x + 0.5 * swiglu(rmsnorm(x, norm_ffn1[l]), ffn1_w_gate[l], ffn1_w_up[l], ffn1_w_down[l])
            h = rmsnorm(x, norm_mix[l])
            if l < N_A_LAYERS:
                y, st = gla_mix(l, h)
                states.append(st)
            else:
                y = fox_mix(l - N_A_LAYERS, h, ctx)
            x = x + y
            x = x + 0.5 * swiglu(rmsnorm(x, norm_ffn2[l]), ffn2_w_gate[l], ffn2_w_up[l], ffn2_w_down[l])
            if l == N_A_LAYERS - 1:
                rows, ctx = kv_ctx(x)
        return rmsnorm(x, final_norm), jnp.stack(states, axis=0), rows

    def gla_prompt(l, h):
        q, k, v, la, r = gla_project(h, gla_w_in[l], gla_w_alpha2[l], gla_b_alpha[l])
        s0 = jnp.zeros((h.shape[0], A_HEADS, A_DK, A_DV), jnp.float32)
        s_m, o_m = gla_chunk(s0, q[:, :N_META], k[:, :N_META], v[:, :N_META], la[:, :N_META])
        s, o_r = gla_sequence(s_m, q[:, N_META:], k[:, N_META:], v[:, N_META:], la[:, N_META:])
        return gla_output(jnp.concatenate([o_m, o_r], axis=1), r, gla_g_head[l], gla_w_out[l]), s

    def kv_prompt(x):
        k, v, logf = shared_kv(x, kv_norm, kv_w_in, kv_b_f)
        return (k, v, logf), (k, v, jnp.cumsum(logf, axis=1))

    def fox_prompt(lb, h, ctx):
        k, v, c = ctx
        bsz, t = h.shape[0], h.shape[1]
        q = (h @ fox_w_q[lb]).reshape(bsz, t, B_HEADS, B_HD)
        pos = jnp.arange(t)
        o_m = fox_attend(q[:, :N_META], k[:, :N_META], v[:, :N_META], c[:, :N_META], c[:, :N_META],
                         pos[:N_META], pos[:N_META])
        nb = (t - N_META) // B_QBLOCK

        def blocks(a):
            return jnp.moveaxis(a[:, N_META:].reshape((bsz, nb, B_QBLOCK) + a.shape[2:]), 1, 0)

        pos_b = pos[N_META:].reshape(nb, B_QBLOCK)
        o_b = lax.map(lambda xs: fox_attend(xs[0], k, v, xs[1], c, xs[2], pos), (blocks(q), blocks(c), pos_b))
        o_r = jnp.moveaxis(o_b, 0, 1).reshape(bsz, t - N_META, B_HEADS, B_HD)
        o = jnp.concatenate([o_m, o_r], axis=1).reshape(bsz, t, D_MODEL)
        return o @ fox_w_out[lb]

    def gla_sample(l, h):
        q, k, v, la, r = gla_project(h, gla_w_in[l], gla_w_alpha2[l], gla_b_alpha[l])
        s, o = gla_chunk(state_gla[l].astype(jnp.float32), q, k, v, la)
        return gla_output(o, r, gla_g_head[l], gla_w_out[l]), s.astype(state_gla.dtype)

    def kv_sample(x):
        k, v, logf = shared_kv(x, kv_norm, kv_w_in, kv_b_f)
        bsz = x.shape[0]
        n_pages = page_table.shape[1]

        def gather(cache):
            return cache[page_table].reshape((bsz, n_pages * PAGE_SIZE) + cache.shape[2:])

        k_all = jnp.concatenate([gather(cache_k).astype(k.dtype), k], axis=1)
        v_all = jnp.concatenate([gather(cache_v).astype(v.dtype), v], axis=1)
        lf_all = jnp.concatenate([gather(cache_logf).astype(jnp.float32), logf], axis=1)
        return (k, v, logf), (k_all, v_all, jnp.cumsum(lf_all, axis=1))

    def fox_sample(lb, h, ctx):
        k_all, v_all, c_all = ctx
        bsz, t = h.shape[0], h.shape[1]
        past = k_all.shape[1] - t
        q = (h @ fox_w_q[lb]).reshape(bsz, t, B_HEADS, B_HD)
        pos_k = jnp.arange(past + t)
        o = fox_attend(q, k_all, v_all, c_all[:, past:], c_all, pos_k[past:], pos_k)
        return o.reshape(bsz, t, D_MODEL) @ fox_w_out[lb]

    meta = jnp.broadcast_to(meta_tokens.astype(x_prompt.dtype)[None], (x_prompt.shape[0], N_META, D_MODEL))
    x0 = jnp.concatenate([meta, x_prompt], axis=1)
    y_p, st_p, rows_p = trunk(x0, gla_prompt, kv_prompt, fox_prompt)
    y_s, st_s, rows_s = trunk(x_sample, gla_sample, kv_sample, fox_sample)
    k_p, v_p, lf_p = rows_p
    k_s, v_s, lf_s = rows_s
    return (y_p[:, N_META:], y_s, st_p, k_p, v_p, lf_p, st_s, k_s, v_s, lf_s)


_drawn_inputs = setup_inputs


def setup_inputs(seed=0):
    import zlib

    import numpy as np

    out = dict(_drawn_inputs(seed))
    spreads = {}
    factors = {'norm_ffn1': 4.032,
     'norm_ffn2': 5.58,
     'gla_b_alpha': 6.767,
     'gla_g_head': 18.145,
     'kv_norm': 7.805,
     'kv_b_f': 16.685,
     'final_norm': 28.997,
     'cache_k': 2.733,
     'cache_logf': 4.879}
    for name, (base, spread) in spreads.items():
        noise = np.random.default_rng([zlib.crc32(name.encode()), seed]).standard_normal(out[name].shape)
        drawn = base * np.exp(spread * noise) if base else spread * noise
        out[name] = __import__('jax').numpy.asarray(drawn.astype(out[name].dtype))
    for name, factor in factors.items():
        out[name] = (out[name] * factor).astype(out[name].dtype)
    return out
```

```python
import concourse.bass as bass
from concourse import mybir
from contextlib import ExitStack

P = 128
D = 1024
KB = D // P
META, SEQ, SMP = 16, 256, 8
PRM = META + SEQ
TOK = PRM + SMP
FF = 2816
FB = FF // P
UPW = KB * P
DNT = FB // 2
DNW = DNT * P
SLOTS = 4
AH, DV = 4, 256
BH, HD = 16, 64
RANK = 16
PAGE, NPG = 128, 2
EPS = 1e-6
LEVELS = [1, 2, 4, 8, 16, 32, 64]

SEGS = []
for _name in ("ffn0", "gla", "ffn1", "kv", "ffn2", "fox", "ffn3"):
    if _name.startswith("ffn"):
        SEGS += [(_name + "_up", 2 * FB, KB), (_name + "_down", 2 * KB, DNT)]
    elif _name == "gla":
        SEGS += [("gla_in", 24, KB), ("gla_out", KB, KB)]
    elif _name == "kv":
        SEGS += [("kv_in", 16, KB)]
    else:
        SEGS += [("fox_q", KB, KB), ("fox_out", KB, KB)]
CHUNK0, UNIT0, COUNT, TILES, NEXT = {}, {}, {}, {}, {}
_c = _u = 0
for _i, (_name, _n, _t) in enumerate(SEGS):
    CHUNK0[_name], UNIT0[_name], COUNT[_name], TILES[_name] = _c, _u, _n, _t
    NEXT[_name] = SEGS[_i + 1][0] if _i + 1 < len(SEGS) else None
    _c += _n
    _u += _n if _name.endswith(("_up", "_in", "_q")) else 0
MIX0 = {"gla_in": 0, "gla_out": 24, "kv_in": 32, "fox_q": 48, "fox_out": 56}
GAINS = ("ffn0", "gla", "ffn1", "kv", "ffn2", "fox", "ffn3", "final")
GAIN = {n: i for i, n in enumerate(GAINS)}
STAGE = {"ffn0": 0, "gla": 1, "ffn1": 2, "kv": 3, "ffn2": 3, "fox": 4, "ffn3": 5, "final": 6}

COL = {}
_at = 0
for _n, _w in (("ident", P), ("mean_d", P), ("mean_dv", P), ("tri", P), ("own", SMP), ("rep", P),
               ("gain", 8 * KB), ("ghead", 2), ("balpha", AH), ("bf", 1), ("walpha2", 4 * P),
               ("wa", KB * RANK), ("wf", KB * BH)):
    COL[_n] = (_at, _at + _w)
    _at += _w
NCOL = _at


def misc_plan():
    keys = [("stat", 0), ("stat", 1)] + [("a", 0)] + [("z", h) for h in range(AH)]
    keys += [("vt", i, h) for i in range(3) for h in range(2)]
    keys += [("vs", 0), ("vs", 1), ("ks", 0)]
    keys += [("lv", 0, 0), ("lv", 0, 1), ("lv", 0, 2)]
    for l in LEVELS:
        keys += [("lv", l, i) for i in range(3 if l <= 8 else 2)]
    keys += [("lv", 128, 0), ("lv", 256, 0)]
    keys += [("ke", i) for i in range(3)] + [("sp", 0), ("sp", 1)]
    keys += [("o", b) for b in range(KB)]
    keys += [("kv", n, g) for n in range(SMP) for g in range(2)]
    keys += [("hn", h) for h in range(AH)]
    keys += [("stat", 2), ("stat", 3), ("f", 0)]
    keys += [("fvt", i, h) for i in range(3) for h in range(2)] + [("fvs", 0), ("fvs", 1)]
    keys += [("stat", 4)]
    keys += [("s", 0, 0), ("s", 0, 1)]
    for h in range(BH):
        if h + 1 < BH:
            keys += [("s", h + 1, 0), ("s", h + 1, 1)]
        keys += [("pt", h)]
    for n in range(SMP):
        for g in range(NPG):
            keys += [("kt", n, g, 0), ("kt", n, g, 1)]
    keys += [("lf", 0), ("lown", 0), ("sct", 0), ("pdt", 0)]
    keys += [("stat", 5), ("stat", 6)]
    count, plan = [0, 0, 0], {}
    for i, k in enumerate(keys):
        plan[k] = (i % 3, count[i % 3])
        count[i % 3] += 1
    return plan, keys


def build(nc, x_all, up_w, down_w, mix_w, small, level_masks, state_in, cache_k, cache_v, cache_f, table,
          y_out, k_out, v_out, lf_out, state_prompt, state_sample):
    f32, f32r = mybir.dt.float32, mybir.dt.float32r
    i32 = mybir.dt.int32
    ALU, ACT = mybir.AluOpType, mybir.ActivationFunctionType
    AX = mybir.AxisListType
    PLAN, PLAN_KEYS = misc_plan()
    n_phys = cache_k.shape[0]

    ctx = ExitStack()
    with ctx:
        def sb(name, shape, dt=f32, where=ctx):
            return where.enter_context(nc.sbuf_tensor(name, shape, dt))

        def sem(name):
            return ctx.enter_context(nc.semaphore(name))

        raw = [sb(f"raw{s}", [P, DNW]) for s in range(SLOTS)]
        w_hi = [sb(f"w_hi{s}", [P, DNW], f32r) for s in range(SLOTS)]
        w_lo = [sb(f"w_lo{s}", [P, DNW], f32r) for s in range(SLOTS)]
        X = sb("X", [P, KB, TOK])
        XG = sb("XG", [P, KB, TOK])
        XH = sb("XH", [P, KB, TOK], f32r)
        XL = sb("XL", [P, KB, TOK], f32r)
        RS = sb("RS", [P, TOK])
        rs_tmp = sb("rs_tmp", [P, TOK])
        SQ = sb("SQ", [P, 1, TOK])
        SS = sb("SS", [P, TOK])
        const = sb("const", [P, NCOL])
        tab = sb("tab", [1, SMP * NPG], i32)
        KVf = sb("KVf", [P, 2 * KB, TOK])
        Kf, Vf = KVf[:, 0:KB, :], KVf[:, KB:2 * KB, :]
        Vtok = sb("Vtok", [P, 3, D])
        Vs = sb("Vs", [SMP, D])
        ones = sb("ones", [P, PRM])
        LG = sb("LG", [BH, TOK])
        CC = sb("CC", [BH, PRM])

        def part(name):
            return const[:, COL[name][0]:COL[name][1]]
        ident = part("ident")
        gain = part("gain")
        wa = part("wa").rearrange("p (k r) -> p k r", k=KB)
        wf = part("wf").rearrange("p (k r) -> p k r", k=KB)

        with ExitStack() as s:
            HH = sb("HH", [P, FB, TOK], f32r, s)
            HL = sb("HL", [P, FB, TOK], f32r, s)
            g_s = sb("g_s", [P, 2, TOK], f32, s)
            sil = sb("sil", [P, 2, TOK], f32, s)
            u_s = sb("u_s", [P, 2, TOK], f32, s)
            h_s = sb("h_s", [P, 2, TOK], f32, s)
        with ExitStack() as s:
            QKVR = sb("QKVR", [P, 24, TOK], f32, s)
            BB = sb("BB", [P, AH, TOK], f32, s)
            EE = sb("EE", [P, AH, TOK], f32, s)
            M1 = sb("M1", [P, AH, TOK], f32, s)
            ST = sb("ST", [P, AH * (PRM + 144)], f32, s)
            ST2 = sb("ST2", [META, AH, META], f32, s)
            ela = sb("ela", [P, AH, SMP], f32, s)
            a_s = sb("a_s", [RANK, TOK], f32, s)
        ST0 = ST[:, 0:AH * PRM].rearrange("p (h t) -> p h t", h=AH)
        ST1 = ST[:, AH * PRM:].rearrange("p (h t) -> p h t", h=AH)
        Q, K, V, R = (QKVR[:, 0:4, :], QKVR[:, 4:8, :], QKVR[:, 8:16, :], QKVR[:, 16:24, :])
        KE = V.rearrange("p a t -> p (a t)")[:, 0:3 * AH * P].rearrange("p (i n) -> p i n", i=3)
        SPS = M1[:, :, 0:DV]
        spare = KVf[:, :, :].rearrange("p k t -> p (k t)")
        S0 = spare[:, 0:2 * AH * DV].rearrange("p (i h v) -> p i h v", i=2, h=AH)
        KM = spare[0:SMP, 2048:2048 + 2 * AH * P].rearrange("p (i n) -> p i n", i=2)
        Ks = spare[0:SMP, 3072:3072 + AH * P]
        masks = spare[:, 3584:3584 + len(LEVELS) * P].rearrange("p (l t) -> p l t", l=len(LEVELS))
        O = XG
        OSQ = QKVR[:, 0:KB, :]
        RH = BB
        with ExitStack() as s:
            Qf = sb("Qf", [P, KB, TOK], f32, s)
            PP = sb("PP", [P, 2, P + 2 * P + PRM], f32, s)
            PTs = sb("PTs", [P, 2, PRM + 144 + META], f32, s)
            NM = sb("NM", [P, 2, 3], f32, s)
            MX = sb("MX", [P, 2, 3], f32, s)
            RW = sb("RW", [P, 2, 3], f32, s)
            QB = sb("QB", [P, KB, SMP, 2], f32, s)
            KP = [sb(f"KP{i}", [P, D], f32, s) for i in range(2)]
            KT = sb("KT", [P, 2, KB, P], f32, s)
            VP = [sb(f"VP{i}", [P, D], f32, s) for i in range(4)]
            LFp = sb("LFp", [P, NPG, SMP, BH], f32, s)
            SC = sb("SC", [P, NPG, SMP, BH], f32, s)
            SO = sb("SO", [SMP, P], f32, s)
            LD = sb("LD", [P, 2 * P + 1], f32, s)
            SD = sb("SD", [P, 2 * P + 1], f32, s)
            PD = sb("PD", [P, 2 * P + 1], f32, s)
            own_t = sb("own_t", [P, 2, SMP], f32, s)
            PM = sb("PM", [P, SMP], f32, s)
            col = sb("col", [P, 4], f32, s)
            PDT = sb("PDT", [P, NPG, P], f32, s)
            PMT = sb("PMT", [SMP, P], f32, s)
            C8 = sb("C8", [BH, PRM], f32, s)
        CD = PD
        lt = Qf[0:BH, 0:3, :]

        bank = [ctx.enter_context(nc.psum_tensor(f"bank{i}", [P, 512], f32)) for i in range(4)]
        misc = [ctx.enter_context(nc.psum_tensor(f"misc{i}", [P, 512], f32)) for i in range(3)]
        held = ctx.enter_context(nc.psum_tensor("held", [P, 512], f32))

        raw_in = [sem(f"raw_in{s}") for s in range(SLOTS)]
        x_in, const_in = sem("x_in"), sem("const_in")
        hi_ready, lo_ready = sem("hi_ready"), sem("lo_ready")
        chunk_used = sem("chunk_used")
        bank_free = sem("bank_free")
        x_new = sem("x_new")
        ss_ready, rs_ready, rs_sq = sem("ss_ready"), sem("rs_ready"), sem("rs_sq")
        xg_ready, xh_ready, xl_ready = sem("xg_ready"), sem("xh_ready"), sem("xl_ready")
        g_ready, sil_ready, h_ready = sem("g_ready"), sem("sil_ready"), sem("h_ready")
        hh_ready, hid_ready = sem("hh_ready"), sem("hid_ready")
        misc_full = [sem(f"misc_full{i}") for i in range(3)]
        misc_free = [sem(f"misc_free{i}") for i in range(3)]
        held_full = sem("held_full")
        pool_step, dve_step, act_step = sem("pool_step"), sem("dve_step"), sem("act_step")
        a_ready, z_ready, l_ready = sem("a_ready"), sem("z_ready"), sem("l_ready")
        b_ready, d_ready, e_ready, m_ready, m_used = (sem(n) for n in (
            "b_ready", "d_ready", "e_ready", "m_ready", "m_used"))
        tok_ready, st_ready = sem("tok_ready"), sem("st_ready")
        ke_ready, sp_ready, sp_out = sem("ke_ready"), sem("sp_ready"), sem("sp_out")
        s_in = [sem("s_in0"), sem("s_in1")]
        s_out = [sem("s_out0"), sem("s_out1")]
        km_ready, s_ready, s_used = sem("km_ready"), sem("s_ready"), sem("s_used")
        o_ready, osq_ready, sr_ready = sem("o_ready"), sem("osq_ready"), sem("sr_ready")
        of_ready, oh_ready, ol_ready = sem("of_ready"), sem("oh_ready"), sem("ol_ready")
        rh_in, rh_out = sem("rh_in"), sem("rh_out")
        kvout, lf_in, lf_ready, lf_done = sem("kvout"), sem("lf_in"), sem("lf_ready"), sem("lf_done")
        ones_ready, ela_ready, qb_zero, fo_done = sem("ones_ready"), sem("ela_ready"), sem("qb_zero"), sem("fo_done")
        qb_ready, nm_ready, p_ready, pn_ready = sem("qb_ready"), sem("nm_ready"), sem("p_ready"), sem("pn_ready")
        pt_ready, fo_ready = sem("pt_ready"), sem("fo_ready")
        kp_in = [sem("kp_in0"), sem("kp_in1")]
        vp_in = [sem(f"vp_in{i}") for i in range(4)]
        qk_done = sem("qk_done")
        lfp_in, sc_ready, sd_ready, pd_ready, pe_ready, pv_done = (sem(n) for n in (
            "lfp_in", "sc_ready", "sd_ready", "pd_ready", "pe_ready", "pv_done"))
        po_read = sem("po_read")
        tab_in, y_ready, y_done = sem("tab_in"), sem("y_ready"), sem("y_done")

        block = ctx.enter_context(nc.Block())

        def full(eng, key):
            b, n = PLAN[key]
            eng.wait_ge(misc_full[b], n + 1)
            return misc[b]

        def freed(ins, key):
            ins.then_inc(misc_free[PLAN[key][0]], 1)

        def taken(eng, key):
            b, n = PLAN[key]
            eng.wait_ge(misc_free[b], n + 1)

        def in_pairs(eng, seg, split, use):
            n = COUNT[seg] // 2
            with eng.Fori(0, (n - 2) // 2) as i:
                split(seg, i, 1)
                use(i * 2, i, 0)
                split(seg, i + 1, 0)
                use(i * 2 + 1, i, 1)
            half = (n - 2) // 2
            split(seg, half, 1)
            use(n - 2, half, 0)
            if NEXT[seg]:
                split(NEXT[seg], 0, 0)
            use(n - 1, half, 1)

        @block.sync
        def _(sp):
            for s in range(SLOTS):
                sp.dma_start(raw[s][:, 0:UPW], up_w[s]).then_inc(raw_in[s], 16)
            for seg, n, tiles in SEGS:
                if tiles == DNT:
                    src, first = down_w, int(seg[3]) * 2 * KB
                elif seg.endswith("_up"):
                    src, first = up_w, int(seg[3]) * 2 * FB
                else:
                    src, first = mix_w, MIX0[seg]
                skip = SLOTS if CHUNK0[seg] == 0 else 0
                with sp.Fori(0, (n - skip) // SLOTS) as i:
                    for s in range(SLOTS):
                        sp.wait_ge(lo_ready, i * SLOTS + (CHUNK0[seg] + skip + s + 1 - SLOTS))
                        sp.dma_start(raw[s][:, 0:tiles * P],
                                     src[i * SLOTS + (first + skip + s)]).then_inc(raw_in[s], 16)
            sp.wait_ge(y_ready, KB)
            sp.dma_start(y_out.rearrange("k p t -> p k t"), XG[:, :, :]).then_inc(y_done, 16)
            sp.wait_ge(y_done, 16)

        @block.gpsimd
        def _(pool):
            steps = [0]

            def step(ins):
                steps[0] += 1
                ins.then_inc(pool_step, 1)
                pool.wait_ge(pool_step, steps[0])

            pool.dma_start(X[:, :, :], x_all.rearrange("k p t -> p k t")).then_inc(x_in, 16)
            pool.dma_start(const[:, :], small).then_inc(const_in, 16)
            pool.dma_start(masks, level_masks).then_inc(const_in, 16)
            pool.dma_start(tab[:, :], table).then_inc(tab_in, 16)
            nc.gpsimd.memset(ones[:, :], 1.0).then_inc(ones_ready, 1)

            def square_sum(stage):
                for m in range(KB):
                    if stage:
                        pool.wait_ge(x_new, KB * (stage - 1) + m + 3)
                    if m == 0:
                        step(nc.gpsimd.tensor_tensor(SS[:, :], X[:, 0, :], X[:, 0, :], ALU.mult))
                        continue
                    step(nc.gpsimd.tensor_tensor(SQ[:, 0, :], X[:, m, :], X[:, m, :], ALU.mult))
                    steps[0] += 1
                    nc.gpsimd.tensor_tensor(SS[:, :], SS[:, :], SQ[:, 0, :], ALU.add).then_inc(pool_step, 1)
                    pool.wait_ge(pool_step, steps[0])
                pool.sem_inc(ss_ready, 1)

            pool.wait_ge(x_in, 16)
            square_sum(0)
            square_sum(1)

            def store_state(n):
                taken(pool, ("kv", n, 1))
                pool.dma_start(state_sample[n].rearrange("h d v -> d h v"), S0[:, n % 2, :, :]).then_inc(s_out[n % 2], 16)

            for n in range(SMP):
                if n >= 2:
                    store_state(n - 2)
                    pool.wait_ge(s_used, n - 1)
                    pool.wait_ge(s_out[n % 2], 16 * (n // 2))
                pool.dma_start(S0[:, n % 2, :, :], state_in[n].rearrange("h d v -> d h v")).then_inc(s_in[n % 2], 16)
            store_state(SMP - 2)
            store_state(SMP - 1)
            taken(pool, ("sp", 1))
            pool.dma_start(state_prompt.rearrange("h d v -> d h v"), SPS).then_inc(sp_out, 16)
            square_sum(2)
            square_sum(3)

            pool.wait_ge(bank_free, SLOTS + UNIT0["kv_in"] + 16)
            pool.dma_start(k_out.rearrange("k p t -> p k t"), Kf[:, :, :]).then_inc(kvout, 16)
            pool.dma_start(v_out.rearrange("k p t -> p k t"), Vf[:, :, :]).then_inc(kvout, 16)
            pool.wait_ge(lf_ready, 1)
            pool.dma_start(lf_out, LG[:, :]).then_inc(lf_done, 16)
            square_sum(4)

            step(nc.gpsimd.memset(QB[:, :, :, :], 0.0))
            step(nc.gpsimd.memset(NM[:, :, :], 0.0))
            step(nc.gpsimd.memset(MX[:, :, :], 0.0))
            step(nc.gpsimd.memset(RW[:, :, :], 1.0))
            pool.sem_inc(qb_zero, 1)
            pool.wait_ge(tab_in, 16)
            for n in range(SMP):
                for g in range(NPG):
                    i = n * NPG + g
                    page = pool.value_load(tab[0:1, i:i + 1], min_val=0, max_val=n_phys - 1)
                    pool.dma_start(LFp[:, g, n, :], cache_f[page]).then_inc(lfp_in, 16)
                    if i >= 2:
                        full(pool, ("kt", n - 1, g, 1))
                    pool.dma_start(KP[i % 2][:, :], cache_k[page]).then_inc(kp_in[i % 2], 16)
            for i in range(SMP * NPG):
                if i >= 4:
                    pool.wait_ge(pv_done, (i - 4) // 2 + 1)
                page = pool.value_load(tab[0:1, i:i + 1], min_val=0, max_val=n_phys - 1)
                pool.dma_start(VP[i % 4][:, :], cache_v[page]).then_inc(vp_in[i % 4], 16)
            square_sum(5)
            square_sum(6)
            for o in range(2):
                pool.wait_ge(s_out[o], 16 * SMP // 2)
            pool.wait_ge(sp_out, 16)
            pool.wait_ge(kvout, 32)
            pool.wait_ge(lf_done, 16)

        @block.scalar
        def _(act):
            steps = [0]

            def step(ins):
                steps[0] += 1
                ins.then_inc(act_step, 1)
                act.wait_ge(act_step, steps[0])

            def split(seg, half, par):
                w = TILES[seg] * P
                for k in range(2):
                    s = 2 * par + k
                    c = half * 4 + (CHUNK0[seg] + s)
                    act.wait_ge(raw_in[s], half * 16 + 16 * (CHUNK0[seg] // 4 + 1))
                    act.wait_ge(chunk_used, c + 1)
                    nc.scalar.activation(w_hi[s][:, 0:w], raw[s][:, 0:w], ACT.Copy).then_inc(hi_ready, 1)

            def norm_root(n):
                act.wait_ge(rs_sq, n + 1)
                nc.scalar.activation(RS[:, :], rs_tmp[:, :], ACT.Sqrt).then_inc(rs_ready, 1)

            def prep(name, m):
                n = m + KB * GAIN[name]
                act.wait_ge(xg_ready, n + 1)
                nc.scalar.activation(XH[:, bass.ds(m, 1), :].rearrange("p a t -> p (a t)"),
                                     XG[:, bass.ds(m, 1), :].rearrange("p a t -> p (a t)"), ACT.Copy).then_inc(xh_ready, 1)

            def ffn(n):
                f0 = n * FB

                def hidden(f, half, par):
                    act.wait_ge(g_ready, f + (f0 + 1))
                    nc.scalar.activation(sil[:, par, :], g_s[:, par, :], ACT.Silu).then_inc(sil_ready, 1)
                    act.wait_ge(h_ready, f + (f0 + 1))
                    nc.scalar.activation(HH[:, bass.ds(f, 1), :].rearrange("p a t -> p (a t)"),
                                         h_s[:, par, :], ACT.Copy).then_inc(hh_ready, 1)

                in_pairs(act, f"ffn{n}_up", split, hidden)
                after = GAINS[GAIN[f"ffn{n}"] + 1]
                in_pairs(act, f"ffn{n}_down", split,
                         lambda m, half, par: prep(after, m) if after != "final" else None)

            act.wait_ge(x_in, 16)
            act.wait_ge(const_in, 32)
            for m in range(KB):
                prep("ffn0", m)
            split("ffn0_up", 0, 0)
            norm_root(0)
            ffn(0)

            norm_root(1)
            for h in range(AH):
                taken(act, ("z", h))
            step(nc.scalar.activation(EE[:, :, :], M1[:, :, :], ACT.Abs))
            step(nc.scalar.activation(EE[:, :, :], EE[:, :, :], ACT.Exp, scale=-1.0))
            nc.scalar.activation(EE[:, :, :], EE[:, :, :], ACT.Ln, bias=1.0).then_inc(l_ready, 1)
            act.wait_ge(b_ready, 1)
            nc.scalar.activation(ela[:, :, :], M1[:, :, PRM:TOK], ACT.Exp, scale=1.0 / 16).then_inc(ela_ready, 1)
            in_pairs(act, "gla_in", split, lambda g, half, par: None)
            for i in range(3):
                rows = P if i < 2 else META
                for h in range(2):
                    b = full(act, ("vt", i, h))
                    freed(nc.scalar.activation(Vtok[0:rows, i, h * 512:(h + 1) * 512], b[0:rows, :], ACT.Copy), ("vt", i, h))
            for h in range(2):
                b = full(act, ("vs", h))
                freed(nc.scalar.activation(Vs[:, h * 512:(h + 1) * 512], b[0:SMP, :], ACT.Copy), ("vs", h))
            b = full(act, ("ks", 0))
            freed(nc.scalar.activation(Ks[:, :], b[0:SMP, :], ACT.Copy), ("ks", 0))
            for l in range(len(LEVELS) + 3):
                act.wait_ge(d_ready, l + 1)
                nc.scalar.activation(EE[:, :, 0:PRM], EE[:, :, 0:PRM], ACT.Exp, scale=1.0 / 16).then_inc(e_ready, 1)
            for i in range(3):
                rows = P if i < 2 else META
                b = full(act, ("ke", i))
                freed(nc.scalar.activation(KE[0:rows, i, :], b[0:rows, :], ACT.Copy), ("ke", i))
            for g in range(2):
                b = full(act, ("sp", g))
                freed(nc.scalar.activation(SPS[:, 2 * g:2 * g + 2, :], b[:, :].rearrange("p (h v) -> p h v", h=2), ACT.Copy), ("sp", g))
            act.wait_ge(o_ready, 1)
            nc.scalar.activation(OSQ, O[:, :, :], ACT.Square).then_inc(osq_ready, 1)
            nc.scalar.activation(R, R, ACT.Silu).then_inc(sr_ready, 1)
            act.wait_ge(rh_in, 1)
            nc.scalar.activation(RH[:, :, :], RH[:, :, :], ACT.Sqrt).then_inc(rh_out, 1)
            act.wait_ge(of_ready, 1)
            act.wait_ge(s_out[0], 16 * SMP // 2)
            act.wait_ge(s_out[1], 16 * SMP // 2)
            act.wait_ge(sp_out, 16)
            nc.scalar.activation(HH[:, 0:KB, :], XG[:, :, :], ACT.Copy).then_inc(oh_ready, 1)
            in_pairs(act, "gla_out", split, lambda g, half, par: [prep("ffn1", 2 * g + k) for k in range(2)])
            norm_root(2)
            ffn(1)

            norm_root(3)
            in_pairs(act, "kv_in", split, lambda g, half, par: None)
            act.wait_ge(lf_in, 1)
            step(nc.scalar.activation(lt[:, 1, :], lt[:, 0, :], ACT.Abs))
            step(nc.scalar.activation(lt[:, 1, :], lt[:, 1, :], ACT.Exp, scale=-1.0))
            nc.scalar.activation(lt[:, 1, :], lt[:, 1, :], ACT.Ln, bias=1.0).then_inc(l_ready, 1)
            for i in range(3):
                rows = P if i < 2 else META
                for h in range(2):
                    b = full(act, ("fvt", i, h))
                    freed(nc.scalar.activation(Vtok[0:rows, i, h * 512:(h + 1) * 512], b[0:rows, :], ACT.Copy), ("fvt", i, h))
            for h in range(2):
                b = full(act, ("fvs", h))
                freed(nc.scalar.activation(Vs[:, h * 512:(h + 1) * 512], b[0:SMP, :], ACT.Copy), ("fvs", h))
            for m in range(KB):
                prep("ffn2", m)
            act.wait_ge(lf_ready, 1)
            ffn(2)

            norm_root(4)
            in_pairs(act, "fox_q", split, lambda g, half, par: None)

            def attend(h):
                q = h % 2
                for i, (key, rows, src, dst) in enumerate((
                        (("s", h, 0), P, slice(0, P), PP[:, q, 0:P]),
                        (("s", h, 0), P, slice(P, 3 * P), PP[:, q, P:3 * P]),
                        (("s", h, 1), META, slice(0, PRM), PP[0:META, q, 3 * P:3 * P + PRM]))):
                    if i != 1:
                        full(act, key)
                    act.wait_ge(nm_ready, 2 * h + (1 if i < 2 else 2))
                    ins = nc.scalar.activation(dst, misc[PLAN[key][0]][0:rows, src], ACT.Exp,
                                               bias=NM[0:rows, q, i:i + 1], scale=HD ** -0.5,
                                               accum_out=RW[0:rows, q, i:i + 1])
                    if i:
                        freed(ins, key)

            attend(0)
            for h in range(BH):
                if h + 1 < BH:
                    attend(h + 1)
                b = full(act, ("pt", h))
                if h >= 2:
                    act.wait_ge(fo_done, h - 1)
                nc.scalar.activation(PTs[:, h % 2, 0:PRM + 144], b[:, 0:PRM + 144], ACT.Copy)
                ins = nc.scalar.activation(PTs[0:META, h % 2, PRM + 144:PRM + 144 + META],
                                           b[0:META, PRM + 144:PRM + 144 + META], ACT.Copy)
                freed(ins, ("pt", h))
            for i in range(SMP * NPG):
                b = full(act, ("kt", i // NPG, i % NPG, 0))
                if i >= 2:
                    act.wait_ge(qk_done, i - 1)
                ins = nc.scalar.activation(KT[:, i % 2, 0:4, :], b[:, :].rearrange("p (j s) -> p j s", j=4), ACT.Copy)
                freed(ins, ("kt", i // NPG, i % NPG, 0))
            act.wait_ge(sd_ready, 1)
            nc.scalar.activation(PD[:, :], SD[:, :], ACT.Exp, bias=col[:, 0:1], accum_out=col[:, 1:2]).then_inc(pd_ready, 1)
            act.wait_ge(of_ready, 2)
            nc.scalar.activation(HH[:, 0:KB, :], XG[:, :, :], ACT.Copy).then_inc(oh_ready, 1)
            in_pairs(act, "fox_out", split, lambda g, half, par: [prep("ffn3", 2 * g + k) for k in range(2)])
            norm_root(5)
            ffn(3)
            norm_root(6)

        @block.vector
        def _(dve):
            steps = [0]

            def step(ins):
                steps[0] += 1
                ins.then_inc(dve_step, 1)
                dve.wait_ge(dve_step, steps[0])

            def split(seg, half, par):
                w = TILES[seg] * P
                for k in range(2):
                    s = 2 * par + k
                    c = half * 4 + (CHUNK0[seg] + s)
                    dve.wait_ge(hi_ready, c + 1)
                    nc.vector.tensor_tensor(w_lo[s][:, 0:w], raw[s][:, 0:w],
                                            w_hi[s][:, 0:w].bitcast(f32), ALU.subtract).then_inc(lo_ready, 1)

            def block_of(t, m):
                return t[:, bass.ds(m, 1), :].rearrange("p a t -> p (a t)")

            def norm_square(n):
                b = full(dve, ("stat", n))
                ins = nc.vector.tensor_scalar(rs_tmp[:, :], b[:, 0:TOK], EPS, None, ALU.add)
                freed(ins, ("stat", n))
                dve.wait_ge(misc_free[PLAN[("stat", n)][0]], PLAN[("stat", n)][1] + 1)
                nc.vector.reciprocal(rs_tmp[:, :], rs_tmp[:, :]).then_inc(rs_sq, 1)

            def prep(name, m):
                n = m + KB * GAIN[name]
                nc.vector.tensor_scalar(block_of(XG, m), block_of(X, m), gain[:, bass.ds(n, 1)], None,
                                        ALU.mult).then_inc(xg_ready, 1)
                dve.wait_ge(xh_ready, n + 1)
                nc.vector.tensor_tensor(block_of(XL, m), block_of(XG, m), block_of(XH, m).bitcast(f32),
                                        ALU.subtract).then_inc(xl_ready, 1)

            def residual(seg, stage, scale, after, m, b):
                per = 1 if TILES[seg] == KB else 2
                dve.wait_ge(chunk_used, m * per + (SLOTS + CHUNK0[seg] + per))
                ins = nc.vector.scalar_tensor_tensor(block_of(X, m), bank[b][:, 0:TOK], scale, block_of(X, m),
                                                     ALU.mult, ALU.add)
                ins.then_inc(x_new, 1)
                dve.wait_ge(x_new, m + (KB * (stage - 1) + 3))
                if after != "final":
                    prep(after, m)

            def scaled(seg, dst):
                def use(g, half, par):
                    for k in range(2):
                        dve.wait_ge(chunk_used, g * 2 + (SLOTS + CHUNK0[seg] + k + 1))
                        nc.vector.tensor_tensor(block_of(dst, g * 2 + k), bank[2 * par + k][:, 0:TOK], RS[:, :],
                                                ALU.mult).then_inc(bank_free, 1)
                return use

            def ffn(n, after, stage):
                f0, seg = n * FB, f"ffn{n}_up"

                def hidden(f, half, par):
                    u = f * 2 + UNIT0[seg]
                    c = f * 2 + (SLOTS + CHUNK0[seg])
                    dve.wait_ge(chunk_used, c + 1)
                    nc.vector.tensor_tensor(g_s[:, par, :], bank[2 * par][:, 0:TOK], RS[:, :], ALU.mult).then_inc(g_ready, 1)
                    dve.wait_ge(chunk_used, c + 2)
                    nc.vector.tensor_tensor(u_s[:, par, :], bank[2 * par + 1][:, 0:TOK], RS[:, :],
                                            ALU.mult).then_inc(bank_free, 2)
                    dve.wait_ge(bank_free, u + (SLOTS + 2))
                    dve.wait_ge(sil_ready, f + (f0 + 1))
                    nc.vector.tensor_tensor(h_s[:, par, :], sil[:, par, :], u_s[:, par, :], ALU.mult).then_inc(h_ready, 1)
                    dve.wait_ge(hh_ready, f + (f0 + 1))
                    nc.vector.tensor_tensor(block_of(HL, f), h_s[:, par, :], block_of(HH, f).bitcast(f32),
                                            ALU.subtract).then_inc(hid_ready, 1)

                in_pairs(dve, seg, split, hidden)
                in_pairs(dve, f"ffn{n}_down", split,
                         lambda m, half, par: residual(f"ffn{n}_down", stage, 0.5, after, m, par))

            dve.sem_inc(bank_free, SLOTS)
            dve.sem_inc(x_new, 2)
            dve.wait_ge(x_in, 16)
            dve.wait_ge(const_in, 32)
            for m in range(KB):
                prep("ffn0", m)
            split("ffn0_up", 0, 0)
            norm_square(0)
            dve.wait_ge(rs_ready, 1)
            ffn(0, "gla", 1)

            norm_square(1)
            dve.wait_ge(rs_ready, 2)
            b = full(dve, ("a", 0))
            freed(nc.vector.tensor_tensor(a_s[:, :], b[0:RANK, 0:TOK], RS[0:RANK, :], ALU.mult), ("a", 0))
            for h in range(AH):
                b = full(dve, ("z", h))
                freed(nc.vector.tensor_scalar(M1[:, h, :], b[:, 0:TOK], part("balpha")[:, h:h + 1], None, ALU.add), ("z", h))
            dve.wait_ge(l_ready, 1)
            step(nc.vector.tensor_scalar(M1[:, :, :], M1[:, :, :], 0.0, None, ALU.min))
            step(nc.vector.tensor_tensor(M1[:, :, :], M1[:, :, :], EE[:, :, :], ALU.subtract))
            dve.wait_ge(ones_ready, 1)
            for h in range(AH):
                step(nc.vector.tensor_tensor_scan(BB[:, h, 0:PRM], ones[:, :], M1[:, h, 0:PRM], 0.0, ALU.mult, ALU.add))
            dve.sem_inc(b_ready, 1)
            in_pairs(dve, "gla_in", split, scaled("gla_in", QKVR))

            b = full(dve, ("lv", 0, 0))
            freed(nc.vector.tensor_tensor(ST0[:, :, 0:P], b[:, :].rearrange("p (h t) -> p h t", h=AH),
                                          ident.unsqueeze(1).to_broadcast([P, AH, P]), ALU.mult), ("lv", 0, 0))
            b = full(dve, ("lv", 0, 1))
            freed(nc.vector.tensor_tensor(ST1[:, :, 0:P], b[:, :].rearrange("p (h t) -> p h t", h=AH),
                                          ident.unsqueeze(1).to_broadcast([P, AH, P]), ALU.mult), ("lv", 0, 1))
            b = full(dve, ("lv", 0, 2))
            freed(nc.vector.tensor_tensor(ST2[:, :, :], b[0:META, 0:AH * META].rearrange("p (h t) -> p h t", h=AH),
                                          ident[0:META, 0:META].unsqueeze(1).to_broadcast([META, AH, META]),
                                          ALU.mult), ("lv", 0, 2))
            for li, l in enumerate(LEVELS + [128, 256]):
                if l == 256:
                    lo_ = lambda t: t[:, :, 0:256]
                    hi_ = lambda t: t[:, :, 256:PRM]
                    ref = BB[:, :, 255:256]
                    lshape, rshape = [P, AH, 256], [P, AH, META]
                else:
                    n = (PRM if l <= 8 else 256) // (2 * l)
                    view = lambda t: t[:, :, 0:2 * l * n].rearrange("p h (n l) -> p h n l", l=2 * l)
                    lo_ = lambda t: view(t)[:, :, :, 0:l]
                    hi_ = lambda t: view(t)[:, :, :, l:2 * l]
                    ref = view(BB)[:, :, :, l - 1:l]
                    lshape = rshape = [P, AH, n, l]
                if li:
                    dve.wait_ge(m_ready, li)
                nc.vector.tensor_tensor(lo_(EE), ref.to_broadcast(lshape), lo_(BB), ALU.subtract)
                ins = nc.vector.tensor_tensor(hi_(EE), hi_(BB), ref.to_broadcast(rshape), ALU.subtract)
                ins.then_inc(d_ready, 1)
                dve.wait_ge(e_ready, li + 1)
                nc.vector.tensor_tensor(lo_(M1), lo_(EE), lo_(K), ALU.mult)
                nc.vector.tensor_tensor(hi_(M1), hi_(EE), hi_(Q), ALU.mult).then_inc(m_ready, 1)
                if l < 128:
                    for i, S in enumerate((ST0, ST1, ST2)[0:3 if l <= 8 else 2]):
                        b = full(dve, ("lv", l, i))
                        r = META if i == 2 else P
                        freed(nc.vector.copy_predicated(
                            S[:, :, 0:r], masks[0:r, li, 0:r].bitcast(i32).unsqueeze(1).to_broadcast([r, AH, r]),
                            b[0:r, 0:AH * r].rearrange("p (h t) -> p h t", h=AH)), ("lv", l, i))
                elif l == 128:
                    b = full(dve, ("lv", 128, 0))
                    freed(nc.vector.tensor_copy(ST0[:, :, P:256], b[:, :].rearrange("p (h t) -> p h t", h=AH)), ("lv", 128, 0))
                else:
                    b = full(dve, ("lv", 256, 0))
                    nc.vector.tensor_copy(ST0[:, :, 256:PRM], b[:, 0:64].rearrange("p (h t) -> p h t", h=AH))
                    freed(nc.vector.tensor_copy(ST1[:, :, P:144], b[:, 64:128].rearrange("p (h t) -> p h t", h=AH)), ("lv", 256, 0))
            dve.wait_ge(m_ready, len(LEVELS) + 2)
            nc.vector.tensor_tensor(EE[:, :, 0:PRM], BB[:, :, PRM - 1:PRM].to_broadcast([P, AH, PRM]), BB[:, :, 0:PRM],
                                    ALU.subtract).then_inc(d_ready, 1)
            dve.wait_ge(e_ready, len(LEVELS) + 3)
            nc.vector.tensor_tensor(M1[:, :, 0:PRM], EE[:, :, 0:PRM], K[:, :, 0:PRM], ALU.mult).then_inc(m_ready, 1)
            for o in range(KB):
                b = full(dve, ("o", o))
                freed(nc.vector.tensor_scalar(O[:, o, 0:PRM], b[:, 0:PRM], P ** -0.5, None, ALU.mult), ("o", o))

            dve.wait_ge(ela_ready, 1)
            dve.wait_ge(misc_free[PLAN[("ks", 0)][0]], PLAN[("ks", 0)][1] + 1)
            for n in range(SMP):
                if n >= 2:
                    dve.wait_ge(misc_full[PLAN[("kv", n - 2, 1)][0]], PLAN[("kv", n - 2, 1)][1] + 1)
                nc.vector.tensor_scalar(KM[:, n % 2, :], Ks[:, :], ident[0:SMP, n:n + 1], None, ALU.mult).then_inc(km_ready, 1)
                dve.wait_ge(s_in[n % 2], 16 * (n // 2 + 1))
                for g in range(2):
                    b = full(dve, ("kv", n, g))
                    for k in range(2):
                        h = 2 * g + k
                        ins = nc.vector.scalar_tensor_tensor(S0[:, n % 2, h, :], S0[:, n % 2, h, :], ela[:, h, n:n + 1],
                                                             b[:, k * DV:(k + 1) * DV], ALU.mult, ALU.add)
                    freed(ins, ("kv", n, g))
            dve.wait_ge(s_used, SMP)
            nc.vector.tensor_scalar(O[:, :, PRM:TOK], held[:, 0:KB * SMP].rearrange("p (b n) -> p b n", b=KB),
                                    P ** -0.5, None, ALU.mult).then_inc(o_ready, 1)
            for h in range(AH):
                b = full(dve, ("hn", h))
                freed(nc.vector.tensor_scalar(RH[:, h, :], b[:, 0:TOK], EPS, None, ALU.add), ("hn", h))
            last = ("hn", AH - 1)
            dve.wait_ge(misc_free[PLAN[last][0]], PLAN[last][1] + 1)
            nc.vector.reciprocal(RH[:, :, :], RH[:, :, :]).then_inc(rh_in, 1)
            dve.wait_ge(rh_out, 1)
            dve.wait_ge(sr_ready, 1)
            heads = lambda t: t.rearrange("p (h j) t -> p h j t", j=2)
            for j in range(2):
                step(nc.vector.tensor_tensor(heads(O[:, :, :])[:, :, j, :], heads(O[:, :, :])[:, :, j, :], RH[:, :, :], ALU.mult))
            for j in range(2):
                ins = nc.vector.scalar_tensor_tensor(heads(O[:, :, :])[:, :, j, :], heads(O[:, :, :])[:, :, j, :],
                                                     part("ghead")[:, j:j + 1], heads(R)[:, :, j, :], ALU.mult, ALU.mult)
            ins.then_inc(of_ready, 1)
            dve.wait_ge(s_out[0], 16 * SMP // 2)
            dve.wait_ge(s_out[1], 16 * SMP // 2)
            dve.wait_ge(sp_out, 16)
            dve.wait_ge(oh_ready, 1)
            nc.vector.tensor_tensor(HL[:, 0:KB, :], XG[:, :, :], HH[:, 0:KB, :].bitcast(f32), ALU.subtract).then_inc(ol_ready, 1)
            in_pairs(dve, "gla_out", split, lambda g, half, par: [
                residual("gla_out", 2, 1.0, "ffn1", 2 * g + k, 2 * par + k) for k in range(2)])
            norm_square(2)
            dve.wait_ge(rs_ready, 3)
            ffn(1, "kv", 3)

            norm_square(3)
            dve.wait_ge(rs_ready, 4)
            in_pairs(dve, "kv_in", split, scaled("kv_in", KVf))
            b = full(dve, ("f", 0))
            ins = nc.vector.tensor_tensor(lt[:, 2, :], b[0:BH, 0:TOK], RS[0:BH, :], ALU.mult)
            freed(ins, ("f", 0))
            dve.wait_ge(misc_free[PLAN[("f", 0)][0]], PLAN[("f", 0)][1] + 1)
            nc.vector.tensor_scalar(lt[:, 0, :], lt[:, 2, :], part("bf")[0:BH, :], None, ALU.add).then_inc(lf_in, 1)
            dve.wait_ge(l_ready, 2)
            step(nc.vector.tensor_scalar(lt[:, 0, :], lt[:, 0, :], 0.0, None, ALU.min))
            step(nc.vector.tensor_tensor(LG[:, :], lt[:, 0, :], lt[:, 1, :], ALU.subtract))
            nc.vector.tensor_tensor_scan(CC[:, :], ones[0:BH, :], LG[:, 0:PRM], 0.0, ALU.mult, ALU.add).then_inc(lf_ready, 1)
            for m in range(KB):
                prep("ffn2", m)
            ffn(2, "fox", 4)

            norm_square(4)
            dve.wait_ge(rs_ready, 5)
            in_pairs(dve, "fox_q", split, scaled("fox_q", Qf))
            dve.wait_ge(bank_free, SLOTS + UNIT0["fox_q"] + KB)
            dve.wait_ge(qb_zero, 1)
            nc.vector.tensor_scalar(C8[:, :], CC[:, :], -(HD ** 0.5), None, ALU.mult).then_inc(qb_ready, 1)
            for e in range(2):
                r = slice(HD * e, HD * (e + 1))
                nc.vector.tensor_copy(QB[r, :, :, e], Qf[r, :, PRM:TOK]).then_inc(qb_ready, 1)

            def maxima(h):
                q = h % 2
                b = full(dve, ("s", h, 0))
                if h >= 2:
                    taken(dve, ("s", h - 2, 1))
                nc.vector.reduce_max(MX[:, q, 0:1], b[:, 0:P], AX.X)
                step(nc.vector.reduce_max(MX[:, q, 1:2], b[:, P:3 * P], AX.X))
                nc.vector.tensor_scalar(NM[:, q, 0:2], MX[:, q, 0:2], -(HD ** -0.5), None, ALU.mult).then_inc(nm_ready, 1)
                b = full(dve, ("s", h, 1))
                step(nc.vector.reduce_max(MX[0:META, q, 2:3], b[0:META, 0:PRM], AX.X))
                nc.vector.tensor_scalar(NM[0:META, q, 2:3], MX[0:META, q, 2:3], -(HD ** -0.5), None,
                                        ALU.mult).then_inc(nm_ready, 1)

            maxima(0)
            for h in range(BH):
                q = h % 2
                if h + 1 < BH:
                    maxima(h + 1)
                taken(dve, ("s", h, 1))
                step(nc.vector.reciprocal(RW[:, q, :], RW[:, q, :]))
                nc.vector.tensor_scalar(PP[:, q, 0:P], PP[:, q, 0:P], RW[:, q, 0:1], None, ALU.mult)
                nc.vector.tensor_scalar(PP[:, q, P:3 * P], PP[:, q, P:3 * P], RW[:, q, 1:2], None, ALU.mult)
                nc.vector.tensor_scalar(PP[0:META, q, 3 * P:], PP[0:META, q, 3 * P:], RW[0:META, q, 2:3], None,
                                        ALU.mult).then_inc(pn_ready, 1)
                if q:
                    dve.wait_ge(fo_done, h + 1)
                    nc.vector.tensor_copy(XG[:, h // 2, 0:PRM], held[:, 0:PRM]).then_inc(po_read, 1)
            for i in range(SMP * NPG):
                key = ("kt", i // NPG, i % NPG, 1)
                b = full(dve, key)
                if i >= 2:
                    dve.wait_ge(qk_done, i - 1)
                ins = nc.vector.tensor_copy(KT[:, i % 2, 4:8, :], b[:, :].rearrange("p (j s) -> p j s", j=4))
                freed(ins, key)
            dve.wait_ge(qk_done, SMP * NPG + 1)
            nc.vector.tensor_copy(SC[:, :, :, :].rearrange("p g n h -> p (g n h)"), held[:, 0:2 * P])
            nc.vector.tensor_copy(SO[:, :], held[0:SMP, 2 * P:3 * P]).then_inc(sc_ready, 1)
            b = full(dve, ("lf", 0))
            freed(nc.vector.tensor_copy(LD[:, 0:2 * P], b[:, 0:2 * P]), ("lf", 0))
            b = full(dve, ("lown", 0))
            ins = nc.vector.tensor_tensor(own_t[:, 0, :], b[:, 0:SMP], part("own"), ALU.mult)
            freed(ins, ("lown", 0))
            dve.wait_ge(misc_free[PLAN[("lown", 0)][0]], PLAN[("lown", 0)][1] + 1)
            step(nc.vector.reduce_sum(LD[:, 2 * P:2 * P + 1], own_t[:, 0, :], AX.X))
            step(nc.vector.tensor_tensor_scan(CD[:, :], ones[:, 0:2 * P + 1], LD[:, :], 0.0, ALU.mult, ALU.add))
            step(nc.vector.tensor_scalar(LD[:, :], CD[:, :], -1.0, CD[:, 2 * P:2 * P + 1], ALU.mult, ALU.add))
            b = full(dve, ("sct", 0))
            step(nc.vector.tensor_tensor(own_t[:, 1, :], b[:, 2 * P:2 * P + SMP], part("own"), ALU.mult))
            step(nc.vector.reduce_sum(col[:, 2:3], own_t[:, 1, :], AX.X))
            nc.vector.scalar_tensor_tensor(SD[:, 2 * P:2 * P + 1], col[:, 2:3], HD ** -0.5, LD[:, 2 * P:2 * P + 1],
                                           ALU.mult, ALU.add)
            ins = nc.vector.scalar_tensor_tensor(SD[:, 0:2 * P], b[:, 0:2 * P], HD ** -0.5, LD[:, 0:2 * P],
                                                 ALU.mult, ALU.add)
            freed(ins, ("sct", 0))
            dve.wait_ge(misc_free[PLAN[("sct", 0)][0]], PLAN[("sct", 0)][1] + 1)
            nc.vector.tensor_reduce(col[:, 0:1], SD[:, :], AX.X, ALU.max, negate=True).then_inc(sd_ready, 1)
            dve.wait_ge(pd_ready, 1)
            step(nc.vector.reciprocal(col[:, 3:4], col[:, 1:2]))
            step(nc.vector.tensor_scalar(PD[:, :], PD[:, :], col[:, 3:4], None, ALU.mult))
            nc.vector.tensor_scalar(PM[:, :], part("own"), PD[:, 2 * P:2 * P + 1], None, ALU.mult).then_inc(pe_ready, 1)
            b = full(dve, ("pdt", 0))
            nc.vector.tensor_copy(PDT[:, :, :], b[:, 0:2 * P].rearrange("p (g c) -> p g c", g=NPG))
            ins = nc.vector.tensor_copy(PMT[:, :], b[0:SMP, 2 * P:3 * P])
            freed(ins, ("pdt", 0))
            dve.wait_ge(pv_done, SMP)
            ov = held[:, 0:KB * SMP * 2].rearrange("p (k n e) -> p k n e", k=KB, e=2)
            for e in range(2):
                r = slice(HD * e, HD * (e + 1))
                ins = nc.vector.tensor_copy(XG[r, :, PRM:TOK], ov[r, :, :, e])
                (ins.then_inc(of_ready, 1) if e else None)
            dve.wait_ge(oh_ready, 2)
            nc.vector.tensor_tensor(HL[:, 0:KB, :], XG[:, :, :], HH[:, 0:KB, :].bitcast(f32), ALU.subtract).then_inc(ol_ready, 1)
            in_pairs(dve, "fox_out", split, lambda g, half, par: [
                residual("fox_out", 5, 1.0, "ffn3", 2 * g + k, 2 * par + k) for k in range(2)])
            norm_square(5)
            dve.wait_ge(rs_ready, 6)
            ffn(3, "final", 6)
            norm_square(6)
            dve.wait_ge(rs_ready, 7)
            for m in range(KB):
                nc.vector.scalar_tensor_tensor(XG[:, m, :], X[:, m, :], gain[:, 7 * KB + m:7 * KB + m + 1], RS[:, :],
                                               ALU.mult, ALU.mult).then_inc(y_ready, 1)

        @block.tensor
        def _(pe):
            mm = nc.tensor.matmul

            def empty(key):
                b, n = PLAN[key]
                if n:
                    pe.wait_ge(misc_free[b], n)
                return misc[b]

            def filled(ins, key):
                ins.then_inc(misc_full[PLAN[key][0]], 1)

            def products(out, s, act_hi, act_lo, k0, tiles, first, last):
                for k in range(tiles):
                    wh, wl = w_hi[s][:, k * P:(k + 1) * P], w_lo[s][:, k * P:(k + 1) * P]
                    mm(out, wh, act_hi[:, k0 + k, :], start=first and k == 0, stop=False)
                    mm(out, wh, act_lo[:, k0 + k, :], start=False, stop=False)
                    ins = mm(out, wl, act_hi[:, k0 + k, :], start=False, stop=last and k == tiles - 1)
                return ins

            def project(seg, act_hi, act_lo, stage=None):
                with pe.Fori(0, COUNT[seg] // SLOTS) as i:
                    for s in range(SLOTS):
                        pe.wait_ge(lo_ready, i * SLOTS + (CHUNK0[seg] + s + 1))
                        if stage:
                            pe.wait_ge(x_new, i * SLOTS + (KB * (stage - 1) + s + 1))
                        else:
                            pe.wait_ge(bank_free, i * SLOTS + (UNIT0[seg] + s + 1))
                        products(bank[s][:, 0:TOK], s, act_hi, act_lo, 0, KB, True, True).then_inc(chunk_used, 1)

            def down(n, stage):
                seg = f"ffn{n}_down"
                pe.wait_ge(hid_ready, FB * (n + 1))
                with pe.Fori(0, COUNT[seg] // SLOTS) as i:
                    for s in range(SLOTS):
                        u = s // 2
                        pe.wait_ge(lo_ready, i * SLOTS + (CHUNK0[seg] + s + 1))
                        if s % 2 == 0:
                            pe.wait_ge(x_new, i * 2 + (KB * (stage - 1) + u + 1))
                        products(bank[u][:, 0:TOK], s, HH, HL, DNT * (s % 2), DNT, s % 2 == 0,
                                 s % 2 == 1).then_inc(chunk_used, 1)

            def stat(n):
                pe.wait_ge(ss_ready, n + 1)
                b = empty(("stat", n))
                filled(mm(b[:, 0:TOK], part("mean_d"), SS[:, :], start=True, stop=True), ("stat", n))

            pe.sem_inc(chunk_used, SLOTS)
            pe.wait_ge(const_in, 32)
            stat(0)
            pe.wait_ge(xl_ready, KB)
            project("ffn0_up", XH, XL)
            down(0, 1)
            stat(1)

            pe.wait_ge(xl_ready, KB * 2)
            b = empty(("a", 0))
            for k in range(KB):
                ins = mm(b[0:RANK, 0:TOK], wa[:, k, :], XG[:, k, :], start=k == 0, stop=k == KB - 1)
            filled(ins, ("a", 0))
            taken(pe, ("a", 0))
            for h in range(AH):
                b = empty(("z", h))
                filled(mm(b[:, 0:TOK], part("walpha2")[0:RANK, h * P:(h + 1) * P], a_s[:, :], start=True, stop=True), ("z", h))
            project("gla_in", XH, XL)
            pe.wait_ge(bank_free, SLOTS + UNIT0["gla_in"] + 24)

            def token_major(src, names):
                for i in range(3):
                    rows = P if i < 2 else META
                    for h in range(2):
                        b = empty((names[0], i, h))
                        for k in range(4):
                            ins = nc.tensor.transpose(b[0:rows, k * P:(k + 1) * P], src[:, 4 * h + k, i * P:i * P + rows], ident)
                        filled(ins, (names[0], i, h))
                for h in range(2):
                    b = empty((names[1], h))
                    for k in range(4):
                        ins = nc.tensor.transpose(b[0:SMP, k * P:(k + 1) * P], src[:, 4 * h + k, PRM:TOK], ident)
                    filled(ins, (names[1], h))

            token_major(V, ("vt", "vs"))
            b = empty(("ks", 0))
            for k in range(AH):
                ins = nc.tensor.transpose(b[0:SMP, k * P:(k + 1) * P], K[:, k, PRM:TOK], ident)
            filled(ins, ("ks", 0))
            for li, l in enumerate([0] + LEVELS):
                left, right = (M1, M1) if l else (K, Q)
                if l:
                    pe.wait_ge(m_ready, li)
                for i in range(3 if l <= 8 else 2):
                    r = META if i == 2 else P
                    b = empty(("lv", l, i))
                    for h in range(AH):
                        ins = mm(b[0:r, h * r:(h + 1) * r], left[:, h, i * P:i * P + r], right[:, h, i * P:i * P + r],
                                 start=True, stop=True)
                    filled(ins, ("lv", l, i))
            pe.wait_ge(m_ready, len(LEVELS) + 1)
            b = empty(("lv", 128, 0))
            for h in range(AH):
                ins = mm(b[:, h * P:(h + 1) * P], M1[:, h, 0:P], M1[:, h, P:256], start=True, stop=True)
            filled(ins, ("lv", 128, 0))
            pe.wait_ge(m_ready, len(LEVELS) + 2)
            b = empty(("lv", 256, 0))
            for i in range(2):
                for h in range(AH):
                    ins = mm(b[:, i * 64 + h * META:i * 64 + (h + 1) * META], M1[:, h, i * P:(i + 1) * P], M1[:, h, 256:PRM],
                             start=True, stop=True)
            filled(ins, ("lv", 256, 0))
            pe.wait_ge(m_ready, len(LEVELS) + 3)
            for i in range(3):
                rows = P if i < 2 else META
                b = empty(("ke", i))
                for h in range(AH):
                    ins = nc.tensor.transpose(b[0:rows, h * P:(h + 1) * P], M1[:, h, i * P:i * P + rows], ident)
                filled(ins, ("ke", i))
            pe.wait_ge(misc_free[PLAN[("ke", 2)][0]], PLAN[("ke", 2)][1] + 1)
            for g in range(2):
                b = empty(("sp", g))
                for h in (2 * g, 2 * g + 1):
                    for i in range(3):
                        r = P if i < 2 else META
                        ins = mm(b[:, (h % 2) * DV:(h % 2 + 1) * DV], KE[0:r, i, h * P:(h + 1) * P],
                                 Vtok[0:r, i, h * DV:(h + 1) * DV], start=i == 0, stop=i == 2)
                filled(ins, ("sp", g))
            taken(pe, ("lv", 256, 0))
            for o in range(KB):
                h = o // 2
                v = slice(o * P, (o + 1) * P)
                b = empty(("o", o))
                mm(b[:, 0:PRM], Vtok[:, 0, v], ST0[:, h, :], start=True, stop=False)
                mm(b[:, P:PRM], Vtok[:, 1, v], ST1[:, h, :], start=False, stop=False)
                filled(mm(b[:, 2 * P:PRM], Vtok[0:META, 2, v], ST2[:, h, :], start=False, stop=True), ("o", o))
            for n in range(SMP):
                pe.wait_ge(km_ready, n + 1)
                for g in range(2):
                    b = empty(("kv", n, g))
                    for h in (2 * g, 2 * g + 1):
                        ins = mm(b[:, (h % 2) * DV:(h % 2 + 1) * DV], KM[:, n % 2, h * P:(h + 1) * P],
                                 Vs[:, h * DV:(h + 1) * DV], start=True, stop=True)
                    filled(ins, ("kv", n, g))
                taken(pe, ("kv", n, 1))
                for o in range(KB):
                    h = o // 2
                    ins = mm(held[:, o * SMP + n:o * SMP + n + 1], S0[:, n % 2, h, (o % 2) * P:(o % 2 + 1) * P],
                             Q[:, h, PRM + n:PRM + n + 1], start=True, stop=True)
                ins.then_inc(s_used, 1)
            pe.wait_ge(osq_ready, 1)
            for h in range(AH):
                b = empty(("hn", h))
                mm(b[:, 0:TOK], part("mean_dv"), OSQ[:, 2 * h, :], start=True, stop=False)
                filled(mm(b[:, 0:TOK], part("mean_dv"), OSQ[:, 2 * h + 1, :], start=False, stop=True), ("hn", h))
            pe.wait_ge(ol_ready, 1)
            project("gla_out", HH, HL, 2)
            stat(2)
            pe.wait_ge(xl_ready, KB * 3)
            project("ffn1_up", XH, XL)
            down(1, 3)
            stat(3)

            pe.wait_ge(xl_ready, KB * 4)
            b = empty(("f", 0))
            for k in range(KB):
                ins = mm(b[0:BH, 0:TOK], wf[:, k, :], XG[:, k, :], start=k == 0, stop=k == KB - 1)
            filled(ins, ("f", 0))
            project("kv_in", XH, XL)
            pe.wait_ge(bank_free, SLOTS + UNIT0["kv_in"] + 16)
            token_major(Vf, ("fvt", "fvs"))
            pe.wait_ge(xl_ready, KB * 5)
            project("ffn2_up", XH, XL)
            down(2, 4)
            stat(4)

            pe.wait_ge(xl_ready, KB * 6)
            project("fox_q", XH, XL)
            pe.wait_ge(qb_ready, 3)

            def scores(h):
                r = slice(HD * (h % 2), HD * (h % 2 + 1))
                pick = ident[0:BH, h:h + 1]
                for i in range(3):
                    rows = P if i < 2 else META
                    keys = min((i + 1) * P, PRM)
                    b = empty(("s", h, i // 2)) if i != 1 else b
                    out = b[0:rows, (P if i == 1 else 0):(P if i == 1 else 0) + keys]
                    mm(out, Qf[r, h // 2, i * P:i * P + rows], Kf[r, h // 2, 0:keys], start=True, stop=False)
                    mm(out, pick.to_broadcast([BH, rows]), C8[:, 0:keys], start=False, stop=False)
                    diag = b[0:rows, (P if i == 1 else 0) + i * P:(P if i == 1 else 0) + keys]
                    ins = mm(diag, ident[0:rows, 0:rows], part("tri")[0:rows, 0:rows], start=False, stop=True)
                    if i:
                        filled(ins, ("s", h, i // 2))

            scores(0)
            for h in range(BH):
                q = h % 2
                if h + 1 < BH:
                    scores(h + 1)
                pe.wait_ge(pn_ready, h + 1)
                b = empty(("pt", h))
                nc.tensor.transpose(b[:, 0:P], PP[:, q, 0:P], ident)
                nc.tensor.transpose(b[:, P:2 * P], PP[:, q, P:2 * P], ident)
                nc.tensor.transpose(b[:, 2 * P:PRM], PP[0:META, q, 3 * P:4 * P], ident[0:META, 0:META])
                nc.tensor.transpose(b[:, PRM:PRM + P], PP[:, q, 2 * P:3 * P], ident)
                nc.tensor.transpose(b[:, PRM + P:PRM + 144], PP[0:META, q, 4 * P:5 * P], ident[0:META, 0:META])
                filled(nc.tensor.transpose(b[0:META, PRM + 144:PRM + 144 + META], PP[0:META, q, 5 * P:5 * P + META],
                                           ident[0:META, 0:META]), ("pt", h))
                taken(pe, ("pt", h))
                if q == 0 and h:
                    pe.wait_ge(po_read, h // 2)
                out = held[HD * q:HD * (q + 1), :]
                v = slice(h * HD, (h + 1) * HD)
                mm(out[:, 0:PRM], Vtok[:, 0, v], PTs[:, q, 0:PRM], start=True, stop=False)
                mm(out[:, P:PRM], Vtok[:, 1, v], PTs[:, q, PRM:PRM + 144], start=False, stop=False)
                ins = mm(out[:, 2 * P:PRM], Vtok[0:META, 2, v], PTs[0:META, q, PRM + 144:PRM + 144 + META],
                         start=False, stop=True)
                ins.then_inc(fo_done, 1)
            pe.wait_ge(po_read, BH // 2)
            for i in range(SMP * NPG):
                n, g = i // NPG, i % NPG
                pe.wait_ge(kp_in[i % 2], 16 * (i // 2 + 1))
                for half in range(2):
                    b = empty(("kt", n, g, half))
                    for k in range(4):
                        j = 4 * half + k
                        ins = nc.tensor.transpose(b[:, k * P:(k + 1) * P], KP[i % 2][:, j * P:(j + 1) * P], ident)
                    filled(ins, ("kt", n, g, half))
                taken(pe, ("kt", n, g, 0))
                taken(pe, ("kt", n, g, 1))
                for j in range(KB):
                    at = g * P + n * BH + 2 * j
                    ins = mm(held[:, at:at + 2], KT[:, i % 2, j, :], QB[:, j, n, :], start=True, stop=True)
                ins.then_inc(qk_done, 1)
            own_s = held[0:SMP, 2 * P:3 * P].rearrange("p (n j e) -> p n j e", n=SMP, e=2)
            for j in range(KB):
                ins = mm(own_s[:, :, j, :], Kf[:, j, PRM:TOK], QB[:, j, :, :], start=True, stop=True)
            ins.then_inc(qk_done, 1)
            pe.wait_ge(lfp_in, 16 * SMP * NPG)
            b = empty(("lf", 0))
            for g in range(NPG):
                ins = nc.tensor.transpose(b[:, g * P:(g + 1) * P], LFp[:, g, :, :].rearrange("p n h -> p (n h)"), ident)
            filled(ins, ("lf", 0))
            b = empty(("lown", 0))
            filled(mm(b[:, 0:SMP], part("rep")[0:BH, :], LG[:, PRM:TOK], start=True, stop=True), ("lown", 0))
            pe.wait_ge(sc_ready, 1)
            b = empty(("sct", 0))
            for g in range(NPG):
                nc.tensor.transpose(b[:, g * P:(g + 1) * P], SC[:, g, :, :].rearrange("p n h -> p (n h)"), ident)
            filled(nc.tensor.transpose(b[:, 2 * P:2 * P + SMP], SO[:, :], ident[0:SMP, 0:SMP]), ("sct", 0))
            pe.wait_ge(pe_ready, 1)
            b = empty(("pdt", 0))
            for g in range(NPG):
                nc.tensor.transpose(b[:, g * P:(g + 1) * P], PD[:, g * P:(g + 1) * P], ident)
            filled(nc.tensor.transpose(b[0:SMP, 2 * P:3 * P], PM[:, :], ident), ("pdt", 0))
            taken(pe, ("pdt", 0))
            for n in range(SMP):
                for g in range(NPG):
                    i = n * NPG + g
                    pe.wait_ge(vp_in[i % 4], 16 * (i // 4 + 1))
                for j in range(KB):
                    out = held[:, (j * SMP + n) * 2:(j * SMP + n) * 2 + 2]
                    h = slice(n * BH + 2 * j, n * BH + 2 * j + 2)
                    for g in range(NPG):
                        mm(out, VP[(n * NPG + g) % 4][:, j * P:(j + 1) * P], PDT[:, g, h], start=g == 0, stop=False)
                    ins = mm(out, Vs[:, j * P:(j + 1) * P], PMT[:, h], start=False, stop=True)
                ins.then_inc(pv_done, 1)
            pe.wait_ge(ol_ready, 2)
            project("fox_out", HH, HL, 5)
            stat(5)
            pe.wait_ge(xl_ready, KB * 7)
            project("ffn3_up", XH, XL)
            down(3, 6)
            stat(6)


def constants():
    import numpy as np
    s, t = np.arange(P)[:, None], np.arange(P)[None, :]
    eye = (s == t).astype(np.float32)
    own = (np.arange(P)[:, None] // BH == np.arange(SMP)[None, :]).astype(np.float32)
    rep = np.zeros((P, P), np.float32)
    rep[:BH] = (np.arange(BH)[:, None] == np.arange(P)[None, :] % BH)
    tri = np.where(t > s, np.float32(-1e30), np.float32(0))
    masks = np.stack([(s // (2 * l) == t // (2 * l)) & (s % (2 * l) < l) & (t % (2 * l) >= l) for l in LEVELS], 1)
    return {"ident": eye, "mean_d": np.full((P, P), 1.0 / D, np.float32), "mean_dv": np.full((P, P), 1.0 / DV, np.float32),
            "tri": tri, "own": own, "rep": rep}, masks.astype(np.float32)


def kernel(**inputs):
    import numpy as np
    import concourse.bacc as bacc
    from concourse.bass_utils import run_bass_kernel_spmd

    a = {k: np.asarray(v) for k, v in inputs.items()}
    f32 = np.float32

    def chunks(w, tiles, n_cols):
        w = w[:, :n_cols].reshape(w.shape[0] // (P * tiles), tiles, P, n_cols // P, P)
        return w.transpose(3, 0, 2, 1, 4).reshape(-1, P, tiles * P)

    def columns(v):
        return v.reshape(-1, P).T

    up, down = [], []
    for l in range(2):
        for f in ("ffn1", "ffn2"):
            gate, upper = chunks(a[f + "_w_gate"][l], KB, FF), chunks(a[f + "_w_up"][l], KB, FF)
            up.append(np.stack([gate, upper], 1).reshape(2 * FB, P, UPW))
            down.append(chunks(a[f + "_w_down"][l], DNT, D))
    mix = [chunks(a["gla_w_in"][0], KB, 24 * P), chunks(a["gla_w_out"][0], KB, D), chunks(a["kv_w_in"], KB, 2 * D),
           chunks(a["fox_w_q"][0], KB, D), chunks(a["fox_w_out"][0], KB, D)]
    x = np.concatenate([a["meta_tokens"], a["x_prompt"][0], a["x_sample"][:, 0]], 0)

    const, masks = constants()
    gains = [a["norm_ffn1"][0], a["norm_mix"][0], a["norm_ffn2"][0], a["kv_norm"], a["norm_ffn1"][1], a["norm_mix"][1],
             a["norm_ffn2"][1], a["final_norm"]]
    const["gain"] = np.concatenate([columns(g) for g in gains], 1)
    const["ghead"] = columns(a["gla_g_head"][0])
    const["balpha"] = columns(a["gla_b_alpha"][0])
    const["bf"] = a["kv_b_f"][:, None]
    const["walpha2"] = a["gla_w_alpha2"][0]
    const["wa"] = a["gla_w_in"][0][:, 24 * P:].reshape(KB, P, RANK).transpose(1, 0, 2).reshape(P, -1)
    const["wf"] = a["kv_w_in"][:, 2 * D:].reshape(KB, P, BH).transpose(1, 0, 2).reshape(P, -1)
    small = np.zeros((P, NCOL), f32)
    for name, (lo, hi) in COL.items():
        small[:const[name].shape[0], lo:hi] = const[name]

    n_phys = a["cache_k"].shape[0]
    arrays = {
        "x_all": x.T.reshape(KB, P, TOK), "up_w": np.concatenate(up, 0), "down_w": np.concatenate(down, 0),
        "mix_w": np.concatenate(mix, 0), "small": small, "level_masks": masks, "state_in": a["state_gla"][0],
        "cache_k": a["cache_k"].reshape(n_phys, PAGE, D), "cache_v": a["cache_v"].reshape(n_phys, PAGE, D),
        "cache_f": a["cache_logf"], "table": a["page_table"].reshape(1, SMP * NPG),
    }
    arrays = {k: np.ascontiguousarray(v) for k, v in arrays.items()}
    outs = {"y_out": (KB, P, TOK), "k_out": (KB, P, TOK), "v_out": (KB, P, TOK), "lf_out": (BH, TOK),
            "state_prompt": (AH, P, DV), "state_sample": (SMP, AH, P, DV)}

    nc = bacc.Bacc("TRN2", target_bir_lowering=False, num_devices=1)
    args = [nc.dram_tensor(k, v.shape, mybir.dt.from_np(v.dtype), kind="ExternalInput").ap() for k, v in arrays.items()]
    args += [nc.dram_tensor(k, v, mybir.dt.float32, kind="ExternalOutput").ap() for k, v in outs.items()]
    build(nc, *args)
    r = run_bass_kernel_spmd(nc, [arrays], core_ids=[0]).results[0]

    def rows(name):
        return r[name].reshape(D, TOK).T

    y, k, v, lf = rows("y_out"), rows("k_out"), rows("v_out"), r["lf_out"].T
    return (y[None, META:PRM], y[PRM:, None], r["state_prompt"][None, None],
            k[:PRM].reshape(1, PRM, BH, HD), v[:PRM].reshape(1, PRM, BH, HD), lf[None, :PRM],
            r["state_sample"][None],
            k[PRM:].reshape(SMP, 1, BH, HD), v[PRM:].reshape(SMP, 1, BH, HD), lf[PRM:, None])
```

```python
import concourse.bass as bass
from concourse import mybir
from contextlib import ExitStack

P = 128
D = 1024
KB = D // P
META, SEQ, SMP = 16, 256, 8
PRM = META + SEQ
TOK = PRM + SMP
FF = 2816
FB = FF // P
UPW = KB * P
DNT = FB // 2
DNW = DNT * P
SLOTS = 4
AH, DV = 4, 256
BH, HD = 16, 64
RANK = 16
PAGE, NPG = 128, 2
GSLOTS = 4
PAGES = 4
VALUES = {SMP + 3: [0], SMP + 4: [1], SMP + 5: [2, 3], SMP + 6: [4, 5], SMP + 7: [6, 7]}
EPS = 1e-6
LEVELS = [1, 2, 4, 8, 16, 32, 64]

SEGS = []
for _name in ("ffn0", "gla", "ffn1", "kv", "ffn2", "fox", "ffn3"):
    if _name.startswith("ffn"):
        SEGS += [(_name + "_up", 2 * FB, KB), (_name + "_down", 2 * KB, DNT)]
    elif _name == "gla":
        SEGS += [("gla_qk", KB, KB), ("gla_vr", 2 * KB, KB), ("gla_out", KB, KB)]
    elif _name == "kv":
        SEGS += [("kv_in", 16, KB)]
    else:
        SEGS += [("fox_q", KB, KB), ("fox_out", KB, KB)]
CHUNK0, UNIT0, COUNT, TILES, NEXT = {}, {}, {}, {}, {}
_c = _u = 0
for _i, (_name, _n, _t) in enumerate(SEGS):
    CHUNK0[_name], UNIT0[_name], COUNT[_name], TILES[_name] = _c, _u, _n, _t
    NEXT[_name] = SEGS[_i + 1][0] if _i + 1 < len(SEGS) else None
    _c += _n
    _u += _n if not _name.endswith(("_down", "_out")) else 0
MIX0 = {"gla_qk": 0, "gla_vr": 8, "gla_out": 24, "kv_in": 32, "fox_q": 48, "fox_out": 56}
GAINS = ("ffn0", "gla", "ffn1", "kv", "ffn2", "fox", "ffn3", "final")
GAIN = {n: i for i, n in enumerate(GAINS)}
STAGE = {"ffn0": 0, "gla": 1, "ffn1": 2, "kv": 3, "ffn2": 3, "fox": 4, "ffn3": 5, "final": 6}

COL = {}
_at = 0
for _n, _w in (("ident", P), ("mean_d", P), ("mean_dv", P), ("tri", P), ("own", SMP), ("sel", SMP), ("hsel", BH), ("quad", 4), ("rep", P), ("pick", BH),
               ("gain", 8 * KB), ("ghead", 2), ("balpha", AH), ("bf", 1), ("walpha2", 4 * P),
               ("wa", KB * RANK), ("wf", KB * BH)):
    COL[_n] = (_at, _at + _w)
    _at += _w
NCOL = _at


def misc_plan():
    first = [("stat", 0), ("stat", 1), ("a", 0)] + [("z", h) for h in range(AH)]
    gla = [("vt", i, h) for i in range(3) for h in range(2)] + [("vs", 0), ("vs", 1), ("ks", 0)]
    for l in [0] + LEVELS:
        gla += [("lv", l, i) for i in range(3 if l <= 8 else 2)]
    gla += [("lv", 128, 0), ("lv", 256, 0)]
    gla += [("ke", i) for i in range(3)] + [("sp", 0), ("sp", 1)]
    gla += [("o", b) for b in range(KB)]
    gla += [("kv", 0, 0), ("kv", 0, 1)]
    for n in range(SMP):
        if n + 1 < SMP:
            gla += [("kv", n + 1, 0), ("kv", n + 1, 1)]
        if 1 <= n <= AH:
            gla += [("hn", n - 1)]
    gla += [("hns", 0)]
    middle = [("stat", 2), ("stat", 3), ("f", 0)]
    middle += [("fvt", i, h) for i in range(3) for h in range(2)] + [("fvs", 0), ("fvs", 1)]
    middle += [("stat", 4)]
    fox = [("qt", 0), ("qt", 1), ("s", 0, 0), ("s", 0, 1)]
    for h in range(BH):
        if h + 1 < BH:
            fox += [("s", h + 1, 0), ("s", h + 1, 1)]
        if h < SMP:
            fox += [("qb", h, 0), ("qb", h, 1)]
        elif h == SMP:
            fox += [("lf", 0), ("lown", 0)]
        elif h == SMP + 1:
            fox += [("sct", 0)]
        elif h == SMP + 2:
            fox += [("pdt", 0)]
        fox += [("pt", h)]
    fox += [("u", n, k) for n in range(SMP) for k in range(2)]
    last = [("stat", 5), ("stat", 6)]
    count, plan = [0] * 7, {}
    for part, ring in ((first, 3), (gla, 7), (middle, 3)):
        for i, k in enumerate(part):
            plan[k] = (i % ring, count[i % ring])
            count[i % ring] += 1
    side = 0
    for k in fox + last:
        if k[0] == "s":
            b = k[2]
        elif k[0] == "pt":
            b = 2
        elif k[0] == "stat":
            b = 0
        else:
            b, side = 3 + side % 2, side + 1
        plan[k] = (b, count[b])
        count[b] += 1
    return plan


def build(nc, x_all, up_w, down_w, mix_w, small, level_masks, state_in, cache_k, cache_v, cache_f, table,
          y_out, k_out, v_out, lf_out, state_prompt, state_sample):
    f32, f32r = mybir.dt.float32, mybir.dt.float32r
    i32, bf16 = mybir.dt.int32, mybir.dt.bfloat16
    ALU, ACT = mybir.AluOpType, mybir.ActivationFunctionType
    AX = mybir.AxisListType
    PLAN = misc_plan()
    n_phys = cache_k.shape[0]

    ctx = ExitStack()
    with ctx:
        def sb(name, shape, dt=f32, where=ctx):
            return where.enter_context(nc.sbuf_tensor(name, shape, dt))

        def sem(name):
            return ctx.enter_context(nc.semaphore(name))

        raw = [sb(f"raw{s}", [P, DNW]) for s in range(SLOTS)]
        w_hi = [sb(f"w_hi{s}", [P, DNW], f32r) for s in range(SLOTS)]
        w_lo = [sb(f"w_lo{s}", [P, DNW], f32r) for s in range(SLOTS)]
        X = sb("X", [P, KB, TOK])
        XG = sb("XG", [P, KB, TOK])
        XH = sb("XH", [P, KB, TOK], f32r)
        XL = sb("XL", [P, KB, TOK], f32r)
        RS = sb("RS", [P, TOK])
        rs_tmp = sb("rs_tmp", [P, TOK])
        SQ = sb("SQ", [P, 1, TOK])
        SS = sb("SS", [P, TOK])
        const = sb("const", [P, NCOL])
        tab = sb("tab", [1, SMP * NPG], i32)
        Vs = sb("Vs", [SMP, D])
        ones = sb("ones", [P, PRM])
        LG = sb("LG", [BH, TOK])
        CC = sb("CC", [BH, PRM])

        def part(name):
            return const[:, COL[name][0]:COL[name][1]]
        ident = part("ident")
        gain = part("gain")
        wa = part("wa").rearrange("p (k r) -> p k r", k=KB)
        wf = part("wf").rearrange("p (k r) -> p k r", k=KB)

        inner = ctx.enter_context(ExitStack())
        KVf = sb("KVf", [P, 2 * KB, TOK], f32, inner)
        Vtok = sb("Vtok", [P, 3, D], f32, inner)
        Kf, Vf = KVf[:, 0:KB, :], KVf[:, KB:2 * KB, :]

        with ExitStack() as s:
            HH = sb("HH", [P, FB, TOK], f32r, s)
            HL = sb("HL", [P, FB, TOK], f32r, s)
            g_s = sb("g_s", [P, 2, TOK], f32, s)
            sil = sb("sil", [P, 2, TOK], f32, s)
            u_s = sb("u_s", [P, 2, TOK], f32, s)
            h_s = sb("h_s", [P, 2, TOK], f32, s)
        with ExitStack() as s:
            QKVR = sb("QKVR", [P, 24, TOK], f32, s)
            BB = sb("BB", [P, AH, TOK], f32, s)
            EE = sb("EE", [P, AH, TOK], f32, s)
            M1 = sb("M1", [P, AH, TOK], f32, s)
            ST = sb("ST", [P, AH * (PRM + 144)], f32, s)
            ST2 = sb("ST2", [META, AH, META], f32, s)
            ela = sb("ela", [P, AH, SMP], f32, s)
            a_s = sb("a_s", [RANK, TOK], f32, s)
        ST0 = ST[:, 0:AH * PRM].rearrange("p (h t) -> p h t", h=AH)
        ST1 = ST[:, AH * PRM:].rearrange("p (h t) -> p h t", h=AH)
        Q, K, V, R = (QKVR[:, 0:4, :], QKVR[:, 4:8, :], QKVR[:, 8:16, :], QKVR[:, 16:24, :])
        KE = V.rearrange("p a t -> p (a t)")[:, 0:3 * AH * P].rearrange("p (i n) -> p i n", i=3)
        SPS = M1[:, :, 0:DV]
        spare = KVf[:, :, :].rearrange("p k t -> p (k t)")
        S0 = spare[:, 0:GSLOTS * AH * DV].rearrange("p (i h v) -> p i h v", i=GSLOTS, h=AH)
        masks = spare[:, 3584:3584 + len(LEVELS) * P].rearrange("p (l t) -> p l t", l=len(LEVELS))
        EEs, M1s = (EE, XG[:, 4:8, :]), (M1, XG[:, 0:4, :])
        O = XG
        flat = lambda t: t[:, :, :].rearrange("p k t -> p (k t)")
        V3, K3 = flat(XH)[0:96, 0:AH * DV], flat(XH)[0:96, AH * DV:AH * DV + AH * P]
        KM = flat(XL)[0:96, 0:2 * AH * P].rearrange("p (i n) -> p i n", i=2)
        OSQ = QKVR[:, 0:KB, :]
        RH = BB
        with ExitStack() as s:
            Qf = sb("Qf", [P, KB, TOK], f32, s)
            PP = sb("PP", [P, 2, P + 2 * P + PRM], f32, s)
            PTH = sb("PTH", [P, 2, PRM + 144 + META], f32r, s)
            PTL = sb("PTL", [P, 2, PRM + 144 + META], f32r, s)
            VH = sb("VH", [P, 3, D], f32r, s)
            NM = sb("NM", [P, 2, 3], f32, s)
            MX = sb("MX", [P, 2, 3], f32, s)
            RW = sb("RW", [P, 2, 3], f32, s)
            QB = sb("QB", [P, KB, SMP, 2], f32, s)
            PG = [sb(f"PG{i}", [P, D], f32, s) for i in range(PAGES)]
            LFp = sb("LFp", [P, NPG, SMP, BH], f32, s)
            SC = sb("SC", [P, NPG, SMP, BH], f32, s)
            SO = sb("SO", [SMP, P], f32, s)
            LD = sb("LD", [P, 2 * P + 1], f32, s)
            SD = sb("SD", [P, 2 * P + 1], f32, s)
            PD = sb("PD", [P, 2 * P + 1], f32, s)
            own_t = sb("own_t", [P, 2, SMP], f32, s)
            PM = sb("PM", [P, SMP], f32, s)
            col = sb("col", [P, 4], f32, s)
            PMT = sb("PMT", [SMP, P], f32, s)
            CB = sb("CB", [3 * 32, PRM], bf16, s)
            pick = sb("pick", [3 * 32, BH], bf16, s)
            ident_b = sb("ident_b", [P, P], bf16, s)
            tri_b = sb("tri_b", [P, P], bf16, s)
        with inner:
            pass
        with ExitStack() as s:
            KVr = sb("KVr", [P, 2 * KB, TOK], f32r, s)
            VL = sb("VL", [P, 3, D], f32r, s)
        KL, KH = KVr[:, 0:KB, 0:PRM], KVr[:, KB:2 * KB, 0:PRM]
        QH, QL = XH, XL
        Q3, sel_r = w_hi[2][0:64, 0:D], w_lo[3][0:64, D + 2 * P:D + 2 * P + SMP]
        VpH, VpL = (w_hi[2], w_hi[3]), (w_lo[2], w_lo[3])
        PDT = [t[:, D:D + 2 * P].rearrange("p (n x h) -> p n x h", n=SMP, x=2) for t in (w_hi[3], w_lo[3])]
        UM = Qf[:, :, :].rearrange("p k t -> p (k t)")[:, 0:2 * D].rearrange("p (g c) -> p g c", g=2)
        CD = PD
        lt = Qf[0:BH, 0:3, :]
        C8, part_f = PP[0:BH, 0, 0:PRM], PP[0:BH, 1, 0:PRM]

        bank = [ctx.enter_context(nc.psum_tensor(f"bank{i}", [P, 512], f32)) for i in range(4)]
        misc = [ctx.enter_context(nc.psum_tensor(f"misc{i}", [P, 512], f32)) for i in range(3)] + bank
        held = ctx.enter_context(nc.psum_tensor("held", [P, 512], f32))

        raw_in = [sem(f"raw_in{s}") for s in range(SLOTS)]
        xsq_ready = sem("xsq_ready")
        x_in, const_in = sem("x_in"), sem("const_in")
        hi_ready, lo_ready = sem("hi_ready"), sem("lo_ready")
        chunk_used = sem("chunk_used")
        bank_free = sem("bank_free")
        x_new = sem("x_new")
        ss_ready, rs_ready, rs_sq = sem("ss_ready"), sem("rs_ready"), sem("rs_sq")
        xg_ready, xh_ready, xl_ready = sem("xg_ready"), sem("xh_ready"), sem("xl_ready")
        g_ready, sil_ready, h_ready = sem("g_ready"), sem("sil_ready"), sem("h_ready")
        hh_ready, hid_ready = sem("hh_ready"), sem("hid_ready")
        misc_full = [sem(f"misc_full{i}") for i in range(7)]
        misc_free = [sem(f"misc_free{i}") for i in range(7)]
        held_full = sem("held_full")
        pool_step, dve_step, act_step = sem("pool_step"), sem("dve_step"), sem("act_step")
        a_ready, z_ready, l_ready = sem("a_ready"), sem("z_ready"), sem("l_ready")
        b_ready, d_ready, e_ready, m_ready, m_used = (sem(n) for n in (
            "b_ready", "d_ready", "e_ready", "m_ready", "m_used"))
        tok_ready, st_ready = sem("tok_ready"), sem("st_ready")
        ke_ready, sp_ready, sp_out = sem("ke_ready"), sem("sp_ready"), sem("sp_out")
        s_in = [sem(f"s_in{i}") for i in range(GSLOTS)]
        s_out = [sem(f"s_out{i}") for i in range(GSLOTS)]
        zero3, hi3, all3 = sem("zero3"), sem("hi3"), sem("all3")
        km_ready, s_ready, s_used = sem("km_ready"), sem("s_ready"), sem("s_used")
        o_ready, osq_ready, sr_ready = sem("o_ready"), sem("osq_ready"), sem("sr_ready")
        of_ready, oh_ready, ol_ready = sem("of_ready"), sem("oh_ready"), sem("ol_ready")
        rh_in, rh_out = sem("rh_in"), sem("rh_out")
        kvout, lf_in, lf_ready, lf_done = sem("kvout"), sem("lf_in"), sem("lf_ready"), sem("lf_done")
        ones_ready, ela_ready, qb_zero, fo_done = sem("ones_ready"), sem("ela_ready"), sem("qb_zero"), sem("fo_done")
        qb_ready, nm_ready, p_ready, pn_ready = sem("qb_ready"), sem("nm_ready"), sem("p_ready"), sem("pn_ready")
        pt_ready, fo_ready = sem("pt_ready"), sem("fo_ready")
        page_in = [sem(f"page_in{i}") for i in range(PAGES)]
        own_done, k_used = sem("own_done"), sem("k_used")
        kh_ready, kl_ready, qh_ready, ql_ready, vh_ready, vl_ready = (sem(n) for n in (
            "kh_ready", "kl_ready", "qh_ready", "ql_ready", "vh_ready", "vl_ready"))
        q3_zero, q3h_ready, q3_ready, sel_ready = (sem(n) for n in ("q3_zero", "q3h_ready", "q3_ready", "sel_ready"))
        pth_ready, ptl_ready, pdh_ready = sem("pth_ready"), sem("ptl_ready"), sem("pdh_ready")
        vph_ready, vpl_ready, um_ready, uo_done = (sem(n) for n in ("vph_ready", "vpl_ready", "um_ready", "uo_done"))
        lfp_in, sc_ready, sd_ready, pd_ready, pe_ready, pv_done = (sem(n) for n in (
            "lfp_in", "sc_ready", "sd_ready", "pd_ready", "pe_ready", "pv_done"))
        po_read, masks_in = sem("po_read"), sem("masks_in")
        tab_in, y_ready, y_done = sem("tab_in"), sem("y_ready"), sem("y_done")

        block = ctx.enter_context(nc.Block())

        def full(eng, key):
            b, n = PLAN[key]
            eng.wait_ge(misc_full[b], n + 1)
            return misc[b]

        def freed(ins, key):
            ins.then_inc(misc_free[PLAN[key][0]], 1)

        def taken(eng, key):
            b, n = PLAN[key]
            eng.wait_ge(misc_free[b], n + 1)

        def page_used(eng, i):
            if i % NPG:
                full(eng, ("u", i // NPG, 1))
            else:
                eng.wait_ge(pv_done, i // NPG + 1)

        def in_pairs(eng, seg, split, use, norm=None):
            n = COUNT[seg] // 2
            half = (n - 2) // 2
            split(seg, 0, 1)
            if norm:
                norm()
            with eng.Fori(0, half) as i:
                use(i * 2, i, 0)
                split(seg, i + 1, 0)
                use(i * 2 + 1, i, 1)
                split(seg, i + 1, 1)
            use(n - 2, half, 0)
            if NEXT[seg]:
                split(NEXT[seg], 0, 0)
            use(n - 1, half, 1)

        @block.sync
        def _(sp):
            def load_pages():
                n = SMP * NPG
                sp.wait_ge(tab_in, 16)
                sp.wait_ge(x_new, 2 + KB * 4)
                for i in range(2 * n):
                    if i >= PAGES:
                        j = i - PAGES
                        if j < n:
                            sp.wait_ge(k_used, j + 1)
                        else:
                            sp.wait_ge(vpl_ready, j - n + 1)
                    page = sp.value_load(tab[0:1, i % n:i % n + 1], min_val=0, max_val=n_phys - 1)
                    if i < n:
                        sp.dma_start(LFp[:, i % NPG, i // NPG, :], cache_f[page]).then_inc(lfp_in, 16)
                    sp.dma_start(PG[i % PAGES][:, :], (cache_k if i < n else cache_v)[page]).then_inc(page_in[i % PAGES], 16)

            sp.dma_start(X[:, :, :], x_all.rearrange("k p t -> p k t")).then_inc(x_in, 16)
            sp.dma_start(raw[0][:, 0:UPW], up_w[0]).then_inc(raw_in[0], 16)
            sp.dma_start(const[:, :], small).then_inc(const_in, 16)
            for s in range(1, SLOTS):
                sp.dma_start(raw[s][:, 0:UPW], up_w[s]).then_inc(raw_in[s], 16)
            for seg, n, tiles in SEGS:
                if tiles == DNT:
                    src, first = down_w, int(seg[3]) * 2 * KB
                elif seg.endswith("_up"):
                    src, first = up_w, int(seg[3]) * 2 * FB
                else:
                    src, first = mix_w, MIX0[seg]
                skip = SLOTS if CHUNK0[seg] == 0 else 0
                if seg == "fox_out":
                    skip = SLOTS
                    for s in range(SLOTS):
                        sp.wait_ge(lo_ready, CHUNK0[seg] + s + 1 - SLOTS)
                        sp.dma_start(raw[s][:, 0:UPW], src[first + s]).then_inc(raw_in[s], 16)
                    load_pages()
                with sp.Fori(0, (n - skip) // SLOTS) as i:
                    for s in range(SLOTS):
                        sp.wait_ge(lo_ready, i * SLOTS + (CHUNK0[seg] + skip + s + 1 - SLOTS))
                        sp.dma_start(raw[s][:, 0:tiles * P],
                                     src[i * SLOTS + (first + skip + s)]).then_inc(raw_in[s], 16)
            sp.wait_ge(y_ready, KB)
            sp.dma_start(y_out.rearrange("k p t -> p k t"), XG[:, :, :]).then_inc(y_done, 16)
            sp.wait_ge(y_done, 16)

        @block.gpsimd
        def _(pool):
            steps = [0]

            def step(ins):
                steps[0] += 1
                ins.then_inc(pool_step, 1)
                pool.wait_ge(pool_step, steps[0])

            pool.dma_start(masks, level_masks).then_inc(masks_in, 16)
            pool.dma_start(tab[:, :], table).then_inc(tab_in, 16)
            nc.gpsimd.memset(ones[:, :], 1.0).then_inc(ones_ready, 1)

            def square_sum(stage):
                for m in range(KB):
                    pool.wait_ge(x_new, KB * (stage - 1) + m + 3)
                    if m == 0:
                        step(nc.gpsimd.tensor_tensor(SS[:, :], X[:, 0, :], X[:, 0, :], ALU.mult))
                        continue
                    step(nc.gpsimd.tensor_tensor(SQ[:, 0, :], X[:, m, :], X[:, m, :], ALU.mult))
                    steps[0] += 1
                    nc.gpsimd.tensor_tensor(SS[:, :], SS[:, :], SQ[:, 0, :], ALU.add).then_inc(pool_step, 1)
                    pool.wait_ge(pool_step, steps[0])
                pool.sem_inc(ss_ready, 1)

            square_sum(1)

            def load_state(n):
                i = n % GSLOTS
                if n == GSLOTS - 1:
                    taken(pool, ("lv", LEVELS[-1], 1))
                if n >= GSLOTS:
                    pool.wait_ge(s_used, n - GSLOTS + 1)
                    pool.wait_ge(s_out[i], 16 * (n // GSLOTS))
                pool.dma_start(S0[:, i, :, :], state_in[n].rearrange("h d v -> d h v")).then_inc(s_in[i], 16)

            def store_state(n):
                taken(pool, ("kv", n, 1))
                pool.dma_start(state_sample[n].rearrange("h d v -> d h v"),
                               S0[:, n % GSLOTS, :, :]).then_inc(s_out[n % GSLOTS], 16)

            for n in range(GSLOTS - 1):
                load_state(n)
            pool.wait_ge(bank_free, SLOTS + UNIT0["gla_vr"] + 16)
            nc.gpsimd.memset(flat(XH)[0:96, 0:AH * (DV + P)].bitcast(f32), 0.0).then_inc(zero3, 1)
            load_state(GSLOTS - 1)
            for n in range(SMP):
                store_state(n)
                if 1 <= n and n - 1 + GSLOTS < SMP:
                    load_state(n - 1 + GSLOTS)
            taken(pool, ("sp", 1))
            pool.dma_start(state_prompt.rearrange("h d v -> d h v"), SPS).then_inc(sp_out, 16)
            square_sum(2)
            square_sum(3)

            pool.wait_ge(bank_free, SLOTS + UNIT0["kv_in"] + 16)
            pool.dma_start(k_out.rearrange("k p t -> p k t"), Kf[:, :, :]).then_inc(kvout, 16)
            pool.dma_start(v_out.rearrange("k p t -> p k t"), Vf[:, :, :]).then_inc(kvout, 16)
            pool.wait_ge(lf_ready, 1)
            pool.dma_start(lf_out, LG[:, :]).then_inc(lf_done, 16)
            square_sum(4)

            step(nc.gpsimd.memset(QB[:, :, :, :], 0.0))
            step(nc.gpsimd.memset(NM[:, :, :], 0.0))
            step(nc.gpsimd.memset(MX[:, :, :], 0.0))
            step(nc.gpsimd.memset(RW[:, :, :], 1.0))
            pool.sem_inc(qb_zero, 1)
            pool.wait_ge(bank_free, SLOTS + UNIT0["fox_q"] + KB)
            nc.gpsimd.memset(Q3.bitcast(f32), 0.0).then_inc(q3_zero, 1)
            square_sum(5)
            square_sum(6)
            for i in range(GSLOTS):
                pool.wait_ge(s_out[i], 16 * SMP // GSLOTS)
            pool.wait_ge(sp_out, 16)
            pool.wait_ge(kvout, 32)
            pool.wait_ge(lf_done, 16)

        @block.scalar
        def _(act):
            steps = [0]

            def step(ins):
                steps[0] += 1
                ins.then_inc(act_step, 1)
                act.wait_ge(act_step, steps[0])

            def split(seg, half, par):
                w = TILES[seg] * P
                for k in range(2):
                    s = 2 * par + k
                    c = half * 4 + (CHUNK0[seg] + s)
                    act.wait_ge(raw_in[s], half * 16 + 16 * (CHUNK0[seg] // 4 + 1))
                    act.wait_ge(chunk_used, c + 1)
                    nc.scalar.copy(w_hi[s][:, 0:w], raw[s][:, 0:w]).then_inc(hi_ready, 1)

            def norm_root(n):
                act.wait_ge(rs_sq, n + 1)
                nc.scalar.activation(RS[:, :], rs_tmp[:, :], ACT.Sqrt).then_inc(rs_ready, 1)

            def prep(name, m):
                n = m + KB * GAIN[name]
                act.wait_ge(xg_ready, n + 1)
                nc.scalar.copy(XH[:, bass.ds(m, 1), :].rearrange("p a t -> p (a t)"),
                                     XG[:, bass.ds(m, 1), :].rearrange("p a t -> p (a t)")).then_inc(xh_ready, 1)

            def ffn(n, norm):
                f0 = n * FB

                def hidden(f, half, par):
                    act.wait_ge(g_ready, f + (f0 + 1))
                    nc.scalar.activation(sil[:, par, :], g_s[:, par, :], ACT.Silu).then_inc(sil_ready, 1)
                    act.wait_ge(h_ready, f + (f0 + 1))
                    nc.scalar.copy(HH[:, bass.ds(f, 1), :].rearrange("p a t -> p (a t)"),
                                         h_s[:, par, :]).then_inc(hh_ready, 1)

                in_pairs(act, f"ffn{n}_up", split, hidden, norm)
                after = GAINS[GAIN[f"ffn{n}"] + 1]
                in_pairs(act, f"ffn{n}_down", split,
                         lambda m, half, par: prep(after, m) if after != "final" else None)

            act.wait_ge(x_in, 16)
            nc.scalar.activation(OSQ, X[:, :, :], ACT.Square).then_inc(xsq_ready, 1)
            split("ffn0_up", 0, 0)
            for m in range(KB):
                prep("ffn0", m)
            ffn(0, lambda: norm_root(0))

            in_pairs(act, "gla_qk", split, lambda g, half, par: None, lambda: norm_root(1))

            def gate():
                for h in range(AH):
                    taken(act, ("z", h))
                step(nc.scalar.activation(EE[:, :, :], M1[:, :, :], ACT.Abs))
                step(nc.scalar.activation(EE[:, :, :], EE[:, :, :], ACT.Exp, scale=-1.0))
                nc.scalar.activation(EE[:, :, :], EE[:, :, :], ACT.Ln, bias=1.0).then_inc(l_ready, 1)
                act.wait_ge(b_ready, 1)
                nc.scalar.activation(ela[:, :, :], M1[:, :, PRM:TOK], ACT.Exp, scale=1.0 / 16).then_inc(ela_ready, 1)

            in_pairs(act, "gla_vr", split, lambda g, half, par: None, gate)
            for i in range(3):
                rows = P if i < 2 else META
                for h in range(2):
                    b = full(act, ("vt", i, h))
                    freed(nc.scalar.copy(Vtok[0:rows, i, h * 512:(h + 1) * 512], b[0:rows, :]), ("vt", i, h))
            for h in range(2):
                b = full(act, ("vs", h))
                freed(nc.scalar.copy(Vs[:, h * 512:(h + 1) * 512], b[0:SMP, :]), ("vs", h))
            act.wait_ge(zero3, 1)
            taken(act, ("vs", 1))
            for at in (0, 64):
                nc.scalar.copy(V3[at:at + SMP, :], Vs[:, :])
            b = full(act, ("ks", 0))
            nc.scalar.copy(K3[0:SMP, :], b[0:SMP, :])
            nc.scalar.copy(K3[32:32 + SMP, :], b[0:SMP, :]).then_inc(hi3, 1)
            for l in range(len(LEVELS) + 3):
                act.wait_ge(d_ready, l + 1)
                e = EEs[l % 2][:, :, 0:PRM]
                nc.scalar.activation(e, e, ACT.Exp, scale=1.0 / 16).then_inc(e_ready, 1)
            for i in range(3):
                rows = P if i < 2 else META
                b = full(act, ("ke", i))
                freed(nc.scalar.copy(KE[0:rows, i, :], b[0:rows, :]), ("ke", i))
            for g in range(2):
                b = full(act, ("sp", g))
                freed(nc.scalar.copy(SPS[:, 2 * g:2 * g + 2, :], b[:, :].rearrange("p (h v) -> p h v", h=2)), ("sp", g))
            act.wait_ge(o_ready, 1)
            nc.scalar.activation(OSQ[:, :, 0:PRM], O[:, :, 0:PRM], ACT.Square).then_inc(osq_ready, 1)
            nc.scalar.activation(R, R, ACT.Silu).then_inc(sr_ready, 1)
            for h in range(AH):
                act.wait_ge(rh_in, h + 1)
                nc.scalar.activation(RH[:, h, 0:PRM], RH[:, h, 0:PRM], ACT.Sqrt).then_inc(rh_out, 1)
            act.wait_ge(o_ready, 2)
            nc.scalar.activation(OSQ[:, :, PRM:TOK], O[:, :, PRM:TOK], ACT.Square).then_inc(osq_ready, 1)
            act.wait_ge(rh_in, AH + 1)
            nc.scalar.activation(RH[:, :, PRM:TOK], RH[:, :, PRM:TOK], ACT.Sqrt).then_inc(rh_out, 1)
            act.wait_ge(of_ready, 1)
            for m in range(0, KB, 2):
                nc.scalar.copy(HH[:, m:m + 2, :], XG[:, m:m + 2, :]).then_inc(oh_ready, 1)
            in_pairs(act, "gla_out", split, lambda g, half, par: [prep("ffn1", 2 * g + k) for k in range(2)])
            ffn(1, lambda: norm_root(2))

            in_pairs(act, "kv_in", split, lambda g, half, par: None, lambda: norm_root(3))
            act.wait_ge(lf_in, 1)
            step(nc.scalar.activation(lt[:, 1, :], lt[:, 0, :], ACT.Abs))
            step(nc.scalar.activation(lt[:, 1, :], lt[:, 1, :], ACT.Exp, scale=-1.0))
            nc.scalar.activation(lt[:, 1, :], lt[:, 1, :], ACT.Ln, bias=1.0).then_inc(l_ready, 1)
            for i in range(3):
                rows = P if i < 2 else META
                for h in range(2):
                    b = full(act, ("fvt", i, h))
                    freed(nc.scalar.copy(Vtok[0:rows, i, h * 512:(h + 1) * 512], b[0:rows, :]), ("fvt", i, h))
            for h in range(2):
                b = full(act, ("fvs", h))
                freed(nc.scalar.copy(Vs[:, h * 512:(h + 1) * 512], b[0:SMP, :]), ("fvs", h))
            for m in range(KB):
                prep("ffn2", m)
            act.wait_ge(lf_ready, 1)
            ffn(2, None)

            def norm_and_keys():
                norm_root(4)
                act.wait_ge(kvout, 32)
                nc.scalar.copy(KH, Kf[:, :, 0:PRM]).then_inc(kh_ready, 1)

            in_pairs(act, "fox_q", split, lambda g, half, par: None, norm_and_keys)

            def attend(h):
                q = h % 2
                for i, (key, rows, src, dst) in enumerate((
                        (("s", h, 0), P, slice(0, P), PP[:, q, 0:P]),
                        (("s", h, 0), P, slice(P, 3 * P), PP[:, q, P:3 * P]),
                        (("s", h, 1), META, slice(0, PRM), PP[0:META, q, 3 * P:3 * P + PRM]))):
                    if i != 1:
                        full(act, key)
                    act.wait_ge(nm_ready, 2 * h + (1 if i < 2 else 2))
                    ins = nc.scalar.activation(dst, misc[PLAN[key][0]][0:rows, src], ACT.Exp,
                                               bias=NM[0:rows, q, i:i + 1], scale=HD ** -0.5,
                                               accum_out=RW[0:rows, q, i:i + 1])
                    if i:
                        freed(ins, key)

            def probs_high(h):
                b = full(act, ("pt", h))
                nc.scalar.copy(PTH[:, h % 2, 0:PRM + 144], b[:, 0:PRM + 144])
                nc.scalar.copy(PTH[0:META, h % 2, PRM + 144:], b[0:META, PRM + 144:PRM + 144 + META]).then_inc(pth_ready, 1)

            def page_high(i):
                j = SMP * NPG + i
                act.wait_ge(page_in[j % PAGES], 16 * (j // PAGES + 1))
                if i >= 2:
                    page_used(act, i - 2)
                nc.scalar.copy(VpH[i % 2][:, 0:D], PG[j % PAGES][:, :]).then_inc(vph_ready, 1)

            def head_out(h):
                act.wait_ge(fo_done, h + 1)
                r = slice(HD * (h % 2), HD * (h % 2 + 1))
                nc.scalar.copy(XG[r, h // 2, 0:PRM], bank[2 + h % 2][r, 0:PRM]).then_inc(po_read, 1)

            act.wait_ge(bank_free, SLOTS + UNIT0["fox_q"] + KB)
            for m in range(0, KB, 2):
                nc.scalar.copy(QH[:, m:m + 2, :], Qf[:, m:m + 2, :]).then_inc(qh_ready, 1)
            nc.scalar.copy(sel_r, part("sel")[0:64, :]).then_inc(sel_ready, 1)
            act.wait_ge(q3_zero, 1)
            for k in range(2):
                b = full(act, ("qt", k))
                nc.scalar.copy(Q3[0:SMP, k * 512:(k + 1) * 512], b[0:SMP, :]).then_inc(q3h_ready, 1)
            attend(0)
            nc.scalar.copy(VH[:, 0:2, :], Vtok[:, 0:2, :])
            nc.scalar.copy(VH[0:META, 2, :], Vtok[0:META, 2, :]).then_inc(vh_ready, 1)
            for h in range(BH):
                if h:
                    probs_high(h - 1)
                if h + 1 < BH:
                    attend(h + 1)
                if h >= 2:
                    head_out(h - 2)
                if h == SMP + 1:
                    act.wait_ge(sd_ready, 1)
                    nc.scalar.activation(PD[:, :], SD[:, :], ACT.Exp, bias=col[:, 0:1], accum_out=col[:, 1:2]).then_inc(pd_ready, 1)
                if h == SMP + 2:
                    b = full(act, ("pdt", 0))
                    for g in range(NPG):
                        nc.scalar.copy(PDT[g][:, :, 0, :], b[:, g * P:(g + 1) * P].rearrange(
                            "p (n h) -> p n h", n=SMP)).then_inc(pdh_ready, 1)
                for n in VALUES.get(h, []):
                    page_high(2 * n)
                    page_high(2 * n + 1)
            probs_high(BH - 1)
            head_out(BH - 2)
            head_out(BH - 1)
            act.wait_ge(po_read, BH)
            act.wait_ge(of_ready, 2)
            for m in range(0, KB, 2):
                nc.scalar.copy(HH[:, m:m + 2, :], XG[:, m:m + 2, :]).then_inc(oh_ready, 1)
            in_pairs(act, "fox_out", split, lambda g, half, par: [prep("ffn3", 2 * g + k) for k in range(2)])
            ffn(3, lambda: norm_root(5))
            norm_root(6)

        @block.vector
        def _(dve):
            steps = [0]

            def step(ins):
                steps[0] += 1
                ins.then_inc(dve_step, 1)
                dve.wait_ge(dve_step, steps[0])

            def split(seg, half, par):
                w = TILES[seg] * P
                for k in range(2):
                    s = 2 * par + k
                    c = half * 4 + (CHUNK0[seg] + s)
                    dve.wait_ge(hi_ready, c + 1)
                    nc.vector.tensor_tensor(w_lo[s][:, 0:w], raw[s][:, 0:w],
                                            w_hi[s][:, 0:w].bitcast(f32), ALU.subtract).then_inc(lo_ready, 1)

            def block_of(t, m):
                return t[:, bass.ds(m, 1), :].rearrange("p a t -> p (a t)")

            def norm_square(n):
                b = full(dve, ("stat", n))
                ins = nc.vector.tensor_scalar(rs_tmp[:, :], b[:, 0:TOK], EPS, None, ALU.add)
                freed(ins, ("stat", n))
                dve.wait_ge(misc_free[PLAN[("stat", n)][0]], PLAN[("stat", n)][1] + 1)
                nc.vector.reciprocal(rs_tmp[:, :], rs_tmp[:, :]).then_inc(rs_sq, 1)

            def prep(name, m):
                n = m + KB * GAIN[name]
                nc.vector.tensor_scalar(block_of(XG, m), block_of(X, m), gain[:, bass.ds(n, 1)], None,
                                        ALU.mult).then_inc(xg_ready, 1)
                dve.wait_ge(xh_ready, n + 1)
                nc.vector.tensor_tensor(block_of(XL, m), block_of(XG, m), block_of(XH, m).bitcast(f32),
                                        ALU.subtract).then_inc(xl_ready, 1)

            def highs(name):
                n = KB * GAIN[name]
                for m in range(KB):
                    nc.vector.tensor_scalar(XG[:, m, :], X[:, m, :], gain[:, n + m:n + m + 1], None,
                                            ALU.mult).then_inc(xg_ready, 1)

            def lows(name):
                n = KB * GAIN[name]
                for m in range(KB):
                    dve.wait_ge(xh_ready, n + m + 1)
                    nc.vector.tensor_tensor(XL[:, m, :], XG[:, m, :], XH[:, m, :].bitcast(f32),
                                            ALU.subtract).then_inc(xl_ready, 1)

            def residual(seg, stage, scale, after, m, b):
                per = 1 if TILES[seg] == KB else 2
                dve.wait_ge(chunk_used, m * per + (SLOTS + CHUNK0[seg] + per))
                ins = nc.vector.scalar_tensor_tensor(block_of(X, m), bank[b][:, 0:TOK], scale, block_of(X, m),
                                                     ALU.mult, ALU.add)
                ins.then_inc(x_new, 1)
                dve.wait_ge(x_new, m + (KB * (stage - 1) + 3))
                if after != "final":
                    prep(after, m)

            def scaled(seg, dst):
                def use(g, half, par):
                    for k in range(2):
                        dve.wait_ge(chunk_used, g * 2 + (SLOTS + CHUNK0[seg] + k + 1))
                        nc.vector.tensor_tensor(block_of(dst, g * 2 + k), bank[2 * par + k][:, 0:TOK], RS[:, :],
                                                ALU.mult).then_inc(bank_free, 1)
                return use

            def norm(n):
                norm_square(n)
                dve.wait_ge(rs_ready, n + 1)

            def ffn(n, after, stage, norm=None):
                f0, seg = n * FB, f"ffn{n}_up"

                def hidden(f, half, par):
                    u = f * 2 + UNIT0[seg]
                    c = f * 2 + (SLOTS + CHUNK0[seg])
                    dve.wait_ge(chunk_used, c + 1)
                    nc.vector.tensor_tensor(g_s[:, par, :], bank[2 * par][:, 0:TOK], RS[:, :], ALU.mult).then_inc(g_ready, 1)
                    dve.wait_ge(chunk_used, c + 2)
                    nc.vector.tensor_tensor(u_s[:, par, :], bank[2 * par + 1][:, 0:TOK], RS[:, :],
                                            ALU.mult).then_inc(bank_free, 2)
                    dve.wait_ge(bank_free, u + (SLOTS + 2))
                    dve.wait_ge(sil_ready, f + (f0 + 1))
                    nc.vector.tensor_tensor(h_s[:, par, :], sil[:, par, :], u_s[:, par, :], ALU.mult).then_inc(h_ready, 1)
                    dve.wait_ge(hh_ready, f + (f0 + 1))
                    nc.vector.tensor_tensor(block_of(HL, f), h_s[:, par, :], block_of(HH, f).bitcast(f32),
                                            ALU.subtract).then_inc(hid_ready, 1)

                in_pairs(dve, seg, split, hidden, norm)
                in_pairs(dve, f"ffn{n}_down", split,
                         lambda m, half, par: residual(f"ffn{n}_down", stage, 0.5, after, m, par))

            dve.sem_inc(bank_free, SLOTS)
            dve.sem_inc(x_new, 2)
            dve.wait_ge(x_in, 16)
            dve.wait_ge(const_in, 16)
            highs("ffn0")
            split("ffn0_up", 0, 0)
            lows("ffn0")
            dve.wait_ge(xsq_ready, 1)
            for m in (4, 2):
                step(nc.vector.tensor_tensor(OSQ[:, 0:m, :], OSQ[:, 0:m, :], OSQ[:, m:2 * m, :], ALU.add))
            nc.vector.tensor_tensor(SS[:, :], OSQ[:, 0, :], OSQ[:, 1, :], ALU.add).then_inc(ss_ready, 1)
            ffn(0, "gla", 1, lambda: norm(0))

            in_pairs(dve, "gla_qk", split, scaled("gla_qk", QKVR), lambda: norm(1))
            b = full(dve, ("a", 0))
            freed(nc.vector.tensor_tensor(a_s[:, :], b[0:RANK, 0:TOK], RS[0:RANK, :], ALU.mult), ("a", 0))

            def gate():
                for h in range(AH):
                    b = full(dve, ("z", h))
                    freed(nc.vector.tensor_scalar(M1[:, h, :], b[:, 0:TOK], part("balpha")[:, h:h + 1], None, ALU.add), ("z", h))
                dve.wait_ge(l_ready, 1)
                step(nc.vector.tensor_scalar(M1[:, :, :], M1[:, :, :], 0.0, None, ALU.min))
                step(nc.vector.tensor_tensor(M1[:, :, :], M1[:, :, :], EE[:, :, :], ALU.subtract))
                dve.wait_ge(ones_ready, 1)
                for h in range(AH):
                    step(nc.vector.tensor_tensor_scan(BB[:, h, 0:PRM], ones[:, :], M1[:, h, 0:PRM], 0.0, ALU.mult, ALU.add))
                dve.sem_inc(b_ready, 1)

            in_pairs(dve, "gla_vr", split, scaled("gla_vr", QKVR[:, KB:24, :]), gate)

            b = full(dve, ("lv", 0, 0))
            freed(nc.vector.tensor_tensor(ST0[:, :, 0:P], b[:, :].rearrange("p (h t) -> p h t", h=AH),
                                          ident.unsqueeze(1).to_broadcast([P, AH, P]), ALU.mult), ("lv", 0, 0))
            b = full(dve, ("lv", 0, 1))
            freed(nc.vector.tensor_tensor(ST1[:, :, 0:P], b[:, :].rearrange("p (h t) -> p h t", h=AH),
                                          ident.unsqueeze(1).to_broadcast([P, AH, P]), ALU.mult), ("lv", 0, 1))
            b = full(dve, ("lv", 0, 2))
            freed(nc.vector.tensor_tensor(ST2[:, :, :], b[0:META, 0:AH * META].rearrange("p (h t) -> p h t", h=AH),
                                          ident[0:META, 0:META].unsqueeze(1).to_broadcast([META, AH, META]),
                                          ALU.mult), ("lv", 0, 2))
            dve.wait_ge(masks_in, 16)
            levels = LEVELS + [128, 256]

            def sides(l):
                if l == 256:
                    return lambda t: t[:, :, 0:256], lambda t: t[:, :, 256:PRM], BB[:, :, 255:256]
                n = (PRM if l <= 8 else 256) // (2 * l)
                view = lambda t: t[:, :, 0:2 * l * n].rearrange("p h (n l) -> p h n l", l=2 * l)
                return lambda t: view(t)[:, :, :, 0:l], lambda t: view(t)[:, :, :, l:2 * l], view(BB)[:, :, :, l - 1:l]

            def exponents(j):
                e = EEs[j % 2]
                if j >= 2:
                    dve.wait_ge(m_ready, j - 1)
                if j == len(levels):
                    nc.vector.tensor_tensor(e[:, :, 0:PRM], BB[:, :, PRM - 1:PRM].to_broadcast([P, AH, PRM]), BB[:, :, 0:PRM],
                                            ALU.subtract).then_inc(d_ready, 1)
                    return
                left, right, ref = sides(levels[j])
                nc.vector.tensor_tensor(left(e), ref.to_broadcast(list(left(e).shape)), left(BB), ALU.subtract)
                nc.vector.tensor_tensor(right(e), right(BB), ref.to_broadcast(list(right(e).shape)),
                                        ALU.subtract).then_inc(d_ready, 1)

            def decayed(j):
                e, m = EEs[j % 2], M1s[j % 2]
                dve.wait_ge(e_ready, j + 1)
                if j == len(levels):
                    nc.vector.tensor_tensor(m[:, :, 0:PRM], e[:, :, 0:PRM], K[:, :, 0:PRM], ALU.mult).then_inc(m_ready, 1)
                    return
                left, right, _ = sides(levels[j])
                nc.vector.tensor_tensor(left(m), left(e), left(K), ALU.mult)
                nc.vector.tensor_tensor(right(m), right(e), right(Q), ALU.mult).then_inc(m_ready, 1)

            def level_scores(j):
                l = levels[j]
                heads_of = lambda b, lo, hi: b[:, lo:hi].rearrange("p (h t) -> p h t", h=AH)
                if l < 128:
                    for i, S in enumerate((ST0, ST1, ST2)[0:3 if l <= 8 else 2]):
                        b = full(dve, ("lv", l, i))
                        r = META if i == 2 else P
                        taken(dve, ("lv", ([0] + LEVELS)[j], i))
                        freed(nc.vector.copy_predicated(
                            S[:, :, 0:r], masks[0:r, j, 0:r].bitcast(i32).unsqueeze(1).to_broadcast([r, AH, r]),
                            b[0:r, 0:AH * r].rearrange("p (h t) -> p h t", h=AH)), ("lv", l, i))
                elif l == 128:
                    b = full(dve, ("lv", 128, 0))
                    freed(nc.vector.tensor_copy(ST0[:, :, P:256], heads_of(b, 0, AH * P)), ("lv", 128, 0))
                else:
                    b = full(dve, ("lv", 256, 0))
                    nc.vector.tensor_copy(ST0[:, :, 256:PRM], heads_of(b, 0, 64))
                    freed(nc.vector.tensor_copy(ST1[:, :, P:144], heads_of(b, 64, 128)), ("lv", 256, 0))

            exponents(0)
            for j in range(len(levels) + 1):
                if j < len(levels):
                    exponents(j + 1)
                decayed(j)
                if j == 1:
                    dve.wait_ge(hi3, 1)
                    nc.vector.tensor_tensor(V3[32:32 + SMP, :], Vs[:, :], V3[0:SMP, :].bitcast(f32), ALU.subtract)
                    b = full(dve, ("ks", 0))
                    freed(nc.vector.tensor_tensor(K3[64:64 + SMP, :], b[0:SMP, :], K3[0:SMP, :].bitcast(f32),
                                                  ALU.subtract), ("ks", 0))
                if j:
                    level_scores(j - 1)
            for o in range(KB):
                b = full(dve, ("o", o))
                freed(nc.vector.tensor_scalar(O[:, o, 0:PRM], b[:, 0:PRM], P ** -0.5, None, ALU.mult), ("o", o))

            taken(dve, ("o", KB - 1))
            dve.sem_inc(o_ready, 1)

            heads = lambda t: t.rearrange("p (h j) t -> p h j t", j=2)

            def mask_key(n):
                if n >= 2:
                    full(dve, ("kv", n - 2, 1))
                nc.vector.tensor_scalar(KM[:, n % 2, :], K3[:, :].bitcast(f32), part("sel")[0:96, n:n + 1], None,
                                        ALU.mult).then_inc(km_ready, 1)

            def head_mean(h):
                b = full(dve, ("hn", h))
                freed(nc.vector.tensor_scalar(RH[:, h, 0:PRM], b[:, 0:PRM], EPS, None, ALU.add), ("hn", h))
                taken(dve, ("hn", h))
                nc.vector.reciprocal(RH[:, h, 0:PRM], RH[:, h, 0:PRM]).then_inc(rh_in, 1)

            def head_out(h):
                dve.wait_ge(rh_out, h + 1)
                for j in range(2):
                    step(nc.vector.tensor_tensor(O[:, 2 * h + j, 0:PRM], O[:, 2 * h + j, 0:PRM], RH[:, h, 0:PRM], ALU.mult))
                    nc.vector.scalar_tensor_tensor(O[:, 2 * h + j, 0:PRM], O[:, 2 * h + j, 0:PRM], part("ghead")[:, j:j + 1],
                                                   R[:, 2 * h + j, 0:PRM], ALU.mult, ALU.mult)

            dve.wait_ge(ela_ready, 1)
            taken(dve, ("ks", 0))
            mask_key(0)
            mask_key(1)
            for n in range(SMP):
                if 2 <= n <= AH + 1:
                    head_mean(n - 2)
                i = n % GSLOTS
                dve.wait_ge(s_in[i], 16 * (n // GSLOTS + 1))
                for g in range(2):
                    b = full(dve, ("kv", n, g))
                    for k in range(2):
                        h = 2 * g + k
                        ins = nc.vector.scalar_tensor_tensor(S0[:, i, h, :], S0[:, i, h, :], ela[:, h, n:n + 1],
                                                             b[:, k * DV:(k + 1) * DV], ALU.mult, ALU.add)
                    freed(ins, ("kv", n, g))
                if n + 2 < SMP:
                    mask_key(n + 2)
                if n == 2:
                    dve.wait_ge(sr_ready, 1)
                if 2 <= n <= AH + 1:
                    head_out(n - 2)
            dve.wait_ge(s_used, SMP)
            nc.vector.tensor_scalar(O[:, :, PRM:TOK], held[:, 0:KB * SMP].rearrange("p (b n) -> p b n", b=KB),
                                    P ** -0.5, None, ALU.mult).then_inc(o_ready, 1)
            b = full(dve, ("hns", 0))
            freed(nc.vector.tensor_scalar(RH[:, :, PRM:TOK], b[:, 0:AH * SMP].rearrange("p (h n) -> p h n", h=AH), EPS, None,
                                          ALU.add), ("hns", 0))
            taken(dve, ("hns", 0))
            nc.vector.reciprocal(RH[:, :, PRM:TOK], RH[:, :, PRM:TOK]).then_inc(rh_in, 1)
            dve.wait_ge(rh_out, AH + 1)
            for j in range(2):
                own = heads(O[:, :, PRM:TOK])[:, :, j, :]
                step(nc.vector.tensor_tensor(own, own, RH[:, :, PRM:TOK], ALU.mult))
                step(nc.vector.scalar_tensor_tensor(own, own, part("ghead")[:, j:j + 1], heads(R)[:, :, j, PRM:TOK],
                                                    ALU.mult, ALU.mult))
            dve.sem_inc(of_ready, 1)
            for m in range(0, KB, 2):
                dve.wait_ge(oh_ready, m // 2 + 1)
                nc.vector.tensor_tensor(HL[:, m:m + 2, :], XG[:, m:m + 2, :], HH[:, m:m + 2, :].bitcast(f32),
                                        ALU.subtract).then_inc(ol_ready, 1)
            in_pairs(dve, "gla_out", split, lambda g, half, par: [
                residual("gla_out", 2, 1.0, "ffn1", 2 * g + k, 2 * par + k) for k in range(2)])
            dve.wait_ge(sp_out, 16)
            ffn(1, "kv", 3, lambda: norm(2))

            for i in range(GSLOTS):
                dve.wait_ge(s_out[i], 16 * SMP // GSLOTS)
            in_pairs(dve, "kv_in", split, scaled("kv_in", KVf), lambda: norm(3))
            b = full(dve, ("f", 0))
            ins = nc.vector.tensor_tensor(lt[:, 2, :], b[0:BH, 0:TOK], RS[0:BH, :], ALU.mult)
            freed(ins, ("f", 0))
            dve.wait_ge(misc_free[PLAN[("f", 0)][0]], PLAN[("f", 0)][1] + 1)
            nc.vector.tensor_scalar(lt[:, 0, :], lt[:, 2, :], part("bf")[0:BH, :], None, ALU.add).then_inc(lf_in, 1)
            dve.wait_ge(l_ready, 2)
            step(nc.vector.tensor_scalar(lt[:, 0, :], lt[:, 0, :], 0.0, None, ALU.min))
            step(nc.vector.tensor_tensor(LG[:, :], lt[:, 0, :], lt[:, 1, :], ALU.subtract))
            nc.vector.tensor_tensor_scan(CC[:, :], ones[0:BH, :], LG[:, 0:PRM], 0.0, ALU.mult, ALU.add).then_inc(lf_ready, 1)
            highs("ffn2")
            lows("ffn2")
            ffn(2, "fox", 4)

            def norm_and_keys():
                norm(4)
                dve.wait_ge(kh_ready, 1)
                nc.vector.tensor_tensor(KL, Kf[:, :, 0:PRM], KH.bitcast(f32), ALU.subtract).then_inc(kl_ready, 1)

            in_pairs(dve, "fox_q", split, scaled("fox_q", Qf), norm_and_keys)
            dve.wait_ge(bank_free, SLOTS + UNIT0["fox_q"] + KB)

            def queries_low(m):
                dve.wait_ge(qh_ready, m // 2 + 1)
                nc.vector.tensor_tensor(QL[:, m:m + 2, :], Qf[:, m:m + 2, :], QH[:, m:m + 2, :].bitcast(f32),
                                        ALU.subtract).then_inc(ql_ready, 1)

            queries_low(0)
            step(nc.vector.tensor_scalar(C8[:, :], CC[:, :], -(HD ** 0.5), None, ALU.mult))
            step(nc.vector.memset(CB[:, :], 0.0))
            for k in range(3):
                rows = CB[32 * k:32 * k + BH, :]
                step(nc.vector.tensor_copy(rows, C8[:, :]))
                if k < 2:
                    step(nc.vector.tensor_copy(part_f[:, :], rows))
                    step(nc.vector.tensor_tensor(C8[:, :], C8[:, :], part_f[:, :], ALU.subtract))
            nc.vector.tensor_copy(pick[:, :], part("pick")[0:96, :])
            nc.vector.tensor_copy(ident_b[:, :], ident)
            nc.vector.tensor_copy(tri_b[:, :], part("tri")).then_inc(qb_ready, 1)
            dve.wait_ge(qb_zero, 1)
            for e in range(2):
                r = slice(HD * e, HD * (e + 1))
                nc.vector.tensor_copy(QB[r, :, :, e], Qf[r, :, PRM:TOK]).then_inc(qb_ready, 1)

            def maxima(h):
                q = h % 2
                b = full(dve, ("s", h, 0))
                if h >= 2:
                    taken(dve, ("s", h - 2, 1))
                nc.vector.reduce_max(MX[:, q, 0:1], b[:, 0:P], AX.X)
                step(nc.vector.reduce_max(MX[:, q, 1:2], b[:, P:3 * P], AX.X))
                nc.vector.tensor_scalar(NM[:, q, 0:2], MX[:, q, 0:2], -(HD ** -0.5), None, ALU.mult).then_inc(nm_ready, 1)
                b = full(dve, ("s", h, 1))
                step(nc.vector.reduce_max(MX[0:META, q, 2:3], b[0:META, 0:PRM], AX.X))
                nc.vector.tensor_scalar(NM[0:META, q, 2:3], MX[0:META, q, 2:3], -(HD ** -0.5), None,
                                        ALU.mult).then_inc(nm_ready, 1)

            def probs_low(h):
                b = misc[PLAN[("pt", h)][0]]
                dve.wait_ge(pth_ready, h + 1)
                for rows, c in ((P, slice(0, PRM + 144)), (META, slice(PRM + 144, PRM + 144 + META))):
                    ins = nc.vector.tensor_tensor(PTL[0:rows, h % 2, c], b[0:rows, c], PTH[0:rows, h % 2, c].bitcast(f32),
                                                  ALU.subtract)
                freed(ins, ("pt", h))

            def normalize(h):
                q = h % 2
                taken(dve, ("s", h, 1))
                step(nc.vector.reciprocal(RW[:, q, :], RW[:, q, :]))
                nc.vector.tensor_scalar(PP[:, q, 0:P], PP[:, q, 0:P], RW[:, q, 0:1], None, ALU.mult)
                nc.vector.tensor_scalar(PP[:, q, P:3 * P], PP[:, q, P:3 * P], RW[:, q, 1:2], None, ALU.mult)
                nc.vector.tensor_scalar(PP[0:META, q, 3 * P:], PP[0:META, q, 3 * P:], RW[0:META, q, 2:3], None,
                                        ALU.mult).then_inc(pn_ready, 1)

            def page_scores(n):
                for i in (2 * n, 2 * n + 1):
                    dve.wait_ge(page_in[i % PAGES], 16 * (i // PAGES + 1))
                for k in range(2):
                    b = full(dve, ("qb", n, k))
                    for i in (2 * n, 2 * n + 1):
                        c = PG[i % PAGES][:, k * 512:(k + 1) * 512]
                        ins = nc.vector.tensor_tensor(c, c, b[:, :], ALU.mult)
                    freed(ins, ("qb", n, k))
                taken(dve, ("qb", n, 1))
                for i in (2 * n, 2 * n + 1):
                    nc.vector.reduce_sum(SC[:, i % NPG, n, :], PG[i % PAGES][:, :].rearrange("p (h d) -> p h d", h=BH),
                                         AX.X).then_inc(k_used, 1)

            def page_low(i):
                dve.wait_ge(vph_ready, i + 1)
                nc.vector.tensor_tensor(VpL[i % 2][:, 0:D], PG[(SMP * NPG + i) % PAGES][:, :], VpH[i % 2][:, 0:D].bitcast(f32),
                                        ALU.subtract).then_inc(vpl_ready, 1)

            def sampled_scores_out():
                dve.wait_ge(own_done, 1)
                dve.wait_ge(k_used, SMP * NPG)
                nc.vector.tensor_copy(SO[:, :], held[0:SMP, 2 * P:3 * P]).then_inc(sc_ready, 1)
                b = full(dve, ("lf", 0))
                freed(nc.vector.tensor_copy(LD[:, 0:2 * P], b[:, 0:2 * P]), ("lf", 0))
                b = full(dve, ("lown", 0))
                freed(nc.vector.tensor_tensor(own_t[:, 0, :], b[:, 0:SMP], part("own"), ALU.mult), ("lown", 0))
                taken(dve, ("lown", 0))
                step(nc.vector.reduce_sum(LD[:, 2 * P:2 * P + 1], own_t[:, 0, :], AX.X))
                step(nc.vector.tensor_tensor_scan(CD[:, :], ones[:, 0:2 * P + 1], LD[:, :], 0.0, ALU.mult, ALU.add))
                step(nc.vector.tensor_scalar(LD[:, :], CD[:, :], -1.0, CD[:, 2 * P:2 * P + 1], ALU.mult, ALU.add))

            def sampled_scores():
                b = full(dve, ("sct", 0))
                step(nc.vector.tensor_tensor(own_t[:, 1, :], b[:, 2 * P:2 * P + SMP], part("own"), ALU.mult))
                step(nc.vector.reduce_sum(col[:, 2:3], own_t[:, 1, :], AX.X))
                nc.vector.scalar_tensor_tensor(SD[:, 2 * P:2 * P + 1], col[:, 2:3], HD ** -0.5, LD[:, 2 * P:2 * P + 1],
                                               ALU.mult, ALU.add)
                freed(nc.vector.scalar_tensor_tensor(SD[:, 0:2 * P], b[:, 0:2 * P], HD ** -0.5, LD[:, 0:2 * P],
                                                     ALU.mult, ALU.add), ("sct", 0))
                taken(dve, ("sct", 0))
                nc.vector.tensor_reduce(col[:, 0:1], SD[:, :], AX.X, ALU.max, negate=True).then_inc(sd_ready, 1)

            def sampled_probs():
                dve.wait_ge(pd_ready, 1)
                step(nc.vector.reciprocal(col[:, 3:4], col[:, 1:2]))
                step(nc.vector.tensor_scalar(PD[:, :], PD[:, :], col[:, 3:4], None, ALU.mult))
                nc.vector.tensor_scalar(PM[:, :], part("own"), PD[:, 2 * P:2 * P + 1], None, ALU.mult).then_inc(pe_ready, 1)

            def sampled_probs_out():
                b = full(dve, ("pdt", 0))
                dve.wait_ge(pdh_ready, NPG)
                nc.vector.tensor_copy(PMT[:, :], b[0:SMP, 2 * P:3 * P])
                for g in range(NPG):
                    ins = nc.vector.tensor_tensor(PDT[g][:, :, 1, :], b[:, g * P:(g + 1) * P].rearrange("p (n h) -> p n h", n=SMP),
                                                  PDT[g][:, :, 0, :].bitcast(f32), ALU.subtract)
                freed(ins, ("pdt", 0))

            def own_heads(n):
                r = slice(32 * (n % 4), 32 * (n % 4 + 1))
                for k in range(2):
                    b = full(dve, ("u", n, k))
                    own = part("hsel")[0:32, k * BH // 2:(k + 1) * BH // 2].unsqueeze(2).to_broadcast([32, BH // 2, HD])
                    freed(nc.vector.tensor_tensor(UM[r, n // 4, k * 512:(k + 1) * 512].rearrange("p (h d) -> p h d", d=HD),
                                                  b[0:32, :].rearrange("p (h d) -> p h d", d=HD), own, ALU.mult), ("u", n, k))

            for k in range(2):
                dve.wait_ge(q3h_ready, k + 1)
                c = slice(k * 512, (k + 1) * 512)
                b = misc[PLAN[("qt", k)][0]]
                freed(nc.vector.tensor_tensor(Q3[32:32 + SMP, c], b[0:SMP, :], Q3[0:SMP, c].bitcast(f32), ALU.subtract), ("qt", k))
            maxima(0)
            for m in range(2, KB, 2):
                queries_low(m)
            dve.wait_ge(vh_ready, 1)
            nc.vector.tensor_tensor(VL[:, 0:2, :], Vtok[:, 0:2, :], VH[:, 0:2, :].bitcast(f32), ALU.subtract)
            nc.vector.tensor_tensor(VL[0:META, 2, :], Vtok[0:META, 2, :], VH[0:META, 2, :].bitcast(f32),
                                    ALU.subtract).then_inc(vl_ready, 1)
            for h in range(BH):
                if h:
                    probs_low(h - 1)
                normalize(h)
                if h + 1 < BH:
                    maxima(h + 1)
                if h < SMP:
                    page_scores(h)
                if h == SMP:
                    sampled_scores_out()
                if h == SMP + 1:
                    sampled_scores()
                if h == SMP + 2:
                    sampled_probs()
                    sampled_probs_out()
                for n in VALUES.get(h, []):
                    page_low(2 * n)
                    if n:
                        own_heads(n - 1)
                    page_low(2 * n + 1)
            probs_low(BH - 1)
            own_heads(SMP - 1)
            dve.wait_ge(uo_done, 2)
            step(nc.vector.tensor_copy(SD[:, 0:KB * SMP], held[:, 0:KB * SMP]))
            pages = SD[:, 0:KB * SMP].rearrange("p (g k n) -> p g k n", g=2, k=KB)
            ov = held[:, 2 * P:3 * P].rearrange("p (k g n e) -> p g k n e", k=KB, g=2, e=2)
            for e in range(2):
                r = slice(HD * e, HD * (e + 1))
                for g in range(2):
                    ins = nc.vector.tensor_tensor(XG[r, :, PRM + 4 * g:PRM + 4 * (g + 1)], ov[r, g, :, :, e], pages[r, g, :, :],
                                                  ALU.add)
            ins.then_inc(of_ready, 1)
            for m in range(0, KB, 2):
                dve.wait_ge(oh_ready, KB // 2 + m // 2 + 1)
                nc.vector.tensor_tensor(HL[:, m:m + 2, :], XG[:, m:m + 2, :], HH[:, m:m + 2, :].bitcast(f32),
                                        ALU.subtract).then_inc(ol_ready, 1)
            in_pairs(dve, "fox_out", split, lambda g, half, par: [
                residual("fox_out", 5, 1.0, "ffn3", 2 * g + k, 2 * par + k) for k in range(2)])
            ffn(3, "final", 6, lambda: norm(5))
            norm(6)
            for m in range(KB):
                nc.vector.scalar_tensor_tensor(XG[:, m, :], X[:, m, :], gain[:, 7 * KB + m:7 * KB + m + 1], RS[:, :],
                                               ALU.mult, ALU.mult).then_inc(y_ready, 1)

        @block.tensor
        def _(pe):
            mm = nc.tensor.matmul

            def empty(key):
                b, n = PLAN[key]
                if n:
                    pe.wait_ge(misc_free[b], n)
                return misc[b]

            def filled(ins, key):
                ins.then_inc(misc_full[PLAN[key][0]], 1)

            def products(out, s, act_hi, act_lo, k0, tiles, first, last, ready=None):
                for k in range(tiles):
                    wh, wl = w_hi[s][:, k * P:(k + 1) * P], w_lo[s][:, k * P:(k + 1) * P]
                    if ready:
                        ready(k)
                    mm(out, wh, act_hi[:, k0 + k, :], start=first and k == 0, stop=False)
                    mm(out, wh, act_lo[:, k0 + k, :], start=False, stop=False)
                    ins = mm(out, wl, act_hi[:, k0 + k, :], start=False, stop=last and k == tiles - 1)
                return ins

            def project(seg, act_hi, act_lo, ready, stage=None, second=None, fifth=None):
                def chunk(at, s, ready=None):
                    pe.wait_ge(lo_ready, at + (CHUNK0[seg] + s + 1))
                    if stage:
                        pe.wait_ge(x_new, at + (KB * (stage - 1) + s + 1))
                    else:
                        pe.wait_ge(bank_free, at + (UNIT0[seg] + s + 1))
                    products(bank[s][:, 0:TOK], s, act_hi, act_lo, 0, KB, True, True, ready).then_inc(chunk_used, 1)

                chunk(0, 0, ready)
                if second:
                    second()
                for s in range(1, SLOTS):
                    chunk(0, s)
                if fifth:
                    fifth()
                with pe.Fori(1, COUNT[seg] // SLOTS) as i:
                    for s in range(SLOTS):
                        chunk(i * SLOTS, s)

            def normed(name):
                return lambda k: pe.wait_ge(xl_ready, KB * GAIN[name] + k + 1)

            def down(n, stage):
                seg = f"ffn{n}_down"
                with pe.Fori(0, COUNT[seg] // SLOTS) as i:
                    for s in range(SLOTS):
                        u = s // 2
                        pe.wait_ge(hid_ready, FB * n + DNT * (s % 2 + 1))
                        pe.wait_ge(lo_ready, i * SLOTS + (CHUNK0[seg] + s + 1))
                        if s % 2 == 0:
                            pe.wait_ge(x_new, i * 2 + (KB * (stage - 1) + u + 1))
                        products(bank[u][:, 0:TOK], s, HH, HL, DNT * (s % 2), DNT, s % 2 == 0,
                                 s % 2 == 1).then_inc(chunk_used, 1)

            def stat(n):
                pe.wait_ge(ss_ready, n + 1)
                b = empty(("stat", n))
                filled(mm(b[:, 0:TOK], part("mean_d"), SS[:, :], start=True, stop=True), ("stat", n))

            pe.sem_inc(chunk_used, SLOTS)
            pe.wait_ge(const_in, 16)
            project("ffn0_up", XH, XL, normed("ffn0"), second=lambda: stat(0))
            down(0, 1)

            def gate():
                b = empty(("a", 0))
                for k in range(KB):
                    ins = mm(b[0:RANK, 0:TOK], wa[:, k, :], XG[:, k, :], start=k == 0, stop=k == KB - 1)
                filled(ins, ("a", 0))

            project("gla_qk", XH, XL, normed("gla"), second=lambda: stat(1), fifth=gate)
            taken(pe, ("a", 0))
            for h in range(AH):
                b = empty(("z", h))
                filled(mm(b[:, 0:TOK], part("walpha2")[0:RANK, h * P:(h + 1) * P], a_s[:, :], start=True, stop=True), ("z", h))
            project("gla_vr", XH, XL, None)
            pe.wait_ge(bank_free, SLOTS + UNIT0["gla_vr"] + 16)

            def token_major(src, names):
                for i in range(3):
                    rows = P if i < 2 else META
                    for h in range(2):
                        b = empty((names[0], i, h))
                        for k in range(4):
                            ins = nc.tensor.transpose(b[0:rows, k * P:(k + 1) * P], src[:, 4 * h + k, i * P:i * P + rows], ident)
                        filled(ins, (names[0], i, h))
                for h in range(2):
                    b = empty((names[1], h))
                    for k in range(4):
                        ins = nc.tensor.transpose(b[0:SMP, k * P:(k + 1) * P], src[:, 4 * h + k, PRM:TOK], ident)
                    filled(ins, (names[1], h))

            token_major(V, ("vt", "vs"))
            b = empty(("ks", 0))
            for k in range(AH):
                ins = nc.tensor.transpose(b[0:SMP, k * P:(k + 1) * P], K[:, k, PRM:TOK], ident)
            filled(ins, ("ks", 0))
            for li, l in enumerate([0] + LEVELS):
                m = M1s[(li - 1) % 2]
                left, right = (m, m) if l else (K, Q)
                if l:
                    pe.wait_ge(m_ready, li)
                for i in range(3 if l <= 8 else 2):
                    r = META if i == 2 else P
                    b = empty(("lv", l, i))
                    for h in range(AH):
                        ins = mm(b[0:r, h * r:(h + 1) * r], left[:, h, i * P:i * P + r], right[:, h, i * P:i * P + r],
                                 start=True, stop=True)
                    filled(ins, ("lv", l, i))
            pe.wait_ge(m_ready, len(LEVELS) + 1)
            b = empty(("lv", 128, 0))
            for h in range(AH):
                ins = mm(b[:, h * P:(h + 1) * P], M1s[1][:, h, 0:P], M1s[1][:, h, P:256], start=True, stop=True)
            filled(ins, ("lv", 128, 0))
            pe.wait_ge(m_ready, len(LEVELS) + 2)
            b = empty(("lv", 256, 0))
            for i in range(2):
                for h in range(AH):
                    ins = mm(b[:, i * 64 + h * META:i * 64 + (h + 1) * META], M1s[0][:, h, i * P:(i + 1) * P], M1s[0][:, h, 256:PRM],
                             start=True, stop=True)
            filled(ins, ("lv", 256, 0))
            pe.wait_ge(m_ready, len(LEVELS) + 3)
            for i in range(3):
                rows = P if i < 2 else META
                b = empty(("ke", i))
                for h in range(AH):
                    ins = nc.tensor.transpose(b[0:rows, h * P:(h + 1) * P], M1s[1][:, h, i * P:i * P + rows], ident)
                filled(ins, ("ke", i))
            pe.wait_ge(misc_free[PLAN[("ke", 2)][0]], PLAN[("ke", 2)][1] + 1)
            for g in range(2):
                b = empty(("sp", g))
                for h in (2 * g, 2 * g + 1):
                    for i in range(3):
                        r = P if i < 2 else META
                        ins = mm(b[:, (h % 2) * DV:(h % 2 + 1) * DV], KE[0:r, i, h * P:(h + 1) * P],
                                 Vtok[0:r, i, h * DV:(h + 1) * DV], start=i == 0, stop=i == 2)
                filled(ins, ("sp", g))
            taken(pe, ("lv", 256, 0))
            for o in range(KB):
                h = o // 2
                v = slice(o * P, (o + 1) * P)
                b = empty(("o", o))
                mm(b[:, 0:PRM], Vtok[:, 0, v], ST0[:, h, :], start=True, stop=False)
                mm(b[:, P:PRM], Vtok[:, 1, v], ST1[:, h, :], start=False, stop=False)
                filled(mm(b[:, 2 * P:PRM], Vtok[0:META, 2, v], ST2[:, h, :], start=False, stop=True), ("o", o))
            def outer(n):
                pe.wait_ge(km_ready, n + 1)
                for g in range(2):
                    b = empty(("kv", n, g))
                    for h in (2 * g, 2 * g + 1):
                        ins = mm(b[:, (h % 2) * DV:(h % 2 + 1) * DV], KM[:, n % 2, h * P:(h + 1) * P],
                                 V3[:, h * DV:(h + 1) * DV], start=True, stop=True)
                    filled(ins, ("kv", n, g))

            outer(0)
            for n in range(SMP):
                if n + 1 < SMP:
                    outer(n + 1)
                if 1 <= n <= AH:
                    h = n - 1
                    pe.wait_ge(osq_ready, 1)
                    b = empty(("hn", h))
                    mm(b[:, 0:PRM], part("mean_dv"), OSQ[:, 2 * h, 0:PRM], start=True, stop=False)
                    filled(mm(b[:, 0:PRM], part("mean_dv"), OSQ[:, 2 * h + 1, 0:PRM], start=False, stop=True), ("hn", h))
                taken(pe, ("kv", n, 1))
                for o in range(KB):
                    h = o // 2
                    ins = mm(held[:, o * SMP + n:o * SMP + n + 1], S0[:, n % GSLOTS, h, (o % 2) * P:(o % 2 + 1) * P],
                             Q[:, h, PRM + n:PRM + n + 1], start=True, stop=True)
                ins.then_inc(s_used, 1)
            pe.wait_ge(osq_ready, 2)
            b = empty(("hns", 0))
            for h in range(AH):
                out = b[:, h * SMP:(h + 1) * SMP]
                mm(out, part("mean_dv"), OSQ[:, 2 * h, PRM:TOK], start=True, stop=False)
                ins = mm(out, part("mean_dv"), OSQ[:, 2 * h + 1, PRM:TOK], start=False, stop=True)
            filled(ins, ("hns", 0))
            project("gla_out", HH, HL, lambda k: pe.wait_ge(ol_ready, k // 2 + 1), stage=2)
            project("ffn1_up", XH, XL, normed("ffn1"), second=lambda: stat(2))
            down(1, 3)

            def forget():
                b = empty(("f", 0))
                for k in range(KB):
                    ins = mm(b[0:BH, 0:TOK], wf[:, k, :], XG[:, k, :], start=k == 0, stop=k == KB - 1)
                filled(ins, ("f", 0))

            project("kv_in", XH, XL, normed("kv"), second=lambda: stat(3), fifth=forget)
            pe.wait_ge(bank_free, SLOTS + UNIT0["kv_in"] + 16)
            token_major(Vf, ("fvt", "fvs"))
            project("ffn2_up", XH, XL, normed("ffn2"))
            down(2, 4)

            project("fox_q", XH, XL, normed("fox"), second=lambda: stat(4))
            pe.wait_ge(bank_free, SLOTS + UNIT0["fox_q"] + KB)
            for k in range(2):
                b = empty(("qt", k))
                for j in range(4):
                    ins = nc.tensor.transpose(b[0:SMP, j * P:(j + 1) * P], Qf[:, 4 * k + j, PRM:TOK], ident)
                filled(ins, ("qt", k))
            pe.wait_ge(qb_ready, 1)
            pe.wait_ge(kl_ready, 1)

            def scores(h):
                r = slice(HD * (h % 2), HD * (h % 2 + 1))
                pe.wait_ge(ql_ready, h // 4 + 1)
                for i in range(3):
                    rows = P if i < 2 else META
                    keys = min((i + 1) * P, PRM)
                    b = empty(("s", h, i // 2)) if i != 1 else b
                    out = b[0:rows, (P if i == 1 else 0):(P if i == 1 else 0) + keys]
                    for qp, kp, first in ((QH, KH, True), (QL, KH, False), (QH, KL, False)):
                        mm(out, qp[r, h // 2, i * P:i * P + rows], kp[r, h // 2, 0:keys], start=first, stop=False)
                    mm(out, pick[:, h:h + 1].to_broadcast([96, rows]), CB[:, 0:keys], start=False, stop=False)
                    diag = b[0:rows, (P if i == 1 else 0) + i * P:(P if i == 1 else 0) + keys]
                    ins = mm(diag, ident_b[0:rows, 0:rows], tri_b[0:rows, 0:rows], start=False, stop=True)
                    if i:
                        filled(ins, ("s", h, i // 2))

            def queries(n):
                taken(pe, ("qt", 1))
                pe.wait_ge(sel_ready, 1)
                for k in range(2):
                    b = empty(("qb", n, k))
                    filled(mm(b[:, :], sel_r[:, n:n + 1].to_broadcast([64, P]), Q3[:, k * 512:(k + 1) * 512],
                              start=True, stop=True), ("qb", n, k))

            def own_scores():
                pe.wait_ge(qb_ready, 3)
                own_s = held[0:SMP, 2 * P:3 * P].rearrange("p (n j e) -> p n j e", n=SMP, e=2)
                for j in range(KB):
                    ins = mm(own_s[:, :, j, :], Kf[:, j, PRM:TOK], QB[:, j, :, :], start=True, stop=True)
                ins.then_inc(own_done, 1)
                pe.wait_ge(lfp_in, 16 * SMP * NPG)
                b = empty(("lf", 0))
                for g in range(NPG):
                    ins = nc.tensor.transpose(b[:, g * P:(g + 1) * P], LFp[:, g, :, :].rearrange("p n h -> p (n h)"), ident)
                filled(ins, ("lf", 0))
                b = empty(("lown", 0))
                filled(mm(b[:, 0:SMP], part("rep")[0:BH, :], LG[:, PRM:TOK], start=True, stop=True), ("lown", 0))

            def sampled_scores():
                pe.wait_ge(sc_ready, 1)
                b = empty(("sct", 0))
                for g in range(NPG):
                    nc.tensor.transpose(b[:, g * P:(g + 1) * P], SC[:, g, :, :].rearrange("p n h -> p (n h)"), ident)
                filled(nc.tensor.transpose(b[:, 2 * P:2 * P + SMP], SO[:, :], ident[0:SMP, 0:SMP]), ("sct", 0))

            def sampled_probs():
                pe.wait_ge(pe_ready, 1)
                b = empty(("pdt", 0))
                for g in range(NPG):
                    nc.tensor.transpose(b[:, g * P:(g + 1) * P], PD[:, g * P:(g + 1) * P], ident)
                filled(nc.tensor.transpose(b[0:SMP, 2 * P:3 * P], PM[:, :], ident), ("pdt", 0))

            def own_values():
                taken(pe, ("pdt", 0))
                for j in range(KB):
                    mm(held[:, 2 * P + j * 2 * SMP:2 * P + (j + 1) * 2 * SMP], Vs[:, j * P:(j + 1) * P],
                       PMT[:, :].rearrange("p (n h) -> p n h", n=SMP)[:, :, 2 * j:2 * j + 2], start=True, stop=True)

            def page_values(n):
                for i in (2 * n, 2 * n + 1):
                    pe.wait_ge(vpl_ready, i + 1)
                    g = i % NPG
                    for k in range(2):
                        b = empty(("u", n, k))
                        probs = PDT[g][:, n, :, :].rearrange("p x h -> p (x h)")
                        mm(b[0:32, :], probs, VpH[i % 2][:, k * 512:(k + 1) * 512], start=g == 0, stop=False)
                        ins = mm(b[0:32, :], probs, VpL[i % 2][:, k * 512:(k + 1) * 512], start=False, stop=g == 1)
                        if g:
                            filled(ins, ("u", n, k))
                    if g == 0:
                        ins.then_inc(pv_done, 1)

            def sampled_outputs(g):
                taken(pe, ("u", 4 * g + 3, 1))
                for j in range(KB):
                    at = (g * KB + j) * 4
                    ins = mm(held[:, at:at + 4], UM[:, g, j * P:(j + 1) * P], part("quad"), start=True, stop=True)
                ins.then_inc(uo_done, 1)

            def transpose_probs(h):
                q = h % 2
                pe.wait_ge(pn_ready, h + 1)
                b = empty(("pt", h))
                nc.tensor.transpose(b[:, 0:P], PP[:, q, 0:P], ident)
                nc.tensor.transpose(b[:, P:2 * P], PP[:, q, P:2 * P], ident)
                nc.tensor.transpose(b[:, 2 * P:PRM], PP[0:META, q, 3 * P:4 * P], ident[0:META, 0:META])
                nc.tensor.transpose(b[:, PRM:PRM + P], PP[:, q, 2 * P:3 * P], ident)
                nc.tensor.transpose(b[:, PRM + P:PRM + 144], PP[0:META, q, 4 * P:5 * P], ident[0:META, 0:META])
                filled(nc.tensor.transpose(b[0:META, PRM + 144:PRM + 144 + META], PP[0:META, q, 5 * P:5 * P + META],
                                           ident[0:META, 0:META]), ("pt", h))

            def values(h):
                q = h % 2
                taken(pe, ("pt", h))
                pe.wait_ge(vl_ready, 1)
                if h >= 2:
                    pe.wait_ge(po_read, h - 1)
                out = bank[2 + q]
                v = slice(h // 2 * P, (h // 2 + 1) * P)
                for vp, pp, k in ((VH, PTH, 0), (VH, PTL, 1), (VL, PTH, 2)):
                    mm(out[:, 0:PRM], vp[:, 0, v], pp[:, q, 0:PRM], start=k == 0, stop=False)
                    mm(out[:, P:PRM], vp[:, 1, v], pp[:, q, PRM:PRM + 144], start=False, stop=False)
                    ins = mm(out[:, 2 * P:PRM], vp[0:META, 2, v], pp[0:META, q, PRM + 144:], start=False, stop=k == 2)
                ins.then_inc(fo_done, 1)

            scores(0)
            for h in range(BH):
                if h + 1 < BH:
                    scores(h + 1)
                if h:
                    values(h - 1)
                if h < SMP:
                    queries(h)
                if h == SMP:
                    own_scores()
                if h == SMP + 1:
                    sampled_scores()
                if h == SMP + 2:
                    sampled_probs()
                transpose_probs(h)
                if h == SMP + 2:
                    own_values()
                if h == SMP + 7:
                    sampled_outputs(0)
                for n in VALUES.get(h, []):
                    page_values(n)
            values(BH - 1)
            sampled_outputs(1)
            project("fox_out", HH, HL, lambda k: pe.wait_ge(ol_ready, KB // 2 + k // 2 + 1), stage=5)
            project("ffn3_up", XH, XL, normed("ffn3"), second=lambda: stat(5))
            down(3, 6)
            stat(6)


def constants():
    import numpy as np
    s, t = np.arange(P)[:, None], np.arange(P)[None, :]
    eye = (s == t).astype(np.float32)
    own = (np.arange(P)[:, None] // BH == np.arange(SMP)[None, :]).astype(np.float32)
    rep = np.zeros((P, P), np.float32)
    rep[:BH] = (np.arange(BH)[:, None] == np.arange(P)[None, :] % BH)
    tri = np.where(t > s, np.float32(-1e30), np.float32(0))
    masks = np.stack([(s // (2 * l) == t // (2 * l)) & (s % (2 * l) < l) & (t % (2 * l) >= l) for l in LEVELS], 1)
    return {"ident": eye, "mean_d": np.full((P, P), 1.0 / D, np.float32), "mean_dv": np.full((P, P), 1.0 / DV, np.float32),
            "tri": tri, "own": own,
            "hsel": (np.arange(P)[:, None] % BH == np.arange(BH)[None, :]).astype(np.float32),
            "quad": (np.arange(P)[:, None] // 32 == np.arange(4)[None, :]).astype(np.float32), "sel": (np.arange(96)[:, None] % 32 == np.arange(SMP)[None, :]).astype(np.float32), "rep": rep,
            "pick": (np.arange(96)[:, None] % 32 == np.arange(BH)[None, :]).astype(np.float32)}, masks.astype(np.float32)


def kernel(**inputs):
    import numpy as np
    import concourse.bacc as bacc
    from concourse.bass_utils import run_bass_kernel_spmd

    a = {k: np.asarray(v) for k, v in inputs.items()}
    f32 = np.float32

    def chunks(w, tiles, n_cols):
        w = w[:, :n_cols].reshape(w.shape[0] // (P * tiles), tiles, P, n_cols // P, P)
        return w.transpose(3, 0, 2, 1, 4).reshape(-1, P, tiles * P)

    def columns(v):
        return v.reshape(-1, P).T

    up, down = [], []
    for l in range(2):
        for f in ("ffn1", "ffn2"):
            gate, upper = chunks(a[f + "_w_gate"][l], KB, FF), chunks(a[f + "_w_up"][l], KB, FF)
            up.append(np.stack([gate, upper], 1).reshape(2 * FB, P, UPW))
            down.append(chunks(a[f + "_w_down"][l], DNT, D))
    mix = [chunks(a["gla_w_in"][0], KB, 24 * P), chunks(a["gla_w_out"][0], KB, D), chunks(a["kv_w_in"], KB, 2 * D),
           chunks(a["fox_w_q"][0], KB, D), chunks(a["fox_w_out"][0], KB, D)]
    x = np.concatenate([a["meta_tokens"], a["x_prompt"][0], a["x_sample"][:, 0]], 0)

    const, masks = constants()
    gains = [a["norm_ffn1"][0], a["norm_mix"][0], a["norm_ffn2"][0], a["kv_norm"], a["norm_ffn1"][1], a["norm_mix"][1],
             a["norm_ffn2"][1], a["final_norm"]]
    const["gain"] = np.concatenate([columns(g) for g in gains], 1)
    const["ghead"] = columns(a["gla_g_head"][0])
    const["balpha"] = columns(a["gla_b_alpha"][0])
    const["bf"] = a["kv_b_f"][:, None]
    const["walpha2"] = a["gla_w_alpha2"][0]
    const["wa"] = a["gla_w_in"][0][:, 24 * P:].reshape(KB, P, RANK).transpose(1, 0, 2).reshape(P, -1)
    const["wf"] = a["kv_w_in"][:, 2 * D:].reshape(KB, P, BH).transpose(1, 0, 2).reshape(P, -1)
    small = np.zeros((P, NCOL), f32)
    for name, (lo, hi) in COL.items():
        small[:const[name].shape[0], lo:hi] = const[name]

    n_phys = a["cache_k"].shape[0]
    arrays = {
        "x_all": x.T.reshape(KB, P, TOK), "up_w": np.concatenate(up, 0), "down_w": np.concatenate(down, 0),
        "mix_w": np.concatenate(mix, 0), "small": small, "level_masks": masks, "state_in": a["state_gla"][0],
        "cache_k": a["cache_k"].reshape(n_phys, PAGE, D), "cache_v": a["cache_v"].reshape(n_phys, PAGE, D),
        "cache_f": a["cache_logf"], "table": a["page_table"].reshape(1, SMP * NPG),
    }
    arrays = {k: np.ascontiguousarray(v) for k, v in arrays.items()}
    outs = {"y_out": (KB, P, TOK), "k_out": (KB, P, TOK), "v_out": (KB, P, TOK), "lf_out": (BH, TOK),
            "state_prompt": (AH, P, DV), "state_sample": (SMP, AH, P, DV)}

    nc = bacc.Bacc("TRN2", target_bir_lowering=False, num_devices=1)
    args = [nc.dram_tensor(k, v.shape, mybir.dt.from_np(v.dtype), kind="ExternalInput").ap() for k, v in arrays.items()]
    args += [nc.dram_tensor(k, v, mybir.dt.float32, kind="ExternalOutput").ap() for k, v in outs.items()]
    build(nc, *args)
    r = run_bass_kernel_spmd(nc, [arrays], core_ids=[0]).results[0]

    def rows(name):
        return r[name].reshape(D, TOK).T

    y, k, v, lf = rows("y_out"), rows("k_out"), rows("v_out"), r["lf_out"].T
    return (y[None, META:PRM], y[PRM:, None], r["state_prompt"][None, None],
            k[:PRM].reshape(1, PRM, BH, HD), v[:PRM].reshape(1, PRM, BH, HD), lf[None, :PRM],
            r["state_sample"][None],
            k[PRM:].reshape(SMP, 1, BH, HD), v[PRM:].reshape(SMP, 1, BH, HD), lf[PRM:, None])
```

```python
import concourse.bass as bass
from concourse import mybir
from contextlib import ExitStack

P = 128
D = 1024
KB = D // P
META, SEQ, SMP = 16, 256, 8
PRM = META + SEQ
TOK = PRM + SMP
FF = 2816
FB = FF // P
UPW = KB * P
DNT = FB // 2
DNW = DNT * P
SLOTS = 4
AH, DV = 4, 256
BH, HD = 16, 64
RANK = 16
PAGE, NPG = 128, 2
GSLOTS = 4
PAGES = 4
VALUES = SMP + 2
EPS = 1e-6
LEVELS = [1, 2, 4, 8, 16, 32, 64]

SEGS = []
for _name in ("ffn0", "gla", "ffn1", "kv", "ffn2", "fox", "ffn3"):
    if _name.startswith("ffn"):
        SEGS += [(_name + "_up", 2 * FB, KB), (_name + "_down", 2 * KB, DNT)]
    elif _name == "gla":
        SEGS += [("gla_qk", KB, KB), ("gla_v", KB, KB), ("gla_r", KB, KB), ("gla_out", KB, KB)]
    elif _name == "kv":
        SEGS += [("kv_in", 16, KB)]
    else:
        SEGS += [("fox_q", KB, KB), ("fox_out", KB, KB)]
CHUNK0, UNIT0, COUNT, TILES, NEXT = {}, {}, {}, {}, {}
_c = _u = 0
for _i, (_name, _n, _t) in enumerate(SEGS):
    CHUNK0[_name], UNIT0[_name], COUNT[_name], TILES[_name] = _c, _u, _n, _t
    NEXT[_name] = SEGS[_i + 1][0] if _i + 1 < len(SEGS) else None
    _c += _n
    _u += _n if not _name.endswith(("_down", "_out")) else 0
MIX0 = {"gla_qk": 0, "gla_v": 8, "gla_r": 16, "gla_out": 24, "kv_in": 32, "fox_q": 48, "fox_out": 56}
GAINS = ("ffn0", "gla", "ffn1", "kv", "ffn2", "fox", "ffn3", "final")
GAIN = {n: i for i, n in enumerate(GAINS)}
STAGE = {"ffn0": 0, "gla": 1, "ffn1": 2, "kv": 3, "ffn2": 3, "fox": 4, "ffn3": 5, "final": 6}

COL = {}
_at = 0
for _n, _w in (("ident", P), ("mean_d", P), ("mean_dv", P), ("tri", P), ("own", SMP), ("sel", SMP), ("hsel", BH), ("quad", 4),
               ("rep", P), ("pick", BH),
               ("gain", 8 * KB), ("ghead", 2), ("balpha", AH), ("bf", 1), ("walpha2", 4 * P),
               ("wa", KB * RANK), ("wf", KB * BH)):
    COL[_n] = (_at, _at + _w)
    _at += _w
NCOL = _at


def misc_plan():
    first = [("stat", 0), ("stat", 1), ("a", 0)] + [("z", h) for h in range(AH)]
    gla = [("vt", i, h) for i in range(3) for h in range(2)] + [("vs", 0), ("vs", 1), ("ks", 0)]
    for l in [0] + LEVELS:
        gla += [("lv", l, i) for i in range(3 if l <= 8 else 2)]
    gla += [("lv", 128, 0), ("lv", 256, 0)]
    gla += [("kv", 0, 0), ("kv", 0, 1), ("kv", 1, 0), ("kv", 1, 1)] + [("ke", i) for i in range(3)]
    for n in range(SMP):
        gla += [("o", 2 * n), ("o", 2 * n + 1)] if n < AH else [("hn", n - AH)]
        if n >= SMP - 2:
            gla += [("sp", n - (SMP - 2))]
        if n + 2 < SMP:
            gla += [("kv", n + 2, 0), ("kv", n + 2, 1)]
    gla += [("hns", 0)]
    middle = [("stat", 2), ("stat", 3), ("f", 0)]
    middle += [("fvt", i, h) for i in range(3) for h in range(2)] + [("fvs", 0), ("fvs", 1)]
    middle += [("stat", 4)]
    fox = [("qt", 0), ("qt", 1), ("s", 0, 0), ("s", 0, 1), ("qb", 0, 0), ("qb", 0, 1)]
    for h in range(BH):
        if h + 1 < BH:
            fox += [("s", h + 1, 0), ("s", h + 1, 1)]
        if h + 1 < SMP:
            fox += [("qb", h + 1, 0), ("qb", h + 1, 1)]
        elif h == SMP:
            fox += [("lf", 0), ("lown", 0)]
        elif h == SMP + 1:
            fox += [("sct", 0)]
        elif h == SMP + 2:
            fox += [("pdt", 0)]
        fox += [("pt", h)]
    fox += [("u", n, k) for n in range(SMP) for k in range(2)]
    last = [("stat", 5), ("stat", 6)]
    count, plan = [0] * 7, {}
    for part, ring in ((first, 3), (gla, 7), (middle, 3)):
        for i, k in enumerate(part):
            plan[k] = (i % ring, count[i % ring])
            count[i % ring] += 1
    side = 0
    for k in fox + last:
        if k[0] == "s":
            b = k[2]
        elif k[0] == "pt":
            b = 2
        elif k[0] == "stat":
            b = 0
        else:
            b, side = 3 + side % 2, side + 1
        plan[k] = (b, count[b])
        count[b] += 1
    return plan


def build(nc, x_all, up_w, down_w, mix_w, small, level_masks, state_in, cache_k, cache_v, cache_f, table,
          y_out, k_out, v_out, lf_out, state_prompt, state_sample):
    f32, f32r = mybir.dt.float32, mybir.dt.float32r
    i32, bf16 = mybir.dt.int32, mybir.dt.bfloat16
    ALU, ACT = mybir.AluOpType, mybir.ActivationFunctionType
    AX = mybir.AxisListType
    PLAN = misc_plan()
    n_phys = cache_k.shape[0]

    ctx = ExitStack()
    with ctx:
        def sb(name, shape, dt=f32, where=ctx):
            return where.enter_context(nc.sbuf_tensor(name, shape, dt))

        def sem(name):
            return ctx.enter_context(nc.semaphore(name))

        raw = [sb(f"raw{s}", [P, DNW]) for s in range(SLOTS)]
        w_hi = [sb(f"w_hi{s}", [P, DNW], f32r) for s in range(SLOTS)]
        w_lo = [sb(f"w_lo{s}", [P, DNW], f32r) for s in range(SLOTS)]
        X = sb("X", [P, KB, TOK])
        XG = sb("XG", [P, KB, TOK])
        XH = sb("XH", [P, KB, TOK], f32r)
        XL = sb("XL", [P, KB, TOK], f32r)
        RS = sb("RS", [P, TOK])
        SQ = sb("SQ", [P, 1, TOK])
        rs_tmp = SQ[:, 0, :]
        SS = sb("SS", [P, TOK])
        const = sb("const", [P, NCOL])
        tab = sb("tab", [1, SMP * NPG], i32)
        Vs = sb("Vs", [SMP, D])
        ones = sb("ones", [P, PRM])
        LG = sb("LG", [BH, TOK])
        CC = sb("CC", [BH, PRM])

        CB = sb("CB", [3 * 32, PRM], bf16)
        pick = sb("pick", [3 * 32, BH], bf16)
        ident_b = sb("ident_b", [P, P], bf16)
        tri_b = sb("tri_b", [P, P], bf16)

        def part(name):
            return const[:, COL[name][0]:COL[name][1]]
        ident = part("ident")
        gain = part("gain")
        wa = part("wa").rearrange("p (k r) -> p k r", k=KB)
        wf = part("wf").rearrange("p (k r) -> p k r", k=KB)

        inner = ctx.enter_context(ExitStack())
        KVf = sb("KVf", [P, 2 * KB, TOK], f32, inner)
        Vtok = sb("Vtok", [P, 3, D], f32, inner)
        Kf, Vf = KVf[:, 0:KB, :], KVf[:, KB:2 * KB, :]

        with ExitStack() as s:
            HH = sb("HH", [P, FB, TOK], f32r, s)
            HL = sb("HL", [P, FB, TOK], f32r, s)
            g_s = sb("g_s", [P, 2, TOK], f32, s)
            sil = sb("sil", [P, 2, TOK], f32, s)
            u_s = sb("u_s", [P, 2, TOK], f32, s)
            h_s = sb("h_s", [P, 2, TOK], f32, s)
        with ExitStack() as s:
            QKVR = sb("QKVR", [P, 24, TOK], f32, s)
            BB = sb("BB", [P, AH, TOK], f32, s)
            EE = sb("EE", [P, AH, TOK], f32, s)
            M1 = sb("M1", [P, AH, TOK], f32, s)
            ST = sb("ST", [P, AH * (PRM + 144)], f32, s)
            ST2 = sb("ST2", [META, AH, META], f32, s)
            ela = sb("ela", [P, AH, SMP], f32, s)
            a_s = sb("a_s", [RANK, TOK], f32, s)
        ST0 = ST[:, 0:AH * PRM].rearrange("p (h t) -> p h t", h=AH)
        ST1 = ST[:, AH * PRM:].rearrange("p (h t) -> p h t", h=AH)
        Q, K, V, R = (QKVR[:, 0:4, :], QKVR[:, 4:8, :], QKVR[:, 8:16, :], QKVR[:, 16:24, :])
        KE = V.rearrange("p a t -> p (a t)")[:, 0:3 * AH * P].rearrange("p (i n) -> p i n", i=3)
        SPS = M1[:, :, 0:DV]
        spare = KVf[:, :, :].rearrange("p k t -> p (k t)")
        S0 = spare[:, 0:GSLOTS * AH * DV].rearrange("p (i h v) -> p i h v", i=GSLOTS, h=AH)
        masks = spare[:, 3584:3584 + len(LEVELS) * P].rearrange("p (l t) -> p l t", l=len(LEVELS))
        EEs, M1s = (EE, XG[:, 4:8, :]), (M1, XG[:, 0:4, :])
        O = XG
        flat = lambda t: t[:, :, :].rearrange("p k t -> p (k t)")
        V3, K3 = flat(XH)[0:96, 0:AH * DV], flat(XH)[0:96, AH * DV:AH * DV + AH * P]
        KM = flat(XL)[0:96, 0:2 * AH * P].rearrange("p (i n) -> p i n", i=2)
        OSQ = QKVR[:, 0:KB, :]
        RH = BB
        with ExitStack() as s:
            Qf = sb("Qf", [P, KB, TOK], f32, s)
            PP = sb("PP", [P, 2, P + 2 * P + PRM], f32, s)
            PTH = sb("PTH", [P, 2, PRM + 144 + META], f32r, s)
            PTL = sb("PTL", [P, 2, PRM + 144 + META], f32r, s)
            VH = sb("VH", [P, 3, D], f32r, s)
            NM = sb("NM", [P, 2, 3], f32, s)
            MX = sb("MX", [P, 2, 3], f32, s)
            RW = sb("RW", [P, 2, 3], f32, s)
            QB = sb("QB", [P, KB, SMP, 2], f32, s)
            PG = [sb(f"PG{i}", [P, D], f32, s) for i in range(PAGES)]
            LFp = sb("LFp", [P, NPG, SMP, BH], f32, s)
            SC = sb("SC", [P, NPG, SMP, BH], f32, s)
            SO = sb("SO", [SMP, P], f32, s)
            LD = sb("LD", [P, 2 * P + 1], f32, s)
            SD = sb("SD", [P, 2 * P + 1], f32, s)
            PD = sb("PD", [P, 2 * P + 1], f32, s)
            own_t = sb("own_t", [P, 2, SMP], f32, s)
            PM = sb("PM", [P, SMP], f32, s)
            col = sb("col", [P, 4], f32, s)
            PMT = sb("PMT", [SMP, P], f32, s)
        inner.close()
        with ExitStack() as s:
            KVr = sb("KVr", [P, 2 * KB, TOK], f32r, s)
            VL = sb("VL", [P, 3, D], f32r, s)
        KL, KH = KVr[:, 0:KB, 0:PRM], KVr[:, KB:2 * KB, 0:PRM]
        QH, QL = XH, XL
        Q3, sel_r = w_hi[2][0:64, 0:D], w_lo[3][0:64, D + 2 * P:D + 2 * P + SMP]
        VpH, VpL = (w_hi[2], w_hi[3]), (w_lo[2], w_lo[3])
        PDT = [t[:, D:D + 2 * P].rearrange("p (n x h) -> p n x h", n=SMP, x=2) for t in (w_hi[3], w_lo[3])]
        QS = [Qf[:, :, :].rearrange("p k t -> p (k t)")[:, i * D:(i + 1) * D] for i in range(2)]
        UM = Qf[:, :, :].rearrange("p k t -> p (k t)")[:, 0:2 * D].rearrange("p (g c) -> p g c", g=2)
        CD = PD
        lt = Qf[0:BH, 0:3, :]
        C8, part_f = PP[0:BH, 0, 0:PRM], PP[0:BH, 1, 0:PRM]

        bank = [ctx.enter_context(nc.psum_tensor(f"bank{i}", [P, 512], f32)) for i in range(4)]
        misc = [ctx.enter_context(nc.psum_tensor(f"misc{i}", [P, 512], f32)) for i in range(3)] + bank
        held = ctx.enter_context(nc.psum_tensor("held", [P, 512], f32))

        raw_in = [sem(f"raw_in{s}") for s in range(SLOTS)]
        x_in, gain_in, const_in, small_in = (sem(n) for n in (
            "x_in", "gain_in", "const_in", "small_in"))
        masks_in, tab_in = sem("masks_in"), sem("tab_in")
        s_in = [sem(f"s_in{i}") for i in range(GSLOTS)]
        s_out = [sem(f"s_out{i}") for i in range(GSLOTS)]
        sp_out, kvout, lf_done, y_done = (sem(n) for n in (
            "sp_out", "kvout", "lf_done", "y_done"))
        page_in = [sem(f"page_in{i}") for i in range(PAGES)]
        lfp_in = sem("lfp_in")
        hi_ready, lo_ready = sem("hi_ready"), sem("lo_ready")
        chunk_used = sem("chunk_used")
        bank_free = sem("bank_free")
        misc_full = [sem(f"misc_full{i}") for i in range(7)]
        misc_free = [sem(f"misc_free{i}") for i in range(7)]
        pool_step, dve_step, act_step = sem("pool_step"), sem("dve_step"), sem("act_step")
        x_new = sem("x_new")
        xsq_ready = sem("xsq_ready")
        ss_ready, rs_sq, rs_ready = (sem(n) for n in (
            "ss_ready", "rs_sq", "rs_ready"))
        xg_ready, xh_ready, xl_ready = (sem(n) for n in (
            "xg_ready", "xh_ready", "xl_ready"))
        g_ready, sil_ready, h_ready, hh_ready, hid_ready = (sem(n) for n in (
            "g_ready", "sil_ready", "h_ready", "hh_ready", "hid_ready"))
        l_ready, b_ready, ela_ready, ones_ready = (sem(n) for n in (
            "l_ready", "b_ready", "ela_ready", "ones_ready"))
        d_ready, e_ready, m_ready = sem("d_ready"), sem("e_ready"), sem("m_ready")
        zero3, hi3, km_ready, s_used = (sem(n) for n in ("zero3", "hi3", "km_ready", "s_used"))
        o_ready, osq_ready, sr_ready, rh_in, rh_out = (sem(n) for n in (
            "o_ready", "osq_ready", "sr_ready", "rh_in", "rh_out"))
        of_ready, oh_ready, ol_ready = sem("of_ready"), sem("oh_ready"), sem("ol_ready")
        lf_in, lf_ready, qb_zero, qb_ready = (sem(n) for n in ("lf_in", "lf_ready", "qb_zero", "qb_ready"))
        kh_ready, kl_ready, qh_ready, ql_ready, vh_ready, vl_ready = (sem(n) for n in (
            "kh_ready", "kl_ready", "qh_ready", "ql_ready", "vh_ready", "vl_ready"))
        nm_ready, rw_ready, pn_ready, pth_ready, fo_done, po_read = (sem(n) for n in (
            "nm_ready", "rw_ready", "pn_ready", "pth_ready", "fo_done", "po_read"))
        q3_zero, q3h_ready, sel_ready, kp_ready, k_used, own_done = (sem(n) for n in (
            "q3_zero", "q3h_ready", "sel_ready", "kp_ready", "k_used", "own_done"))
        sc_ready, sd_ready, pd_ready, pe_ready, pdh_ready = (sem(n) for n in (
            "sc_ready", "sd_ready", "pd_ready", "pe_ready", "pdh_ready"))
        vph_ready, vpl_ready, pv_done, uo_done = (sem(n) for n in ("vph_ready", "vpl_ready", "pv_done", "uo_done"))
        y_ready = sem("y_ready")

        block = ctx.enter_context(nc.Block())

        def full(eng, key):
            b, n = PLAN[key]
            eng.wait_ge(misc_full[b], n + 1)
            return misc[b]

        def freed(ins, key):
            ins.then_inc(misc_free[PLAN[key][0]], 1)

        def taken(eng, key):
            b, n = PLAN[key]
            eng.wait_ge(misc_free[b], n + 1)

        def page_used(eng, i):
            if i % NPG:
                full(eng, ("u", i // NPG, 1))
            else:
                eng.wait_ge(pv_done, i // NPG + 1)

        def in_pairs(eng, seg, split, use, norm=None):
            n = COUNT[seg] // 2
            half = (n - 2) // 2
            split(seg, 0, 1)
            if norm:
                norm()
            with eng.Fori(0, half) as i:
                use(i * 2, i, 0)
                split(seg, i + 1, 0)
                use(i * 2 + 1, i, 1)
                split(seg, i + 1, 1)
            use(n - 2, half, 0)
            if NEXT[seg]:
                split(NEXT[seg], 0, 0)
            use(n - 1, half, 1)

        levels = LEVELS + [128, 256]

        def sides(l):
            if l == 256:
                return lambda t: t[:, :, 0:256], lambda t: t[:, :, 256:PRM], BB[:, :, 255:256]
            n = (PRM if l <= 8 else 256) // (2 * l)
            view = lambda t: t[:, :, 0:2 * l * n].rearrange("p h (n l) -> p h n l", l=2 * l)
            return lambda t: view(t)[:, :, :, 0:l], lambda t: view(t)[:, :, :, l:2 * l], view(BB)[:, :, :, l - 1:l]

        def exponents(eng, ns, j):
            e = EEs[j % 2]
            if j >= 2:
                eng.wait_ge(m_ready, j - 1)
            if j == len(levels):
                ns.tensor_tensor(e[:, :, 0:PRM], BB[:, :, PRM - 1:PRM].to_broadcast([P, AH, PRM]), BB[:, :, 0:PRM],
                                 ALU.subtract).then_inc(d_ready, 1)
                return
            left, right, ref = sides(levels[j])
            ns.tensor_tensor(left(e), ref.to_broadcast(list(left(e).shape)), left(BB), ALU.subtract)
            ns.tensor_tensor(right(e), right(BB), ref.to_broadcast(list(right(e).shape)),
                             ALU.subtract).then_inc(d_ready, 1)

        @block.sync
        def _(sp):
            def load_pages():
                n = SMP * NPG
                sp.wait_ge(tab_in, 16)
                sp.wait_ge(x_new, 2 + KB * 4)
                for i in range(2 * n):
                    if i >= PAGES:
                        j = i - PAGES
                        if j < n:
                            sp.wait_ge(k_used, j + 1)
                        else:
                            sp.wait_ge(vpl_ready, j - n + 1)
                    page = sp.value_load(tab[0:1, i % n:i % n + 1], min_val=0, max_val=n_phys - 1)
                    if i < n:
                        sp.dma_start(LFp[:, i % NPG, i // NPG, :], cache_f[page]).then_inc(lfp_in, 16)
                    sp.dma_start(PG[i % PAGES][:, :], (cache_k if i < n else cache_v)[page]).then_inc(page_in[i % PAGES], 16)

            sp.dma_start(gain, small[:, COL["gain"][0]:COL["gain"][1]]).then_inc(gain_in, 16)
            sp.dma_start(X[:, :, :], x_all.rearrange("k p t -> p k t")).then_inc(x_in, 16)
            for s in range(2):
                sp.dma_start(raw[s][:, 0:UPW], up_w[s]).then_inc(raw_in[s], 16)
            sp.dma_start(const[:, 0:COL["gain"][0]], small[:, 0:COL["gain"][0]]).then_inc(const_in, 16)
            for s in range(2, SLOTS):
                sp.dma_start(raw[s][:, 0:UPW], up_w[s]).then_inc(raw_in[s], 16)
            sp.dma_start(const[:, COL["gain"][1]:], small[:, COL["gain"][1]:]).then_inc(small_in, 16)
            for seg, n, tiles in SEGS:
                if tiles == DNT:
                    src, first = down_w, int(seg[3]) * 2 * KB
                elif seg.endswith("_up"):
                    src, first = up_w, int(seg[3]) * 2 * FB
                else:
                    src, first = mix_w, MIX0[seg]
                skip = SLOTS if CHUNK0[seg] == 0 else 0
                if seg == "fox_out":
                    skip = SLOTS
                    for s in range(SLOTS):
                        sp.wait_ge(lo_ready, CHUNK0[seg] + s + 1 - SLOTS)
                        sp.dma_start(raw[s][:, 0:UPW], src[first + s]).then_inc(raw_in[s], 16)
                    load_pages()
                with sp.Fori(0, (n - skip) // SLOTS) as i:
                    for s in range(SLOTS):
                        sp.wait_ge(lo_ready, i * SLOTS + (CHUNK0[seg] + skip + s + 1 - SLOTS))
                        sp.dma_start(raw[s][:, 0:tiles * P],
                                     src[i * SLOTS + (first + skip + s)]).then_inc(raw_in[s], 16)
            for m in range(0, KB, 2):
                sp.wait_ge(y_ready, m + 2)
                sp.dma_start(y_out[m:m + 2].rearrange("k p t -> p k t"), XG[:, m:m + 2, :]).then_inc(y_done, 16)
            sp.wait_ge(y_done, 16 * KB // 2)

        @block.gpsimd
        def _(pool):
            steps = [0]

            def step(ins):
                steps[0] += 1
                ins.then_inc(pool_step, 1)
                pool.wait_ge(pool_step, steps[0])

            pool.dma_start(tab[:, :], table).then_inc(tab_in, 16)
            nc.gpsimd.memset(ones[:, :], 1.0).then_inc(ones_ready, 1)
            pool.wait_ge(small_in, 16)
            pool.dma_start(masks, level_masks).then_inc(masks_in, 16)

            def square_sum(stage):
                for m in range(KB):
                    pool.wait_ge(x_new, KB * (stage - 1) + m + 3)
                    if m == 0:
                        step(nc.gpsimd.tensor_tensor(SS[:, :], X[:, 0, :], X[:, 0, :], ALU.mult))
                        continue
                    step(nc.gpsimd.tensor_tensor(SQ[:, 0, :], X[:, m, :], X[:, m, :], ALU.mult))
                    steps[0] += 1
                    nc.gpsimd.tensor_tensor(SS[:, :], SS[:, :], SQ[:, 0, :], ALU.add).then_inc(pool_step, 1)
                    pool.wait_ge(pool_step, steps[0])
                pool.sem_inc(ss_ready, 1)

            square_sum(1)

            def load_state(n):
                i = n % GSLOTS
                if n == GSLOTS - 1:
                    taken(pool, ("lv", LEVELS[-1], 1))
                if n >= GSLOTS:
                    pool.wait_ge(s_used, n - GSLOTS + 1)
                    pool.wait_ge(s_out[i], 16 * (n // GSLOTS))
                pool.dma_start(S0[:, i, :, :], state_in[n].rearrange("h d v -> d h v")).then_inc(s_in[i], 16)

            def store_state(n):
                taken(pool, ("kv", n, 1))
                pool.dma_start(state_sample[n].rearrange("h d v -> d h v"),
                               S0[:, n % GSLOTS, :, :]).then_inc(s_out[n % GSLOTS], 16)

            for n in range(GSLOTS - 1):
                load_state(n)
            pool.wait_ge(bank_free, SLOTS + UNIT0["gla_r"] + 8)
            nc.gpsimd.memset(flat(XH)[0:96, 0:AH * (DV + P)].bitcast(f32), 0.0).then_inc(zero3, 1)
            for j in range(2, len(levels) + 1):
                exponents(pool, nc.gpsimd, j)
            load_state(GSLOTS - 1)
            for n in range(SMP):
                store_state(n)
                if 1 <= n and n - 1 + GSLOTS < SMP:
                    load_state(n - 1 + GSLOTS)
            taken(pool, ("sp", 1))
            pool.dma_start(state_prompt.rearrange("h d v -> d h v"), SPS).then_inc(sp_out, 16)
            square_sum(2)
            square_sum(3)

            pool.wait_ge(bank_free, SLOTS + UNIT0["kv_in"] + 16)
            pool.dma_start(k_out.rearrange("k p t -> p k t"), Kf[:, :, :]).then_inc(kvout, 16)
            pool.dma_start(v_out.rearrange("k p t -> p k t"), Vf[:, :, :]).then_inc(kvout, 16)
            pool.wait_ge(lf_ready, 1)
            pool.dma_start(lf_out, LG[:, :]).then_inc(lf_done, 16)
            square_sum(4)

            step(nc.gpsimd.memset(QB[:, :, :, :], 0.0))
            step(nc.gpsimd.memset(NM[:, :, :], 0.0))
            step(nc.gpsimd.memset(MX[:, :, :], 0.0))
            step(nc.gpsimd.memset(RW[:, :, :], 1.0))
            pool.sem_inc(qb_zero, 1)
            pool.wait_ge(bank_free, SLOTS + UNIT0["fox_q"] + KB)
            nc.gpsimd.memset(Q3.bitcast(f32), 0.0).then_inc(q3_zero, 1)
            for n in range(SMP):
                i = NPG * n + 1
                pool.wait_ge(page_in[i % PAGES], 16 * (i // PAGES + 1))
                taken(pool, ("qb", n, 1))
                nc.gpsimd.tensor_tensor(PG[i % PAGES][:, :], PG[i % PAGES][:, :], QS[n % 2], ALU.mult).then_inc(kp_ready, 1)
            square_sum(5)
            square_sum(6)
            for i in range(GSLOTS):
                pool.wait_ge(s_out[i], 16 * SMP // GSLOTS)
            pool.wait_ge(sp_out, 16)
            pool.wait_ge(kvout, 32)
            pool.wait_ge(lf_done, 16)

        @block.scalar
        def _(act):
            steps = [0]

            def step(ins):
                steps[0] += 1
                ins.then_inc(act_step, 1)
                act.wait_ge(act_step, steps[0])

            def split(seg, half, par):
                w = TILES[seg] * P
                for k in range(2):
                    s = 2 * par + k
                    c = half * 4 + (CHUNK0[seg] + s)
                    act.wait_ge(raw_in[s], half * 16 + 16 * (CHUNK0[seg] // 4 + 1))
                    act.wait_ge(chunk_used, c + 1)
                    nc.scalar.copy(w_hi[s][:, 0:w], raw[s][:, 0:w]).then_inc(hi_ready, 1)

            def norm_root(n):
                act.wait_ge(rs_sq, n + 1)
                nc.scalar.activation(RS[:, :], rs_tmp[:, :], ACT.Sqrt).then_inc(rs_ready, 1)

            def prep(name, m):
                n = m + KB * GAIN[name]
                act.wait_ge(xg_ready, n + 1)
                nc.scalar.copy(XH[:, bass.ds(m, 1), :].rearrange("p a t -> p (a t)"),
                                     XG[:, bass.ds(m, 1), :].rearrange("p a t -> p (a t)")).then_inc(xh_ready, 1)

            def ffn(n, norm, then=None):
                f0 = n * FB

                def hidden(f, half, par):
                    act.wait_ge(g_ready, f + (f0 + 1))
                    nc.scalar.activation(sil[:, par, :], g_s[:, par, :], ACT.Silu).then_inc(sil_ready, 1)
                    act.wait_ge(h_ready, f + (f0 + 1))
                    nc.scalar.copy(HH[:, bass.ds(f, 1), :].rearrange("p a t -> p (a t)"),
                                         h_s[:, par, :]).then_inc(hh_ready, 1)

                in_pairs(act, f"ffn{n}_up", split, hidden, norm)
                after = GAINS[GAIN[f"ffn{n}"] + 1]
                in_pairs(act, f"ffn{n}_down", split,
                         lambda m, half, par: prep(after, m) if after != "final" else None, then)

            act.wait_ge(x_in, 16)
            for m in range(KB):
                prep("ffn0", m)
            split("ffn0_up", 0, 0)
            nc.scalar.activation(OSQ, X[:, :, :], ACT.Square).then_inc(xsq_ready, 1)
            ffn(0, lambda: norm_root(0))

            in_pairs(act, "gla_qk", split, lambda g, half, par: None, lambda: norm_root(1))

            def gate():
                for h in range(AH):
                    taken(act, ("z", h))
                step(nc.scalar.activation(EE[:, :, :], M1[:, :, :], ACT.Abs))
                step(nc.scalar.activation(EE[:, :, :], EE[:, :, :], ACT.Exp, scale=-1.0))
                nc.scalar.activation(EE[:, :, :], EE[:, :, :], ACT.Ln, bias=1.0).then_inc(l_ready, 1)
                act.wait_ge(b_ready, 1)
                nc.scalar.activation(ela[:, :, :], M1[:, :, PRM:TOK], ACT.Exp, scale=1.0 / 16).then_inc(ela_ready, 1)

            def decay(j):
                act.wait_ge(d_ready, j + 1)
                e = EEs[j % 2][:, :, 0:PRM]
                nc.scalar.activation(e, e, ACT.Exp, scale=1.0 / 16).then_inc(e_ready, 1)

            in_pairs(act, "gla_v", split, lambda g, half, par: None, gate)
            in_pairs(act, "gla_r", split, lambda g, half, par: None, lambda: [decay(0), decay(1)])
            for i in range(3):
                rows = P if i < 2 else META
                for h in range(2):
                    b = full(act, ("vt", i, h))
                    freed(nc.scalar.copy(Vtok[0:rows, i, h * 512:(h + 1) * 512], b[0:rows, :]), ("vt", i, h))
            for h in range(2):
                b = full(act, ("vs", h))
                freed(nc.scalar.copy(Vs[:, h * 512:(h + 1) * 512], b[0:SMP, :]), ("vs", h))
            act.wait_ge(zero3, 1)
            taken(act, ("vs", 1))
            for at in (0, 64):
                nc.scalar.copy(V3[at:at + SMP, :], Vs[:, :])
            b = full(act, ("ks", 0))
            nc.scalar.copy(K3[0:SMP, :], b[0:SMP, :])
            nc.scalar.copy(K3[32:32 + SMP, :], b[0:SMP, :]).then_inc(hi3, 1)
            for j in range(2, len(LEVELS) + 3):
                decay(j)
            for i in range(3):
                rows = P if i < 2 else META
                b = full(act, ("ke", i))
                freed(nc.scalar.copy(KE[0:rows, i, :], b[0:rows, :]), ("ke", i))
            act.wait_ge(o_ready, 1)
            nc.scalar.activation(OSQ[:, :, 0:PRM], O[:, :, 0:PRM], ACT.Square).then_inc(osq_ready, 1)
            nc.scalar.activation(R, R, ACT.Silu).then_inc(sr_ready, 1)
            for h in range(AH):
                act.wait_ge(rh_in, h + 1)
                nc.scalar.activation(RH[:, h, 0:PRM], RH[:, h, 0:PRM], ACT.Sqrt).then_inc(rh_out, 1)
                if h == AH - 2:
                    for g in range(2):
                        b = full(act, ("sp", g))
                        freed(nc.scalar.copy(SPS[:, 2 * g:2 * g + 2, :], b[:, :].rearrange("p (h v) -> p h v", h=2)), ("sp", g))
            act.wait_ge(o_ready, 2)
            nc.scalar.activation(OSQ[:, :, PRM:TOK], O[:, :, PRM:TOK], ACT.Square).then_inc(osq_ready, 1)
            act.wait_ge(rh_in, AH + 1)
            nc.scalar.activation(RH[:, :, PRM:TOK], RH[:, :, PRM:TOK], ACT.Sqrt).then_inc(rh_out, 1)
            act.wait_ge(of_ready, 1)
            for m in range(0, KB, 2):
                nc.scalar.copy(HH[:, m:m + 2, :], XG[:, m:m + 2, :]).then_inc(oh_ready, 1)
            in_pairs(act, "gla_out", split, lambda g, half, par: [prep("ffn1", 2 * g + k) for k in range(2)])
            ffn(1, lambda: norm_root(2))

            in_pairs(act, "kv_in", split, lambda g, half, par: None, lambda: norm_root(3))
            act.wait_ge(lf_in, 1)
            step(nc.scalar.activation(lt[:, 1, :], lt[:, 0, :], ACT.Abs))
            step(nc.scalar.activation(lt[:, 1, :], lt[:, 1, :], ACT.Exp, scale=-1.0))
            nc.scalar.activation(lt[:, 1, :], lt[:, 1, :], ACT.Ln, bias=1.0).then_inc(l_ready, 1)
            for i in range(3):
                rows = P if i < 2 else META
                for h in range(2):
                    b = full(act, ("fvt", i, h))
                    freed(nc.scalar.copy(Vtok[0:rows, i, h * 512:(h + 1) * 512], b[0:rows, :]), ("fvt", i, h))
            for h in range(2):
                b = full(act, ("fvs", h))
                freed(nc.scalar.copy(Vs[:, h * 512:(h + 1) * 512], b[0:SMP, :]), ("fvs", h))
            for m in range(KB):
                prep("ffn2", m)
            act.wait_ge(lf_ready, 1)
            def keys_high():
                act.wait_ge(kvout, 32)
                nc.scalar.copy(KH, Kf[:, :, 0:PRM]).then_inc(kh_ready, 1)

            ffn(2, None, keys_high)

            def norm_and_values():
                norm_root(4)
                nc.scalar.copy(VH[:, 0:2, :], Vtok[:, 0:2, :])
                nc.scalar.copy(VH[0:META, 2, :], Vtok[0:META, 2, :]).then_inc(vh_ready, 1)

            in_pairs(act, "fox_q", split, lambda g, half, par: None, norm_and_values)

            def attend(h):
                q = h % 2
                for i, (key, rows, src, dst) in enumerate((
                        (("s", h, 0), P, slice(0, P), PP[:, q, 0:P]),
                        (("s", h, 0), P, slice(P, 3 * P), PP[:, q, P:3 * P]),
                        (("s", h, 1), META, slice(0, PRM), PP[0:META, q, 3 * P:3 * P + PRM]))):
                    if i != 1:
                        full(act, key)
                    act.wait_ge(nm_ready, 2 * h + (1 if i < 2 else 2))
                    ins = nc.scalar.activation(dst, misc[PLAN[key][0]][0:rows, src], ACT.Exp,
                                               bias=NM[0:rows, q, i:i + 1], scale=HD ** -0.5,
                                               accum_out=RW[0:rows, q, i:i + 1])
                    if i:
                        freed(ins, key)

            def probs_high(h):
                b = full(act, ("pt", h))
                nc.scalar.copy(PTH[:, h % 2, 0:PRM + 144], b[:, 0:PRM + 144])
                nc.scalar.copy(PTH[0:META, h % 2, PRM + 144:], b[0:META, PRM + 144:PRM + 144 + META]).then_inc(pth_ready, 1)

            def page_high(i):
                j = SMP * NPG + i
                act.wait_ge(page_in[j % PAGES], 16 * (j // PAGES + 1))
                if i >= 2:
                    page_used(act, i - 2)
                nc.scalar.copy(VpH[i % 2][:, 0:D], PG[j % PAGES][:, :]).then_inc(vph_ready, 1)

            def normalize(h):
                q = h % 2
                act.wait_ge(rw_ready, h + 1)
                for dst, w in ((PP[:, q, 0:P], RW[:, q, 0:1]), (PP[:, q, P:3 * P], RW[:, q, 1:2]),
                               (PP[0:META, q, 3 * P:3 * P + PRM], RW[0:META, q, 2:3])):
                    ins = nc.scalar.activation(dst, dst, ACT.Copy, scale=w)
                ins.then_inc(pn_ready, 1)

            def query_copied(n):
                if n >= 2:
                    act.wait_ge(k_used, NPG * (n - 1))
                for k in range(2):
                    b = full(act, ("qb", n, k))
                    freed(nc.scalar.copy(QS[n % 2][:, k * 512:(k + 1) * 512], b[:, :]), ("qb", n, k))

            def head_out(h):
                act.wait_ge(fo_done, h + 1)
                r = slice(HD * (h % 2), HD * (h % 2 + 1))
                nc.scalar.copy(XG[r, h // 2, 0:PRM], bank[2 + h % 2][r, 0:PRM]).then_inc(po_read, 1)

            act.wait_ge(bank_free, SLOTS + UNIT0["fox_q"] + KB)
            for m in range(0, KB, 2):
                nc.scalar.copy(QH[:, m:m + 2, :], Qf[:, m:m + 2, :]).then_inc(qh_ready, 1)
            nc.scalar.copy(sel_r, part("sel")[0:64, :]).then_inc(sel_ready, 1)
            act.wait_ge(q3_zero, 1)
            for k in range(2):
                b = full(act, ("qt", k))
                nc.scalar.copy(Q3[0:SMP, k * 512:(k + 1) * 512], b[0:SMP, :]).then_inc(q3h_ready, 1)
            attend(0)
            act.wait_ge(ql_ready, KB // 2)
            act.wait_ge(qb_ready, 3)
            query_copied(0)
            for h in range(BH):
                if h:
                    probs_high(h - 1)
                normalize(h)
                if h + 1 < BH:
                    attend(h + 1)
                if h + 1 < SMP:
                    query_copied(h + 1)
                if h >= 2:
                    head_out(h - 2)
                if h == SMP + 1:
                    act.wait_ge(sd_ready, 1)
                    nc.scalar.activation(PD[:, :], SD[:, :], ACT.Exp, bias=col[:, 0:1], accum_out=col[:, 1:2]).then_inc(pd_ready, 1)
                if h == SMP + 2:
                    b = full(act, ("pdt", 0))
                    for g in range(NPG):
                        nc.scalar.copy(PDT[g][:, :, 0, :], b[:, g * P:(g + 1) * P].rearrange(
                            "p (n h) -> p n h", n=SMP)).then_inc(pdh_ready, 1)
                if h >= VALUES:
                    page_high(2 * (h - VALUES))
                    page_high(2 * (h - VALUES) + 1)
            probs_high(BH - 1)
            for i in range(NPG * (BH - VALUES), NPG * SMP):
                page_high(i)
                if i == NPG * (BH - VALUES) + 1:
                    head_out(BH - 2)
                    head_out(BH - 1)
            act.wait_ge(po_read, BH)
            act.wait_ge(of_ready, 2)
            for m in range(0, KB, 2):
                nc.scalar.copy(HH[:, m:m + 2, :], XG[:, m:m + 2, :]).then_inc(oh_ready, 1)
            in_pairs(act, "fox_out", split, lambda g, half, par: [prep("ffn3", 2 * g + k) for k in range(2)])
            ffn(3, lambda: norm_root(5))
            norm_root(6)

        @block.vector
        def _(dve):
            steps = [0]

            def step(ins):
                steps[0] += 1
                ins.then_inc(dve_step, 1)
                dve.wait_ge(dve_step, steps[0])

            def split(seg, half, par):
                w = TILES[seg] * P
                for k in range(2):
                    s = 2 * par + k
                    c = half * 4 + (CHUNK0[seg] + s)
                    dve.wait_ge(hi_ready, c + 1)
                    nc.vector.tensor_tensor(w_lo[s][:, 0:w], raw[s][:, 0:w],
                                            w_hi[s][:, 0:w].bitcast(f32), ALU.subtract).then_inc(lo_ready, 1)

            def block_of(t, m):
                return t[:, bass.ds(m, 1), :].rearrange("p a t -> p (a t)")

            def norm_square(n):
                b = full(dve, ("stat", n))
                ins = nc.vector.tensor_scalar(rs_tmp[:, :], b[:, 0:TOK], EPS, None, ALU.add)
                freed(ins, ("stat", n))
                dve.wait_ge(misc_free[PLAN[("stat", n)][0]], PLAN[("stat", n)][1] + 1)
                nc.vector.reciprocal(rs_tmp[:, :], rs_tmp[:, :]).then_inc(rs_sq, 1)

            def prep(name, m):
                n = m + KB * GAIN[name]
                nc.vector.tensor_scalar(block_of(XG, m), block_of(X, m), gain[:, bass.ds(n, 1)], None,
                                        ALU.mult).then_inc(xg_ready, 1)
                dve.wait_ge(xh_ready, n + 1)
                nc.vector.tensor_tensor(block_of(XL, m), block_of(XG, m), block_of(XH, m).bitcast(f32),
                                        ALU.subtract).then_inc(xl_ready, 1)

            def highs(name):
                n = KB * GAIN[name]
                for m in range(KB):
                    nc.vector.tensor_scalar(XG[:, m, :], X[:, m, :], gain[:, n + m:n + m + 1], None,
                                            ALU.mult).then_inc(xg_ready, 1)

            def lows(name):
                n = KB * GAIN[name]
                for m in range(KB):
                    dve.wait_ge(xh_ready, n + m + 1)
                    nc.vector.tensor_tensor(XL[:, m, :], XG[:, m, :], XH[:, m, :].bitcast(f32),
                                            ALU.subtract).then_inc(xl_ready, 1)

            def residual(seg, stage, scale, after, m, b):
                per = 1 if TILES[seg] == KB else 2
                dve.wait_ge(chunk_used, m * per + (SLOTS + CHUNK0[seg] + per))
                ins = nc.vector.scalar_tensor_tensor(block_of(X, m), bank[b][:, 0:TOK], scale, block_of(X, m),
                                                     ALU.mult, ALU.add)
                ins.then_inc(x_new, 1)
                dve.wait_ge(x_new, m + (KB * (stage - 1) + 3))
                if after != "final":
                    prep(after, m)

            def scaled(seg, dst):
                def use(g, half, par):
                    for k in range(2):
                        dve.wait_ge(chunk_used, g * 2 + (SLOTS + CHUNK0[seg] + k + 1))
                        nc.vector.tensor_tensor(block_of(dst, g * 2 + k), bank[2 * par + k][:, 0:TOK], RS[:, :],
                                                ALU.mult).then_inc(bank_free, 1)
                return use

            def norm(n):
                norm_square(n)
                dve.wait_ge(rs_ready, n + 1)

            def ffn(n, after, stage, norm=None, then=None):
                f0, seg = n * FB, f"ffn{n}_up"

                def hidden(f, half, par):
                    u = f * 2 + UNIT0[seg]
                    c = f * 2 + (SLOTS + CHUNK0[seg])
                    dve.wait_ge(chunk_used, c + 1)
                    nc.vector.tensor_tensor(g_s[:, par, :], bank[2 * par][:, 0:TOK], RS[:, :], ALU.mult).then_inc(g_ready, 1)
                    dve.wait_ge(chunk_used, c + 2)
                    nc.vector.tensor_tensor(u_s[:, par, :], bank[2 * par + 1][:, 0:TOK], RS[:, :],
                                            ALU.mult).then_inc(bank_free, 2)
                    dve.wait_ge(bank_free, u + (SLOTS + 2))
                    dve.wait_ge(sil_ready, f + (f0 + 1))
                    nc.vector.tensor_tensor(h_s[:, par, :], sil[:, par, :], u_s[:, par, :], ALU.mult).then_inc(h_ready, 1)
                    dve.wait_ge(hh_ready, f + (f0 + 1))
                    nc.vector.tensor_tensor(block_of(HL, f), h_s[:, par, :], block_of(HH, f).bitcast(f32),
                                            ALU.subtract).then_inc(hid_ready, 1)

                in_pairs(dve, seg, split, hidden, norm)
                in_pairs(dve, f"ffn{n}_down", split,
                         lambda m, half, par: residual(f"ffn{n}_down", stage, 0.5, after, m, par), then)

            dve.sem_inc(bank_free, SLOTS)
            dve.sem_inc(x_new, 2)
            dve.wait_ge(x_in, 16)
            dve.wait_ge(gain_in, 16)
            highs("ffn0")
            lows("ffn0")
            split("ffn0_up", 0, 0)
            dve.wait_ge(xsq_ready, 1)
            for m in (4, 2):
                step(nc.vector.tensor_tensor(OSQ[:, 0:m, :], OSQ[:, 0:m, :], OSQ[:, m:2 * m, :], ALU.add))
            nc.vector.tensor_tensor(SS[:, :], OSQ[:, 0, :], OSQ[:, 1, :], ALU.add).then_inc(ss_ready, 1)
            ffn(0, "gla", 1, lambda: norm(0))

            dve.wait_ge(const_in, 16)
            dve.wait_ge(small_in, 16)
            in_pairs(dve, "gla_qk", split, scaled("gla_qk", QKVR), lambda: norm(1))
            b = full(dve, ("a", 0))
            freed(nc.vector.tensor_tensor(a_s[:, :], b[0:RANK, 0:TOK], RS[0:RANK, :], ALU.mult), ("a", 0))

            def gate():
                for h in range(AH):
                    b = full(dve, ("z", h))
                    freed(nc.vector.tensor_scalar(M1[:, h, :], b[:, 0:TOK], part("balpha")[:, h:h + 1], None, ALU.add), ("z", h))
                dve.wait_ge(l_ready, 1)
                step(nc.vector.tensor_scalar(M1[:, :, :], M1[:, :, :], 0.0, None, ALU.min))
                step(nc.vector.tensor_tensor(M1[:, :, :], M1[:, :, :], EE[:, :, :], ALU.subtract))
                dve.wait_ge(ones_ready, 1)
                for h in range(AH):
                    step(nc.vector.tensor_tensor_scan(BB[:, h, 0:PRM], ones[:, :], M1[:, h, 0:PRM], 0.0, ALU.mult, ALU.add))
                dve.sem_inc(b_ready, 1)

            def decayed(j):
                e, m = EEs[j % 2], M1s[j % 2]
                dve.wait_ge(e_ready, j + 1)
                if j == len(levels):
                    nc.vector.tensor_tensor(m[:, :, 0:PRM], e[:, :, 0:PRM], K[:, :, 0:PRM], ALU.mult).then_inc(m_ready, 1)
                    return
                left, right, _ = sides(levels[j])
                nc.vector.tensor_tensor(left(m), left(e), left(K), ALU.mult)
                nc.vector.tensor_tensor(right(m), right(e), right(Q), ALU.mult).then_inc(m_ready, 1)

            def level_scores(j):
                l = levels[j]
                heads_of = lambda b, lo, hi: b[:, lo:hi].rearrange("p (h t) -> p h t", h=AH)
                if l < 128:
                    for i, S in enumerate((ST0, ST1, ST2)[0:3 if l <= 8 else 2]):
                        b = full(dve, ("lv", l, i))
                        r = META if i == 2 else P
                        taken(dve, ("lv", ([0] + LEVELS)[j], i))
                        freed(nc.vector.copy_predicated(
                            S[:, :, 0:r], masks[0:r, j, 0:r].bitcast(i32).unsqueeze(1).to_broadcast([r, AH, r]),
                            b[0:r, 0:AH * r].rearrange("p (h t) -> p h t", h=AH)), ("lv", l, i))
                elif l == 128:
                    b = full(dve, ("lv", 128, 0))
                    freed(nc.vector.tensor_copy(ST0[:, :, P:256], heads_of(b, 0, AH * P)), ("lv", 128, 0))
                else:
                    b = full(dve, ("lv", 256, 0))
                    nc.vector.tensor_copy(ST0[:, :, 256:PRM], heads_of(b, 0, 64))
                    freed(nc.vector.tensor_copy(ST1[:, :, P:144], heads_of(b, 64, 128)), ("lv", 256, 0))

            def first_levels():
                exponents(dve, nc.vector, 0)
                exponents(dve, nc.vector, 1)
                decayed(0)
                decayed(1)

            in_pairs(dve, "gla_v", split, scaled("gla_v", V), gate)
            in_pairs(dve, "gla_r", split, scaled("gla_r", R), first_levels)

            b = full(dve, ("lv", 0, 0))
            freed(nc.vector.tensor_tensor(ST0[:, :, 0:P], b[:, :].rearrange("p (h t) -> p h t", h=AH),
                                          ident.unsqueeze(1).to_broadcast([P, AH, P]), ALU.mult), ("lv", 0, 0))
            b = full(dve, ("lv", 0, 1))
            freed(nc.vector.tensor_tensor(ST1[:, :, 0:P], b[:, :].rearrange("p (h t) -> p h t", h=AH),
                                          ident.unsqueeze(1).to_broadcast([P, AH, P]), ALU.mult), ("lv", 0, 1))
            b = full(dve, ("lv", 0, 2))
            freed(nc.vector.tensor_tensor(ST2[:, :, :], b[0:META, 0:AH * META].rearrange("p (h t) -> p h t", h=AH),
                                          ident[0:META, 0:META].unsqueeze(1).to_broadcast([META, AH, META]),
                                          ALU.mult), ("lv", 0, 2))
            dve.wait_ge(masks_in, 16)
            level_scores(0)
            dve.wait_ge(hi3, 1)
            nc.vector.tensor_tensor(V3[32:32 + SMP, :], Vs[:, :], V3[0:SMP, :].bitcast(f32), ALU.subtract)
            b = full(dve, ("ks", 0))
            freed(nc.vector.tensor_tensor(K3[64:64 + SMP, :], b[0:SMP, :], K3[0:SMP, :].bitcast(f32), ALU.subtract), ("ks", 0))
            for j in range(2, len(levels) + 1):
                decayed(j)
                level_scores(j - 1)
            heads = lambda t: t.rearrange("p (h j) t -> p h j t", j=2)

            def mask_key(n):
                if n >= 2:
                    full(dve, ("kv", n - 2, 1))
                nc.vector.tensor_scalar(KM[:, n % 2, :], K3[:, :].bitcast(f32), part("sel")[0:96, n:n + 1], None,
                                        ALU.mult).then_inc(km_ready, 1)

            def head_mean(h):
                b = full(dve, ("hn", h))
                freed(nc.vector.tensor_scalar(RH[:, h, 0:PRM], b[:, 0:PRM], EPS, None, ALU.add), ("hn", h))
                taken(dve, ("hn", h))
                nc.vector.reciprocal(RH[:, h, 0:PRM], RH[:, h, 0:PRM]).then_inc(rh_in, 1)

            def head_out(h):
                dve.wait_ge(rh_out, h + 1)
                for j in range(2):
                    step(nc.vector.tensor_tensor(O[:, 2 * h + j, 0:PRM], O[:, 2 * h + j, 0:PRM], RH[:, h, 0:PRM], ALU.mult))
                    nc.vector.scalar_tensor_tensor(O[:, 2 * h + j, 0:PRM], O[:, 2 * h + j, 0:PRM], part("ghead")[:, j:j + 1],
                                                   R[:, 2 * h + j, 0:PRM], ALU.mult, ALU.mult)

            dve.wait_ge(ela_ready, 1)
            taken(dve, ("ks", 0))
            mask_key(0)
            mask_key(1)
            for n in range(SMP):
                i = n % GSLOTS
                dve.wait_ge(s_in[i], 16 * (n // GSLOTS + 1))
                for g in range(2):
                    b = full(dve, ("kv", n, g))
                    for k in range(2):
                        h = 2 * g + k
                        ins = nc.vector.scalar_tensor_tensor(S0[:, i, h, :], S0[:, i, h, :], ela[:, h, n:n + 1],
                                                             b[:, k * DV:(k + 1) * DV], ALU.mult, ALU.add)
                    freed(ins, ("kv", n, g))
                if n + 2 < SMP:
                    mask_key(n + 2)
                if n < AH:
                    for o in (2 * n, 2 * n + 1):
                        b = full(dve, ("o", o))
                        freed(nc.vector.tensor_scalar(O[:, o, 0:PRM], b[:, 0:PRM], P ** -0.5, None, ALU.mult), ("o", o))
                if n == AH - 1:
                    taken(dve, ("o", KB - 1))
                    dve.sem_inc(o_ready, 1)
                if n > AH:
                    head_mean(n - AH - 1)
                if n == SMP - 2:
                    dve.wait_ge(sr_ready, 1)
                if n > AH + 1:
                    head_out(n - AH - 2)
            head_mean(AH - 1)
            head_out(AH - 2)
            dve.wait_ge(s_used, SMP)
            nc.vector.tensor_scalar(O[:, :, PRM:TOK], held[:, 0:KB * SMP].rearrange("p (b n) -> p b n", b=KB),
                                    P ** -0.5, None, ALU.mult).then_inc(o_ready, 1)
            head_out(AH - 1)
            b = full(dve, ("hns", 0))
            freed(nc.vector.tensor_scalar(RH[:, :, PRM:TOK], b[:, 0:AH * SMP].rearrange("p (h n) -> p h n", h=AH), EPS, None,
                                          ALU.add), ("hns", 0))
            taken(dve, ("hns", 0))
            nc.vector.reciprocal(RH[:, :, PRM:TOK], RH[:, :, PRM:TOK]).then_inc(rh_in, 1)
            dve.wait_ge(rh_out, AH + 1)
            for j in range(2):
                own = heads(O[:, :, PRM:TOK])[:, :, j, :]
                step(nc.vector.tensor_tensor(own, own, RH[:, :, PRM:TOK], ALU.mult))
                step(nc.vector.scalar_tensor_tensor(own, own, part("ghead")[:, j:j + 1], heads(R)[:, :, j, PRM:TOK],
                                                    ALU.mult, ALU.mult))
            dve.sem_inc(of_ready, 1)
            for m in range(0, KB, 2):
                dve.wait_ge(oh_ready, m // 2 + 1)
                nc.vector.tensor_tensor(HL[:, m:m + 2, :], XG[:, m:m + 2, :], HH[:, m:m + 2, :].bitcast(f32),
                                        ALU.subtract).then_inc(ol_ready, 1)
            in_pairs(dve, "gla_out", split, lambda g, half, par: [
                residual("gla_out", 2, 1.0, "ffn1", 2 * g + k, 2 * par + k) for k in range(2)])
            dve.wait_ge(sp_out, 16)
            ffn(1, "kv", 3, lambda: norm(2))

            for i in range(GSLOTS):
                dve.wait_ge(s_out[i], 16 * SMP // GSLOTS)
            in_pairs(dve, "kv_in", split, scaled("kv_in", KVf), lambda: norm(3))
            b = full(dve, ("f", 0))
            ins = nc.vector.tensor_tensor(lt[:, 2, :], b[0:BH, 0:TOK], RS[0:BH, :], ALU.mult)
            freed(ins, ("f", 0))
            dve.wait_ge(misc_free[PLAN[("f", 0)][0]], PLAN[("f", 0)][1] + 1)
            nc.vector.tensor_scalar(lt[:, 0, :], lt[:, 2, :], part("bf")[0:BH, :], None, ALU.add).then_inc(lf_in, 1)
            dve.wait_ge(l_ready, 2)
            step(nc.vector.tensor_scalar(lt[:, 0, :], lt[:, 0, :], 0.0, None, ALU.min))
            step(nc.vector.tensor_tensor(LG[:, :], lt[:, 0, :], lt[:, 1, :], ALU.subtract))
            nc.vector.tensor_tensor_scan(CC[:, :], ones[0:BH, :], LG[:, 0:PRM], 0.0, ALU.mult, ALU.add).then_inc(lf_ready, 1)
            highs("ffn2")
            lows("ffn2")
            def keys_low():
                dve.wait_ge(kh_ready, 1)
                nc.vector.tensor_tensor(KL, Kf[:, :, 0:PRM], KH.bitcast(f32), ALU.subtract).then_inc(kl_ready, 1)

            def forgets():
                step(nc.vector.tensor_scalar(C8[:, :], CC[:, :], -(HD ** 0.5), None, ALU.mult))
                step(nc.vector.memset(CB[:, :], 0.0))
                for k in range(3):
                    rows = CB[32 * k:32 * k + BH, :]
                    step(nc.vector.tensor_copy(rows, C8[:, :]))
                    if k < 2:
                        step(nc.vector.tensor_copy(part_f[:, :], rows))
                        step(nc.vector.tensor_tensor(C8[:, :], C8[:, :], part_f[:, :], ALU.subtract))
                nc.vector.tensor_copy(pick[:, :], part("pick")[0:96, :])
                nc.vector.tensor_copy(ident_b[:, :], ident)
                nc.vector.tensor_copy(tri_b[:, :], part("tri")).then_inc(qb_ready, 1)

            ffn(2, "fox", 4, forgets, keys_low)

            in_pairs(dve, "fox_q", split, scaled("fox_q", Qf), lambda: norm(4))
            dve.wait_ge(bank_free, SLOTS + UNIT0["fox_q"] + KB)

            def queries_low(m):
                dve.wait_ge(qh_ready, m // 2 + 1)
                nc.vector.tensor_tensor(QL[:, m:m + 2, :], Qf[:, m:m + 2, :], QH[:, m:m + 2, :].bitcast(f32),
                                        ALU.subtract).then_inc(ql_ready, 1)

            queries_low(0)
            dve.wait_ge(qb_zero, 1)
            for e in range(2):
                r = slice(HD * e, HD * (e + 1))
                nc.vector.tensor_copy(QB[r, :, :, e], Qf[r, :, PRM:TOK]).then_inc(qb_ready, 1)

            def maxima(h):
                q = h % 2
                b = full(dve, ("s", h, 0))
                if h >= 2:
                    taken(dve, ("s", h - 2, 1))
                nc.vector.reduce_max(MX[:, q, 0:1], b[:, 0:P], AX.X)
                step(nc.vector.reduce_max(MX[:, q, 1:2], b[:, P:3 * P], AX.X))
                nc.vector.tensor_scalar(NM[:, q, 0:2], MX[:, q, 0:2], -(HD ** -0.5), None, ALU.mult).then_inc(nm_ready, 1)
                b = full(dve, ("s", h, 1))
                step(nc.vector.reduce_max(MX[0:META, q, 2:3], b[0:META, 0:PRM], AX.X))
                nc.vector.tensor_scalar(NM[0:META, q, 2:3], MX[0:META, q, 2:3], -(HD ** -0.5), None,
                                        ALU.mult).then_inc(nm_ready, 1)

            def probs_low(h):
                b = misc[PLAN[("pt", h)][0]]
                dve.wait_ge(pth_ready, h + 1)
                for rows, c in ((P, slice(0, PRM + 144)), (META, slice(PRM + 144, PRM + 144 + META))):
                    ins = nc.vector.tensor_tensor(PTL[0:rows, h % 2, c], b[0:rows, c], PTH[0:rows, h % 2, c].bitcast(f32),
                                                  ALU.subtract)
                freed(ins, ("pt", h))

            def weights(h):
                taken(dve, ("s", h, 1))
                nc.vector.reciprocal(RW[:, h % 2, :], RW[:, h % 2, :]).then_inc(rw_ready, 1)

            def head_sums(i):
                nc.vector.reduce_sum(SC[:, i % NPG, i // NPG, :], PG[i % PAGES][:, :].rearrange("p (h d) -> p h d", h=BH),
                                     AX.X).then_inc(k_used, 1)

            def page_scores(n):
                i = NPG * n
                page = PG[i % PAGES][:, :]
                dve.wait_ge(page_in[i % PAGES], 16 * (i // PAGES + 1))
                taken(dve, ("qb", n, 1))
                step(nc.vector.tensor_tensor(page, page, QS[n % 2], ALU.mult))
                head_sums(i)

            def page_low(i):
                dve.wait_ge(vph_ready, i + 1)
                nc.vector.tensor_tensor(VpL[i % 2][:, 0:D], PG[(SMP * NPG + i) % PAGES][:, :], VpH[i % 2][:, 0:D].bitcast(f32),
                                        ALU.subtract).then_inc(vpl_ready, 1)

            def sampled_scores_out():
                dve.wait_ge(own_done, 1)
                dve.wait_ge(k_used, SMP * NPG)
                nc.vector.tensor_copy(SO[:, :], held[0:SMP, 2 * P:3 * P]).then_inc(sc_ready, 1)
                b = full(dve, ("lf", 0))
                freed(nc.vector.tensor_copy(LD[:, 0:2 * P], b[:, 0:2 * P]), ("lf", 0))
                b = full(dve, ("lown", 0))
                freed(nc.vector.tensor_tensor(own_t[:, 0, :], b[:, 0:SMP], part("own"), ALU.mult), ("lown", 0))
                taken(dve, ("lown", 0))
                step(nc.vector.reduce_sum(LD[:, 2 * P:2 * P + 1], own_t[:, 0, :], AX.X))
                step(nc.vector.tensor_tensor_scan(CD[:, :], ones[:, 0:2 * P + 1], LD[:, :], 0.0, ALU.mult, ALU.add))
                step(nc.vector.tensor_scalar(LD[:, :], CD[:, :], -1.0, CD[:, 2 * P:2 * P + 1], ALU.mult, ALU.add))

            def sampled_scores():
                b = full(dve, ("sct", 0))
                step(nc.vector.tensor_tensor(own_t[:, 1, :], b[:, 2 * P:2 * P + SMP], part("own"), ALU.mult))
                step(nc.vector.reduce_sum(col[:, 2:3], own_t[:, 1, :], AX.X))
                nc.vector.scalar_tensor_tensor(SD[:, 2 * P:2 * P + 1], col[:, 2:3], HD ** -0.5, LD[:, 2 * P:2 * P + 1],
                                               ALU.mult, ALU.add)
                freed(nc.vector.scalar_tensor_tensor(SD[:, 0:2 * P], b[:, 0:2 * P], HD ** -0.5, LD[:, 0:2 * P],
                                                     ALU.mult, ALU.add), ("sct", 0))
                taken(dve, ("sct", 0))
                nc.vector.tensor_reduce(col[:, 0:1], SD[:, :], AX.X, ALU.max, negate=True).then_inc(sd_ready, 1)

            def sampled_probs():
                dve.wait_ge(pd_ready, 1)
                step(nc.vector.reciprocal(col[:, 3:4], col[:, 1:2]))
                step(nc.vector.tensor_scalar(PD[:, :], PD[:, :], col[:, 3:4], None, ALU.mult))
                nc.vector.tensor_scalar(PM[:, :], part("own"), PD[:, 2 * P:2 * P + 1], None, ALU.mult).then_inc(pe_ready, 1)

            def sampled_probs_out():
                b = full(dve, ("pdt", 0))
                dve.wait_ge(pdh_ready, NPG)
                nc.vector.tensor_copy(PMT[:, :], b[0:SMP, 2 * P:3 * P])
                for g in range(NPG):
                    ins = nc.vector.tensor_tensor(PDT[g][:, :, 1, :], b[:, g * P:(g + 1) * P].rearrange("p (n h) -> p n h", n=SMP),
                                                  PDT[g][:, :, 0, :].bitcast(f32), ALU.subtract)
                freed(ins, ("pdt", 0))

            def own_heads(n):
                r = slice(32 * (n % 4), 32 * (n % 4 + 1))
                for k in range(2):
                    b = full(dve, ("u", n, k))
                    own = part("hsel")[0:32, k * BH // 2:(k + 1) * BH // 2].unsqueeze(2).to_broadcast([32, BH // 2, HD])
                    freed(nc.vector.tensor_tensor(UM[r, n // 4, k * 512:(k + 1) * 512].rearrange("p (h d) -> p h d", d=HD),
                                                  b[0:32, :].rearrange("p (h d) -> p h d", d=HD), own, ALU.mult), ("u", n, k))

            maxima(0)
            for k in range(2):
                dve.wait_ge(q3h_ready, k + 1)
                c = slice(k * 512, (k + 1) * 512)
                b = misc[PLAN[("qt", k)][0]]
                freed(nc.vector.tensor_tensor(Q3[32:32 + SMP, c], b[0:SMP, :], Q3[0:SMP, c].bitcast(f32), ALU.subtract), ("qt", k))
            for m in range(2, KB, 2):
                queries_low(m)
            dve.wait_ge(vh_ready, 1)
            nc.vector.tensor_tensor(VL[:, 0:2, :], Vtok[:, 0:2, :], VH[:, 0:2, :].bitcast(f32), ALU.subtract)
            nc.vector.tensor_tensor(VL[0:META, 2, :], Vtok[0:META, 2, :], VH[0:META, 2, :].bitcast(f32),
                                    ALU.subtract).then_inc(vl_ready, 1)
            for h in range(BH):
                if h:
                    probs_low(h - 1)
                weights(h)
                if h + 1 < BH:
                    maxima(h + 1)
                if 1 <= h <= SMP:
                    dve.wait_ge(kp_ready, h)
                    head_sums(NPG * h - 1)
                if h < SMP:
                    page_scores(h)
                if h == SMP:
                    sampled_scores_out()
                if h == SMP + 1:
                    sampled_scores()
                if h == SMP + 2:
                    sampled_probs()
                    sampled_probs_out()
                if h >= VALUES:
                    page_low(2 * (h - VALUES))
                    page_low(2 * (h - VALUES) + 1)
                if h > VALUES:
                    own_heads(h - VALUES - 1)
            probs_low(BH - 1)
            for n in range(BH - VALUES, SMP):
                page_low(2 * n)
                own_heads(n - 1)
                page_low(2 * n + 1)
            own_heads(SMP - 1)
            dve.wait_ge(uo_done, 2)
            step(nc.vector.tensor_copy(SD[:, 0:KB * SMP], held[:, 0:KB * SMP]))
            pages = SD[:, 0:KB * SMP].rearrange("p (g k n) -> p g k n", g=2, k=KB)
            ov = held[:, 2 * P:3 * P].rearrange("p (k g n e) -> p g k n e", k=KB, g=2, e=2)
            for e in range(2):
                r = slice(HD * e, HD * (e + 1))
                for g in range(2):
                    ins = nc.vector.tensor_tensor(XG[r, :, PRM + 4 * g:PRM + 4 * (g + 1)], ov[r, g, :, :, e], pages[r, g, :, :],
                                                  ALU.add)
            ins.then_inc(of_ready, 1)
            for m in range(0, KB, 2):
                dve.wait_ge(oh_ready, KB // 2 + m // 2 + 1)
                nc.vector.tensor_tensor(HL[:, m:m + 2, :], XG[:, m:m + 2, :], HH[:, m:m + 2, :].bitcast(f32),
                                        ALU.subtract).then_inc(ol_ready, 1)
            in_pairs(dve, "fox_out", split, lambda g, half, par: [
                residual("fox_out", 5, 1.0, "ffn3", 2 * g + k, 2 * par + k) for k in range(2)])
            ffn(3, "final", 6, lambda: norm(5))
            norm(6)
            for m in range(KB):
                nc.vector.scalar_tensor_tensor(XG[:, m, :], X[:, m, :], gain[:, 7 * KB + m:7 * KB + m + 1], RS[:, :],
                                               ALU.mult, ALU.mult).then_inc(y_ready, 1)

        @block.tensor
        def _(pe):
            mm = nc.tensor.matmul

            def empty(key):
                b, n = PLAN[key]
                if n:
                    pe.wait_ge(misc_free[b], n)
                return misc[b]

            def filled(ins, key):
                ins.then_inc(misc_full[PLAN[key][0]], 1)

            def products(out, s, act_hi, act_lo, k0, tiles, first, last, ready=None):
                for k in range(tiles):
                    wh, wl = w_hi[s][:, k * P:(k + 1) * P], w_lo[s][:, k * P:(k + 1) * P]
                    if ready:
                        ready(k)
                    mm(out, wh, act_hi[:, k0 + k, :], start=first and k == 0, stop=False)
                    mm(out, wh, act_lo[:, k0 + k, :], start=False, stop=False)
                    ins = mm(out, wl, act_hi[:, k0 + k, :], start=False, stop=last and k == tiles - 1)
                return ins

            def project(seg, act_hi, act_lo, ready, stage=None, second=None, fifth=None):
                def chunk(at, s, ready=None):
                    pe.wait_ge(lo_ready, at + (CHUNK0[seg] + s + 1))
                    if stage:
                        pe.wait_ge(x_new, at + (KB * (stage - 1) + s + 1))
                    else:
                        pe.wait_ge(bank_free, at + (UNIT0[seg] + s + 1))
                    products(bank[s][:, 0:TOK], s, act_hi, act_lo, 0, KB, True, True, ready).then_inc(chunk_used, 1)

                chunk(0, 0, ready)
                if second:
                    second()
                for s in range(1, SLOTS):
                    chunk(0, s)
                if fifth:
                    fifth()
                with pe.Fori(1, COUNT[seg] // SLOTS) as i:
                    for s in range(SLOTS):
                        chunk(i * SLOTS, s)

            def normed(name):
                return lambda k: pe.wait_ge(xl_ready, KB * GAIN[name] + k + 1)

            def down(n, stage):
                seg = f"ffn{n}_down"
                with pe.Fori(0, COUNT[seg] // SLOTS) as i:
                    for s in range(SLOTS):
                        u = s // 2
                        pe.wait_ge(hid_ready, FB * n + DNT * (s % 2 + 1))
                        pe.wait_ge(lo_ready, i * SLOTS + (CHUNK0[seg] + s + 1))
                        if s % 2 == 0:
                            pe.wait_ge(x_new, i * 2 + (KB * (stage - 1) + u + 1))
                        products(bank[u][:, 0:TOK], s, HH, HL, DNT * (s % 2), DNT, s % 2 == 0,
                                 s % 2 == 1).then_inc(chunk_used, 1)

            def stat(n):
                if n == 0:
                    pe.wait_ge(const_in, 16)
                pe.wait_ge(ss_ready, n + 1)
                b = empty(("stat", n))
                filled(mm(b[:, 0:TOK], part("mean_d"), SS[:, :], start=True, stop=True), ("stat", n))

            pe.sem_inc(chunk_used, SLOTS)
            project("ffn0_up", XH, XL, normed("ffn0"), second=lambda: stat(0))
            down(0, 1)

            pe.wait_ge(small_in, 16)
            def gate():
                b = empty(("a", 0))
                for k in range(KB):
                    ins = mm(b[0:RANK, 0:TOK], wa[:, k, :], XG[:, k, :], start=k == 0, stop=k == KB - 1)
                filled(ins, ("a", 0))

            project("gla_qk", XH, XL, normed("gla"), second=lambda: stat(1), fifth=gate)
            taken(pe, ("a", 0))
            for h in range(AH):
                b = empty(("z", h))
                filled(mm(b[:, 0:TOK], part("walpha2")[0:RANK, h * P:(h + 1) * P], a_s[:, :], start=True, stop=True), ("z", h))
            project("gla_v", XH, XL, None)
            project("gla_r", XH, XL, None)
            pe.wait_ge(bank_free, SLOTS + UNIT0["gla_r"] + 8)

            def token_major(src, names):
                for i in range(3):
                    rows = P if i < 2 else META
                    for h in range(2):
                        b = empty((names[0], i, h))
                        for k in range(4):
                            ins = nc.tensor.transpose(b[0:rows, k * P:(k + 1) * P], src[:, 4 * h + k, i * P:i * P + rows], ident)
                        filled(ins, (names[0], i, h))
                for h in range(2):
                    b = empty((names[1], h))
                    for k in range(4):
                        ins = nc.tensor.transpose(b[0:SMP, k * P:(k + 1) * P], src[:, 4 * h + k, PRM:TOK], ident)
                    filled(ins, (names[1], h))

            token_major(V, ("vt", "vs"))
            b = empty(("ks", 0))
            for k in range(AH):
                ins = nc.tensor.transpose(b[0:SMP, k * P:(k + 1) * P], K[:, k, PRM:TOK], ident)
            filled(ins, ("ks", 0))
            for li, l in enumerate([0] + LEVELS):
                m = M1s[(li - 1) % 2]
                left, right = (m, m) if l else (K, Q)
                if l:
                    pe.wait_ge(m_ready, li)
                for i in range(3 if l <= 8 else 2):
                    r = META if i == 2 else P
                    b = empty(("lv", l, i))
                    for h in range(AH):
                        ins = mm(b[0:r, h * r:(h + 1) * r], left[:, h, i * P:i * P + r], right[:, h, i * P:i * P + r],
                                 start=True, stop=True)
                    filled(ins, ("lv", l, i))
            pe.wait_ge(m_ready, len(LEVELS) + 1)
            b = empty(("lv", 128, 0))
            for h in range(AH):
                ins = mm(b[:, h * P:(h + 1) * P], M1s[1][:, h, 0:P], M1s[1][:, h, P:256], start=True, stop=True)
            filled(ins, ("lv", 128, 0))
            pe.wait_ge(m_ready, len(LEVELS) + 2)
            b = empty(("lv", 256, 0))
            for i in range(2):
                for h in range(AH):
                    ins = mm(b[:, i * 64 + h * META:i * 64 + (h + 1) * META], M1s[0][:, h, i * P:(i + 1) * P], M1s[0][:, h, 256:PRM],
                             start=True, stop=True)
            filled(ins, ("lv", 256, 0))
            def outer(n):
                pe.wait_ge(km_ready, n + 1)
                for g in range(2):
                    b = empty(("kv", n, g))
                    for h in (2 * g, 2 * g + 1):
                        ins = mm(b[:, (h % 2) * DV:(h % 2 + 1) * DV], KM[:, n % 2, h * P:(h + 1) * P],
                                 V3[:, h * DV:(h + 1) * DV], start=True, stop=True)
                    filled(ins, ("kv", n, g))

            def prompt_output(o):
                h = o // 2
                v = slice(o * P, (o + 1) * P)
                b = empty(("o", o))
                mm(b[:, 0:PRM], Vtok[:, 0, v], ST0[:, h, :], start=True, stop=False)
                mm(b[:, P:PRM], Vtok[:, 1, v], ST1[:, h, :], start=False, stop=False)
                filled(mm(b[:, 2 * P:PRM], Vtok[0:META, 2, v], ST2[:, h, :], start=False, stop=True), ("o", o))

            def head_mean(h):
                pe.wait_ge(osq_ready, 1)
                b = empty(("hn", h))
                mm(b[:, 0:PRM], part("mean_dv"), OSQ[:, 2 * h, 0:PRM], start=True, stop=False)
                filled(mm(b[:, 0:PRM], part("mean_dv"), OSQ[:, 2 * h + 1, 0:PRM], start=False, stop=True), ("hn", h))

            def prompt_state(g):
                taken(pe, ("ke", 2))
                b = empty(("sp", g))
                for h in (2 * g, 2 * g + 1):
                    for i in range(3):
                        r = P if i < 2 else META
                        ins = mm(b[:, (h % 2) * DV:(h % 2 + 1) * DV], KE[0:r, i, h * P:(h + 1) * P],
                                 Vtok[0:r, i, h * DV:(h + 1) * DV], start=i == 0, stop=i == 2)
                filled(ins, ("sp", g))

            outer(0)
            outer(1)
            pe.wait_ge(m_ready, len(LEVELS) + 3)
            for i in range(3):
                rows = P if i < 2 else META
                b = empty(("ke", i))
                for h in range(AH):
                    ins = nc.tensor.transpose(b[0:rows, h * P:(h + 1) * P], M1s[1][:, h, i * P:i * P + rows], ident)
                filled(ins, ("ke", i))
            taken(pe, ("lv", 256, 0))
            for n in range(SMP):
                if n < AH:
                    prompt_output(2 * n)
                    prompt_output(2 * n + 1)
                else:
                    head_mean(n - AH)
                if n >= SMP - 2:
                    prompt_state(n - (SMP - 2))
                taken(pe, ("kv", n, 1))
                for o in range(KB):
                    h = o // 2
                    ins = mm(held[:, o * SMP + n:o * SMP + n + 1], S0[:, n % GSLOTS, h, (o % 2) * P:(o % 2 + 1) * P],
                             Q[:, h, PRM + n:PRM + n + 1], start=True, stop=True)
                ins.then_inc(s_used, 1)
                if n + 2 < SMP:
                    outer(n + 2)
            pe.wait_ge(osq_ready, 2)
            b = empty(("hns", 0))
            for h in range(AH):
                out = b[:, h * SMP:(h + 1) * SMP]
                mm(out, part("mean_dv"), OSQ[:, 2 * h, PRM:TOK], start=True, stop=False)
                ins = mm(out, part("mean_dv"), OSQ[:, 2 * h + 1, PRM:TOK], start=False, stop=True)
            filled(ins, ("hns", 0))
            project("gla_out", HH, HL, lambda k: pe.wait_ge(ol_ready, k // 2 + 1), stage=2)
            project("ffn1_up", XH, XL, normed("ffn1"), second=lambda: stat(2))
            down(1, 3)

            def forget():
                b = empty(("f", 0))
                for k in range(KB):
                    ins = mm(b[0:BH, 0:TOK], wf[:, k, :], XG[:, k, :], start=k == 0, stop=k == KB - 1)
                filled(ins, ("f", 0))

            project("kv_in", XH, XL, normed("kv"), second=lambda: stat(3), fifth=forget)
            pe.wait_ge(bank_free, SLOTS + UNIT0["kv_in"] + 16)
            token_major(Vf, ("fvt", "fvs"))
            project("ffn2_up", XH, XL, normed("ffn2"))
            down(2, 4)

            project("fox_q", XH, XL, normed("fox"), second=lambda: stat(4))
            pe.wait_ge(bank_free, SLOTS + UNIT0["fox_q"] + KB)
            for k in range(2):
                b = empty(("qt", k))
                for j in range(4):
                    ins = nc.tensor.transpose(b[0:SMP, j * P:(j + 1) * P], Qf[:, 4 * k + j, PRM:TOK], ident)
                filled(ins, ("qt", k))
            pe.wait_ge(qb_ready, 1)
            pe.wait_ge(kl_ready, 1)

            def scores(h):
                r = slice(HD * (h % 2), HD * (h % 2 + 1))
                pe.wait_ge(ql_ready, h // 4 + 1)
                for i in range(3):
                    rows = P if i < 2 else META
                    keys = min((i + 1) * P, PRM)
                    b = empty(("s", h, i // 2)) if i != 1 else b
                    out = b[0:rows, (P if i == 1 else 0):(P if i == 1 else 0) + keys]
                    for qp, kp, first in ((QH, KH, True), (QL, KH, False), (QH, KL, False)):
                        mm(out, qp[r, h // 2, i * P:i * P + rows], kp[r, h // 2, 0:keys], start=first, stop=False)
                    mm(out, pick[:, h:h + 1].to_broadcast([96, rows]), CB[:, 0:keys], start=False, stop=False)
                    diag = b[0:rows, (P if i == 1 else 0) + i * P:(P if i == 1 else 0) + keys]
                    ins = mm(diag, ident_b[0:rows, 0:rows], tri_b[0:rows, 0:rows], start=False, stop=True)
                    if i:
                        filled(ins, ("s", h, i // 2))

            def queries(n):
                taken(pe, ("qt", 1))
                pe.wait_ge(sel_ready, 1)
                for k in range(2):
                    b = empty(("qb", n, k))
                    filled(mm(b[:, :], sel_r[:, n:n + 1].to_broadcast([64, P]), Q3[:, k * 512:(k + 1) * 512],
                              start=True, stop=True), ("qb", n, k))

            def own_scores():
                pe.wait_ge(qb_ready, 3)
                own_s = held[0:SMP, 2 * P:3 * P].rearrange("p (n j e) -> p n j e", n=SMP, e=2)
                for j in range(KB):
                    ins = mm(own_s[:, :, j, :], Kf[:, j, PRM:TOK], QB[:, j, :, :], start=True, stop=True)
                ins.then_inc(own_done, 1)
                pe.wait_ge(lfp_in, 16 * SMP * NPG)
                b = empty(("lf", 0))
                for g in range(NPG):
                    ins = nc.tensor.transpose(b[:, g * P:(g + 1) * P], LFp[:, g, :, :].rearrange("p n h -> p (n h)"), ident)
                filled(ins, ("lf", 0))
                b = empty(("lown", 0))
                filled(mm(b[:, 0:SMP], part("rep")[0:BH, :], LG[:, PRM:TOK], start=True, stop=True), ("lown", 0))

            def sampled_scores():
                pe.wait_ge(sc_ready, 1)
                b = empty(("sct", 0))
                for g in range(NPG):
                    nc.tensor.transpose(b[:, g * P:(g + 1) * P], SC[:, g, :, :].rearrange("p n h -> p (n h)"), ident)
                filled(nc.tensor.transpose(b[:, 2 * P:2 * P + SMP], SO[:, :], ident[0:SMP, 0:SMP]), ("sct", 0))

            def sampled_probs():
                pe.wait_ge(pe_ready, 1)
                b = empty(("pdt", 0))
                for g in range(NPG):
                    nc.tensor.transpose(b[:, g * P:(g + 1) * P], PD[:, g * P:(g + 1) * P], ident)
                filled(nc.tensor.transpose(b[0:SMP, 2 * P:3 * P], PM[:, :], ident), ("pdt", 0))

            def own_values():
                taken(pe, ("pdt", 0))
                for j in range(KB):
                    mm(held[:, 2 * P + j * 2 * SMP:2 * P + (j + 1) * 2 * SMP], Vs[:, j * P:(j + 1) * P],
                       PMT[:, :].rearrange("p (n h) -> p n h", n=SMP)[:, :, 2 * j:2 * j + 2], start=True, stop=True)

            def page_values(n):
                for i in (2 * n, 2 * n + 1):
                    pe.wait_ge(vpl_ready, i + 1)
                    g = i % NPG
                    for k in range(2):
                        b = empty(("u", n, k))
                        probs = PDT[g][:, n, :, :].rearrange("p x h -> p (x h)")
                        mm(b[0:32, :], probs, VpH[i % 2][:, k * 512:(k + 1) * 512], start=g == 0, stop=False)
                        ins = mm(b[0:32, :], probs, VpL[i % 2][:, k * 512:(k + 1) * 512], start=False, stop=g == 1)
                        if g:
                            filled(ins, ("u", n, k))
                    if g == 0:
                        ins.then_inc(pv_done, 1)

            def sampled_outputs(g):
                taken(pe, ("u", 4 * g + 3, 1))
                for j in range(KB):
                    at = (g * KB + j) * 4
                    ins = mm(held[:, at:at + 4], UM[:, g, j * P:(j + 1) * P], part("quad"), start=True, stop=True)
                ins.then_inc(uo_done, 1)

            def transpose_probs(h):
                q = h % 2
                pe.wait_ge(pn_ready, h + 1)
                b = empty(("pt", h))
                nc.tensor.transpose(b[:, 0:P], PP[:, q, 0:P], ident)
                nc.tensor.transpose(b[:, P:2 * P], PP[:, q, P:2 * P], ident)
                nc.tensor.transpose(b[:, 2 * P:PRM], PP[0:META, q, 3 * P:4 * P], ident[0:META, 0:META])
                nc.tensor.transpose(b[:, PRM:PRM + P], PP[:, q, 2 * P:3 * P], ident)
                nc.tensor.transpose(b[:, PRM + P:PRM + 144], PP[0:META, q, 4 * P:5 * P], ident[0:META, 0:META])
                filled(nc.tensor.transpose(b[0:META, PRM + 144:PRM + 144 + META], PP[0:META, q, 5 * P:5 * P + META],
                                           ident[0:META, 0:META]), ("pt", h))

            def values(h):
                q = h % 2
                taken(pe, ("pt", h))
                pe.wait_ge(vl_ready, 1)
                if h >= 2:
                    pe.wait_ge(po_read, h - 1)
                out = bank[2 + q]
                v = slice(h // 2 * P, (h // 2 + 1) * P)
                for vp, pp, k in ((VH, PTH, 0), (VH, PTL, 1), (VL, PTH, 2)):
                    mm(out[:, 0:PRM], vp[:, 0, v], pp[:, q, 0:PRM], start=k == 0, stop=False)
                    mm(out[:, P:PRM], vp[:, 1, v], pp[:, q, PRM:PRM + 144], start=False, stop=False)
                    ins = mm(out[:, 2 * P:PRM], vp[0:META, 2, v], pp[0:META, q, PRM + 144:], start=False, stop=k == 2)
                ins.then_inc(fo_done, 1)

            scores(0)
            queries(0)
            for h in range(BH):
                if h + 1 < BH:
                    scores(h + 1)
                if h > VALUES:
                    page_values(h - VALUES - 1)
                if h:
                    values(h - 1)
                if h + 1 < SMP:
                    queries(h + 1)
                if h == SMP:
                    own_scores()
                if h == SMP + 1:
                    sampled_scores()
                if h == SMP + 2:
                    sampled_probs()
                transpose_probs(h)
                if h == SMP + 2:
                    own_values()
                if h == BH - 1:
                    sampled_outputs(0)
            page_values(BH - VALUES - 1)
            values(BH - 1)
            for n in range(BH - VALUES, SMP):
                page_values(n)
            sampled_outputs(1)
            project("fox_out", HH, HL, lambda k: pe.wait_ge(ol_ready, KB // 2 + k // 2 + 1), stage=5)
            project("ffn3_up", XH, XL, normed("ffn3"), second=lambda: stat(5))
            down(3, 6)
            stat(6)


def constants():
    import numpy as np
    s, t = np.arange(P)[:, None], np.arange(P)[None, :]
    eye = (s == t).astype(np.float32)
    own = (np.arange(P)[:, None] // BH == np.arange(SMP)[None, :]).astype(np.float32)
    rep = np.zeros((P, P), np.float32)
    rep[:BH] = (np.arange(BH)[:, None] == np.arange(P)[None, :] % BH)
    tri = np.where(t > s, np.float32(-1e30), np.float32(0))
    masks = np.stack([(s // (2 * l) == t // (2 * l)) & (s % (2 * l) < l) & (t % (2 * l) >= l) for l in LEVELS], 1)
    return {"ident": eye, "mean_d": np.full((P, P), 1.0 / D, np.float32), "mean_dv": np.full((P, P), 1.0 / DV, np.float32),
            "tri": tri, "own": own,
            "hsel": (np.arange(P)[:, None] % BH == np.arange(BH)[None, :]).astype(np.float32),
            "quad": (np.arange(P)[:, None] // 32 == np.arange(4)[None, :]).astype(np.float32), "sel": (np.arange(96)[:, None] % 32 == np.arange(SMP)[None, :]).astype(np.float32), "rep": rep,
            "pick": (np.arange(96)[:, None] % 32 == np.arange(BH)[None, :]).astype(np.float32)}, masks.astype(np.float32)


def kernel(**inputs):
    import numpy as np
    import concourse.bacc as bacc
    from concourse.bass_utils import run_bass_kernel_spmd

    a = {k: np.asarray(v) for k, v in inputs.items()}
    f32 = np.float32

    def chunks(w, tiles, n_cols):
        w = w[:, :n_cols].reshape(w.shape[0] // (P * tiles), tiles, P, n_cols // P, P)
        return w.transpose(3, 0, 2, 1, 4).reshape(-1, P, tiles * P)

    def columns(v):
        return v.reshape(-1, P).T

    up, down = [], []
    for l in range(2):
        for f in ("ffn1", "ffn2"):
            gate, upper = chunks(a[f + "_w_gate"][l], KB, FF), chunks(a[f + "_w_up"][l], KB, FF)
            up.append(np.stack([gate, upper], 1).reshape(2 * FB, P, UPW))
            down.append(chunks(a[f + "_w_down"][l], DNT, D))
    mix = [chunks(a["gla_w_in"][0], KB, 24 * P), chunks(a["gla_w_out"][0], KB, D), chunks(a["kv_w_in"], KB, 2 * D),
           chunks(a["fox_w_q"][0], KB, D), chunks(a["fox_w_out"][0], KB, D)]
    x = np.concatenate([a["meta_tokens"], a["x_prompt"][0], a["x_sample"][:, 0]], 0)

    const, masks = constants()
    gains = [a["norm_ffn1"][0], a["norm_mix"][0], a["norm_ffn2"][0], a["kv_norm"], a["norm_ffn1"][1], a["norm_mix"][1],
             a["norm_ffn2"][1], a["final_norm"]]
    const["gain"] = np.concatenate([columns(g) for g in gains], 1)
    const["ghead"] = columns(a["gla_g_head"][0])
    const["balpha"] = columns(a["gla_b_alpha"][0])
    const["bf"] = a["kv_b_f"][:, None]
    const["walpha2"] = a["gla_w_alpha2"][0]
    const["wa"] = a["gla_w_in"][0][:, 24 * P:].reshape(KB, P, RANK).transpose(1, 0, 2).reshape(P, -1)
    const["wf"] = a["kv_w_in"][:, 2 * D:].reshape(KB, P, BH).transpose(1, 0, 2).reshape(P, -1)
    small = np.zeros((P, NCOL), f32)
    for name, (lo, hi) in COL.items():
        small[:const[name].shape[0], lo:hi] = const[name]

    n_phys = a["cache_k"].shape[0]
    arrays = {
        "x_all": x.T.reshape(KB, P, TOK), "up_w": np.concatenate(up, 0), "down_w": np.concatenate(down, 0),
        "mix_w": np.concatenate(mix, 0), "small": small, "level_masks": masks, "state_in": a["state_gla"][0],
        "cache_k": a["cache_k"].reshape(n_phys, PAGE, D), "cache_v": a["cache_v"].reshape(n_phys, PAGE, D),
        "cache_f": a["cache_logf"], "table": a["page_table"].reshape(1, SMP * NPG),
    }
    arrays = {k: np.ascontiguousarray(v) for k, v in arrays.items()}
    outs = {"y_out": (KB, P, TOK), "k_out": (KB, P, TOK), "v_out": (KB, P, TOK), "lf_out": (BH, TOK),
            "state_prompt": (AH, P, DV), "state_sample": (SMP, AH, P, DV)}

    nc = bacc.Bacc("TRN2", target_bir_lowering=False, num_devices=1)
    args = [nc.dram_tensor(k, v.shape, mybir.dt.from_np(v.dtype), kind="ExternalInput").ap() for k, v in arrays.items()]
    args += [nc.dram_tensor(k, v, mybir.dt.float32, kind="ExternalOutput").ap() for k, v in outs.items()]
    build(nc, *args)
    r = run_bass_kernel_spmd(nc, [arrays], core_ids=[0]).results[0]

    def rows(name):
        return r[name].reshape(D, TOK).T

    y, k, v, lf = rows("y_out"), rows("k_out"), rows("v_out"), r["lf_out"].T
    return (y[None, META:PRM], y[PRM:, None], r["state_prompt"][None, None],
            k[:PRM].reshape(1, PRM, BH, HD), v[:PRM].reshape(1, PRM, BH, HD), lf[None, :PRM],
            r["state_sample"][None],
            k[PRM:].reshape(SMP, 1, BH, HD), v[PRM:].reshape(SMP, 1, BH, HD), lf[PRM:, None])
```
